# Optimizing a Trainium2 kernel written in Bass

```python
import functools
import jax, jax.numpy as jnp
from jax import lax
import numpy as np

D_MODEL = 1024
BATCH = 1
SEQ = 1024
DEPTH = 1
DEC_BATCH = 8
DEC_SEQ = 1
PAST_LEN = 1024
PAGE_SIZE = 128

N_ADA = 6
EPS = 1e-6
NEG_INF = -1e30
ROPE_THETA = 500000.0

MLA_HEADS = 8
Q_LORA = 256
KV_LORA = 128
QK_NOPE = 64
QK_ROPE = 32
QK_DIM = QK_NOPE + QK_ROPE
V_HEAD = 64
LAT_DIM = KV_LORA + QK_ROPE
Q_BLOCK = 128

DIL_GROUPS = ((128, 1), (512, 4), (2048, 16))
N_DIL_GROUPS = 3
DIL_HEADS = 4
DIL_HEAD_DIM = 128
ROT_DIM = DIL_HEAD_DIM // 4

PEER_HEADS = 8
N_KEYS = 128
N_EXPERTS = N_KEYS * N_KEYS
PK_DIM = 256
PK_HALF = PK_DIM // 2
PEER_TOPK = 16
PEER_BLOCK = 256

O_KVL = Q_LORA
O_KR = O_KVL + KV_LORA
O_DIL = O_KR + QK_ROPE
O_GATE = O_DIL + 3 * N_DIL_GROUPS * DIL_HEADS * DIL_HEAD_DIM
IN_COLS = O_GATE + 2 * D_MODEL
MLA_OUT = MLA_HEADS * V_HEAD
DIL_OUT = DIL_HEADS * DIL_HEAD_DIM

kernel_name = 'hybrid_mla_dilated_peer_step'

def rms_norm(x, g):
    xf = x.astype(jnp.float32)
    y = xf * lax.rsqrt(jnp.mean(xf * xf, axis=-1, keepdims=True) + EPS)
    return (y * g.astype(jnp.float32)).astype(x.dtype)

def rope_angles(pos, dim):
    half = dim // 2
    inv_freq = ROPE_THETA ** (-jnp.arange(half, dtype=jnp.float32) / half)
    ang = pos.astype(jnp.float32)[:, None] * inv_freq[None, :]
    return jnp.cos(ang), jnp.sin(ang)

def apply_rope(x, cos, sin):
    half = x.shape[-1] // 2
    x1, x2 = x[..., :half], x[..., half:]
    cos, sin = cos.astype(x.dtype), sin.astype(x.dtype)
    return jnp.concatenate([x1 * cos - x2 * sin, x2 * cos + x1 * sin], axis=-1)

def ada_terms(c, w_ada, b_ada):
    m = (jax.nn.silu(c) @ w_ada + b_ada)[:, None, :]
    return jnp.split(m, N_ADA, axis=-1)

def modulate(x, g, shift, scale):
    return rms_norm(x, g) * (1.0 + scale) + shift

def mixer_front(h, pos, lw):
    b, s = h.shape[:2]
    z = h @ lw['w_in']
    cos_m, sin_m = rope_angles(pos, QK_ROPE)
    c_q = rms_norm(z[..., :O_KVL], lw['g_q_lora'])
    q = rms_norm(jnp.einsum('bsr,rhd->bshd', c_q, lw['w_uq']), lw['g_mla_qn'])
    q = jnp.concatenate([q[..., :QK_NOPE], apply_rope(q[..., QK_NOPE:], cos_m[:, None], sin_m[:, None])], axis=-1)
    latent = jnp.concatenate([rms_norm(z[..., O_KVL:O_KR], lw['g_kv_lora']), z[..., O_KR:O_DIL]], axis=-1)
    dqkv = z[..., O_DIL:O_GATE].reshape(b, s, 3, N_DIL_GROUPS, DIL_HEADS, DIL_HEAD_DIM)
    cos_d, sin_d = rope_angles(pos, ROT_DIM)

    def norm_rope(t, g):
        t = rms_norm(t, g)
        rot = apply_rope(t[..., :ROT_DIM], cos_d[:, None, None], sin_d[:, None, None])
        return jnp.concatenate([rot, t[..., ROT_DIM:]], axis=-1)

    dq = norm_rope(dqkv[:, :, 0], lw['g_dil_qn'])
    dk = norm_rope(dqkv[:, :, 1], lw['g_dil_kn'])
    dv = dqkv[:, :, 2]
    gates = jax.nn.sigmoid(z[..., O_GATE:].astype(jnp.float32)).astype(h.dtype)
    return q, latent, dq, dk, dv, gates[..., :D_MODEL], gates[..., D_MODEL:]

def mla_keys(rows, pos, w_uk, g_kn):
    c_kv, kr = rows[..., :KV_LORA], rows[..., KV_LORA:]
    k_nope = jnp.einsum('btr,rhd->bthd', c_kv, w_uk)
    ms = (jnp.sum(jnp.square(k_nope.astype(jnp.float32)), axis=-1)
          + jnp.sum(jnp.square(kr.astype(jnp.float32)), axis=-1, keepdims=True)) / QK_DIM
    inv = lax.rsqrt(ms + EPS)
    k_nope = k_nope * (inv[..., None] * g_kn[:QK_NOPE].astype(jnp.float32)).astype(rows.dtype)
    cos, sin = rope_angles(pos, QK_ROPE)
    kr = apply_rope(kr * g_kn[QK_NOPE:], cos, sin)
    return k_nope, kr, inv.astype(rows.dtype)

def mla_probs(q, k_nope, kr, inv, mask):
    s = jnp.einsum('bqhd,bthd->bhqt', q[..., :QK_NOPE], k_nope)
    s = s + jnp.einsum('bqhr,btr->bhqt', q[..., QK_NOPE:], kr) * jnp.transpose(inv, (0, 2, 1))[:, :, None, :]
    s = jnp.where(mask, s.astype(jnp.float32) * QK_DIM ** -0.5, NEG_INF)
    return jax.nn.softmax(s, axis=-1).astype(q.dtype)

def dilated_prompt(q, k, v, span, dilation):
    b, s, nh, e = q.shape
    unit = dilation * span
    s_pad = -(-s // unit) * unit
    nb = s_pad // unit

    def to_sub(t):
        t = jnp.pad(t, ((0, 0), (0, s_pad - s), (0, 0), (0, 0))).reshape(b, s_pad // dilation, dilation, nh, -1)
        return jnp.transpose(t, (0, 2, 1, 3, 4)).reshape(b, dilation, nb, span, nh, t.shape[-1])

    def from_sub(t):
        t = t.reshape(b, dilation, s_pad // dilation, nh, t.shape[-1])
        return jnp.transpose(t, (0, 2, 1, 3, 4)).reshape(b, s_pad, nh, -1)[:, :s]

    def with_prev(t):
        prev = jnp.pad(t, ((0, 0), (0, 0), (1, 0), (0, 0), (0, 0), (0, 0)))[:, :, :-1]
        return jnp.concatenate([prev, t], axis=3)

    qs, ks, vs = to_sub(q), to_sub(k), to_sub(v)
    kk, vv = with_prev(ks), with_prev(vs)
    sc = jnp.einsum('brnqhe,brnkhe->brnhqk', qs, kk).astype(jnp.float32) * e ** -0.5
    qi = jnp.arange(span)[:, None]
    kj = jnp.arange(2 * span)[None, :]
    delta = span + qi - kj
    band = (delta >= 0) & (delta <= span)
    valid = band[None] & ((jnp.arange(nb)[:, None, None] > 0) | (kj >= span)[None])
    sc = jnp.where(valid[:, None], sc, NEG_INF)
    lse = jax.nn.logsumexp(sc, axis=-1)
    p = jnp.exp(sc - lse[..., None]).astype(v.dtype)
    o = jnp.einsum('brnhqk,brnkhe->brnqhe', p, vv)
    return from_sub(o), from_sub(jnp.swapaxes(lse, 3, 4)[..., None])[..., 0]

def dilated_sample(q, k, v, buf, span, dilation):
    b, s, nh, e = q.shape
    n_buf = buf.shape[1]
    kk = jnp.concatenate([buf[:, :, 0], k], axis=1)
    vv = jnp.concatenate([buf[:, :, 1], v], axis=1)
    idx = n_buf + jnp.arange(s)[:, None] - dilation * jnp.arange(span + 1)[None, :]
    valid = idx >= 0
    idx = jnp.maximum(idx, 0).reshape(-1)
    kg = jnp.take(kk, idx, axis=1).reshape(b, s, span + 1, nh, e)
    vg = jnp.take(vv, idx, axis=1).reshape(b, s, span + 1, nh, e)
    sc = jnp.einsum('bqhe,bqjhe->bhqj', q, kg).astype(jnp.float32) * e ** -0.5
    sc = jnp.where(valid[None, None], sc, NEG_INF)
    lse = jax.nn.logsumexp(sc, axis=-1)
    p = jnp.exp(sc - lse[..., None]).astype(v.dtype)
    o = jnp.einsum('bhqj,bqjhe->bqhe', p, vg)
    return o, jnp.transpose(lse, (0, 2, 1))

def combine_groups(outs, lses):
    wts = jax.nn.softmax(jnp.stack(lses, axis=0), axis=0).astype(outs[0].dtype)
    o = jnp.einsum('gbsh,gbshe->bshe', wts, jnp.stack(outs, axis=0))
    return o.reshape(o.shape[:2] + (DIL_OUT,))

def attend_prompt(q, latent, dq, dk, dv, lw):
    b, s = q.shape[:2]
    pos = jnp.arange(s)
    k_nope, kr, inv = mla_keys(latent, pos, lw['w_uk'], lw['g_mla_kn'])
    v = jnp.einsum('btr,rhd->bthd', latent[..., :KV_LORA], lw['w_uv'])
    nb = s // Q_BLOCK
    qb = jnp.moveaxis(q.reshape(b, nb, Q_BLOCK, MLA_HEADS, QK_DIM), 1, 0)

    def block(args):
        qi, bi = args
        qpos = bi * Q_BLOCK + jnp.arange(Q_BLOCK)
        p = mla_probs(qi, k_nope, kr, inv, qpos[:, None] >= pos[None, :])
        return jnp.einsum('bhqt,bthd->bqhd', p, v)

    o = lax.map(block, (qb, jnp.arange(nb)))
    o_mla = jnp.moveaxis(o, 0, 1).reshape(b, s, MLA_OUT)
    outs, lses, tails = [], [], []
    for g, (win, dil) in enumerate(DIL_GROUPS):
        o_g, l_g = dilated_prompt(dq[:, :, g], dk[:, :, g], dv[:, :, g], win // dil, dil)
        outs.append(o_g)
        lses.append(l_g)
        n_keep = min(win, s)
        tails.append(jnp.stack([dk[:, s - n_keep:, g], dv[:, s - n_keep:, g]], axis=2))
    return o_mla, combine_groups(outs, lses), (latent, tails)

def attend_sample(q, latent, dq, dk, dv, past_rows, bufs, lw):
    b, s = q.shape[:2]
    n_past = past_rows.shape[1]
    rows = jnp.concatenate([past_rows, latent], axis=1)
    kpos = jnp.arange(n_past + s)
    qpos = n_past + jnp.arange(s)
    k_nope, kr, inv = mla_keys(rows, kpos, lw['w_uk'], lw['g_mla_kn'])
    p = mla_probs(q, k_nope, kr, inv, qpos[:, None] >= kpos[None, :])
    ctx = jnp.einsum('bhqt,btr->bqhr', p, rows[..., :KV_LORA])
    o_mla = jnp.einsum('bqhr,rhd->bqhd', ctx, lw['w_uv']).reshape(b, s, MLA_OUT)
    outs, lses, new_rows = [], [], []
    for g, (win, dil) in enumerate(DIL_GROUPS):
        o_g, l_g = dilated_sample(dq[:, :, g], dk[:, :, g], dv[:, :, g], bufs[g], win // dil, dil)
        outs.append(o_g)
        lses.append(l_g)
        new_rows.append(jnp.stack([dk[:, :, g], dv[:, :, g]], axis=2))
    return o_mla, combine_groups(outs, lses), (latent, new_rows)

def peer(h, w_pq, sub_keys, expert_u, expert_v):
    lead = h.shape[:-1]
    hf = h.reshape(-1, h.shape[-1])
    n = hf.shape[0]
    n_pad = -(-n // PEER_BLOCK) * PEER_BLOCK
    hb = jnp.pad(hf, ((0, n_pad - n), (0, 0))).reshape(n_pad // PEER_BLOCK, PEER_BLOCK, -1)

    def block(hx):
        q = (hx @ w_pq).reshape(PEER_BLOCK, PEER_HEADS, 2, PK_HALF)
        s = jnp.einsum('nhpc,hpkc->nhpk', q, sub_keys).astype(jnp.float32)
        top_s, top_i = lax.top_k(s, PEER_TOPK)
        cand = top_s[:, :, 0, :, None] + top_s[:, :, 1, None, :]
        best_s, best = lax.top_k(cand.reshape(PEER_BLOCK, PEER_HEADS, PEER_TOPK * PEER_TOPK), PEER_TOPK)
        i1 = jnp.take_along_axis(top_i[:, :, 0, :], best // PEER_TOPK, axis=-1)
        i2 = jnp.take_along_axis(top_i[:, :, 1, :], best % PEER_TOPK, axis=-1)
        eidx = i1 * N_KEYS + i2
        g = jax.nn.softmax(best_s, axis=-1).astype(hx.dtype)
        a = jax.nn.gelu(jnp.einsum('nd,nhkd->nhk', hx, expert_u[eidx]), approximate=False) * g
        return jnp.einsum('nhk,nhkd->nd', a, expert_v[eidx])

    out = lax.map(block, hb).reshape(n_pad, -1)[:n]
    return out.reshape(lead + (out.shape[-1],))

def residual_layer(x, c, pos, attend, lw):
    sh1, sc1, gt1, sh2, sc2, gt2 = ada_terms(c, lw['w_ada'], lw['b_ada'])
    h = modulate(x, lw['norm_mix_g'], sh1, sc1)
    q, latent, dq, dk, dv, gate_a, gate_b = mixer_front(h, pos, lw)
    o_mla, o_dil, new_state = attend(q, latent, dq, dk, dv)
    y = gate_a * (o_mla @ lw['w_branch_mla']) + gate_b * (o_dil @ lw['w_branch_dil'])
    x = x + gt1 * (y @ lw['w_out'])
    h2 = modulate(x, lw['norm_ffn_g'], sh2, sc2)
    x = x + gt2 * peer(h2, lw['w_pq'], lw['sub_keys'], lw['expert_u'], lw['expert_v'])
    return x, new_state

def setup_inputs(seed: int = 0) -> dict:
    key = jax.random.key(seed)
    keys = iter(jax.random.split(key, 40))

    def nrm(shape, scale):
        return jax.random.normal(next(keys), shape, jnp.float32) * scale

    def gain(n):
        return 1.0 + nrm((DEPTH, n), 0.05)

    d = D_MODEL
    n_pages = PAST_LEN // PAGE_SIZE
    n_pool = (DEC_BATCH * n_pages * 5) // 4
    page_table = jax.random.permutation(next(keys), n_pool)[:DEC_BATCH * n_pages]
    page_table = page_table.reshape(DEC_BATCH, n_pages).astype(jnp.int32)
    return {
        'x_prompt': nrm((BATCH, SEQ, d), 1.0),
        'x_sample': nrm((DEC_BATCH, DEC_SEQ, d), 1.0),
        'c_prompt': nrm((BATCH, d), 1.0),
        'c_sample': nrm((DEC_BATCH, d), 1.0),
        'cache_latent': nrm((DEPTH, n_pool, PAGE_SIZE, LAT_DIM), 1.0),
        'state_dil0': nrm((DEPTH, DEC_BATCH, min(DIL_GROUPS[0][0], PAST_LEN), 2, DIL_HEADS, DIL_HEAD_DIM), 1.0),
        'state_dil1': nrm((DEPTH, DEC_BATCH, min(DIL_GROUPS[1][0], PAST_LEN), 2, DIL_HEADS, DIL_HEAD_DIM), 1.0),
        'state_dil2': nrm((DEPTH, DEC_BATCH, min(DIL_GROUPS[2][0], PAST_LEN), 2, DIL_HEADS, DIL_HEAD_DIM), 1.0),
        'page_table': page_table,
        'norm_mix_g': gain(d),
        'norm_ffn_g': gain(d),
        'w_ada': nrm((DEPTH, d, N_ADA * d), 0.5 * d ** -0.5),
        'b_ada': nrm((DEPTH, N_ADA * d), 0.02),
        'w_in': nrm((DEPTH, d, IN_COLS), d ** -0.5),
        'g_q_lora': gain(Q_LORA),
        'g_kv_lora': gain(KV_LORA),
        'w_uq': nrm((DEPTH, Q_LORA, MLA_HEADS, QK_DIM), Q_LORA ** -0.5),
        'w_uk': nrm((DEPTH, KV_LORA, MLA_HEADS, QK_NOPE), KV_LORA ** -0.5),
        'w_uv': nrm((DEPTH, KV_LORA, MLA_HEADS, V_HEAD), KV_LORA ** -0.5),
        'g_mla_qn': gain(QK_DIM),
        'g_mla_kn': gain(QK_DIM),
        'g_dil_qn': gain(DIL_HEAD_DIM),
        'g_dil_kn': gain(DIL_HEAD_DIM),
        'w_branch_mla': nrm((DEPTH, MLA_OUT, d), MLA_OUT ** -0.5),
        'w_branch_dil': nrm((DEPTH, DIL_OUT, d), DIL_OUT ** -0.5),
        'w_out': nrm((DEPTH, d, d), d ** -0.5),
        'w_pq': nrm((DEPTH, d, PEER_HEADS * PK_DIM), d ** -0.5),
        'sub_keys': nrm((DEPTH, PEER_HEADS, 2, N_KEYS, PK_HALF), PK_HALF ** -0.5),
        'expert_u': nrm((DEPTH, N_EXPERTS, d), d ** -0.5),
        'expert_v': nrm((DEPTH, N_EXPERTS, d), 0.5),
    }

def reference(x_prompt, x_sample, c_prompt, c_sample, cache_latent, state_dil0, state_dil1, state_dil2,
              page_table, norm_mix_g, norm_ffn_g, w_ada, b_ada, w_in, g_q_lora, g_kv_lora, w_uq, w_uk, w_uv,
              g_mla_qn, g_mla_kn, g_dil_qn, g_dil_kn, w_branch_mla, w_branch_dil, w_out, w_pq, sub_keys,
              expert_u, expert_v):
    dec_b = x_sample.shape[0]
    n_past = page_table.shape[1] * cache_latent.shape[2]
    pos_p = jnp.arange(x_prompt.shape[1])
    pos_s = n_past + jnp.arange(x_sample.shape[1])
    xp, xs = x_prompt, x_sample
    lat_p, lat_s, dil_p, dil_s = [], [], [], []
    for l in range(DEPTH):
        lw = {
            'norm_mix_g': norm_mix_g[l], 'norm_ffn_g': norm_ffn_g[l], 'w_ada': w_ada[l], 'b_ada': b_ada[l],
            'w_in': w_in[l], 'g_q_lora': g_q_lora[l], 'g_kv_lora': g_kv_lora[l], 'w_uq': w_uq[l],
            'w_uk': w_uk[l], 'w_uv': w_uv[l], 'g_mla_qn': g_mla_qn[l], 'g_mla_kn': g_mla_kn[l],
            'g_dil_qn': g_dil_qn[l], 'g_dil_kn': g_dil_kn[l], 'w_branch_mla': w_branch_mla[l],
            'w_branch_dil': w_branch_dil[l], 'w_out': w_out[l], 'w_pq': w_pq[l], 'sub_keys': sub_keys[l],
            'expert_u': expert_u[l], 'expert_v': expert_v[l],
        }
        xp, (lp, tp) = residual_layer(xp, c_prompt, pos_p, functools.partial(attend_prompt, lw=lw), lw)
        past = cache_latent[l][page_table].reshape(dec_b, n_past, LAT_DIM)
        bufs = (state_dil0[l], state_dil1[l], state_dil2[l])
        xs, (ls, ts) = residual_layer(xs, c_sample, pos_s,
                                      functools.partial(attend_sample, past_rows=past, bufs=bufs, lw=lw), lw)
        lat_p.append(lp)
        lat_s.append(ls)
        dil_p.append(tp)
        dil_s.append(ts)
    new_latent_prompt = jnp.stack(lat_p)
    new_latent_sample = jnp.stack(lat_s)
    new_dil0_prompt = jnp.stack([t[0] for t in dil_p])
    new_dil1_prompt = jnp.stack([t[1] for t in dil_p])
    new_dil2_prompt = jnp.stack([t[2] for t in dil_p])
    new_dil0_sample = jnp.stack([t[0] for t in dil_s])
    new_dil1_sample = jnp.stack([t[1] for t in dil_s])
    new_dil2_sample = jnp.stack([t[2] for t in dil_s])
    return (xp, xs, new_latent_prompt, new_latent_sample, new_dil0_prompt, new_dil1_prompt, new_dil2_prompt,
            new_dil0_sample, new_dil1_sample, new_dil2_sample)


_drawn_inputs = setup_inputs


def setup_inputs(seed=0):
    import zlib

    import numpy as np

    out = dict(_drawn_inputs(seed))
    spreads = {}
    factors = {'cache_latent': 5.2,
     'state_dil0': 4.662,
     'state_dil1': 4.044,
     'state_dil2': 6.386,
     'norm_ffn_g': 2.991,
     'g_q_lora': 8.0,
     'w_uq': 2.968,
     'w_uk': 3.16,
     'g_mla_qn': 8.0,
     'g_mla_kn': 8.0,
     'g_dil_qn': 8.0}
    for name, (base, spread) in spreads.items():
        noise = np.random.default_rng([zlib.crc32(name.encode()), seed]).standard_normal(out[name].shape)
        drawn = base * np.exp(spread * noise) if base else spread * noise
        out[name] = __import__('jax').numpy.asarray(drawn.astype(out[name].dtype))
    for name, factor in factors.items():
        out[name] = (out[name] * factor).astype(out[name].dtype)
    return out
```

```python
from contextlib import ExitStack

import concourse.bass as bass
import numpy as np
from concourse import mybir

F32 = mybir.dt.float32
F32R = mybir.dt.float32r
I32 = mybir.dt.int32
U32 = mybir.dt.uint32
ACT = mybir.ActivationFunctionType
ALU = mybir.AluOpType
AX = mybir.AxisListType

P = 128
D = 1024
KD = D // P
NPR = 1024
NSA = 8
TOK = NPR + NSA
CH = TOK // 3
NCH = 3
TILES = [(t * P, P) for t in range(NPR // P)] + [(NPR, NSA)]
EPS = 1e-6
NEG = -1e30
THETA = 500000.0

QL, KVL, ROPE, NOPE = 256, 128, 32, 64
QK = NOPE + ROPE
LAT = KVL + ROPE
MH, VH = 8, 64
GROUPS = ((128, 1), (512, 4), (2048, 16))
NG, DH, DE = 3, 4, 128
GW = DH * DE
RH = 16
PAGE, NPAGE, PAST = 128, 8, 1024
PH, NK, TOPK = 8, 128, 16
ADA = 6
MSCALE = QK ** -0.5
DSCALE = DE ** -0.5

O_KVL = QL
O_DIL = QL + LAT
O_GATE = O_DIL + 3 * NG * GW


class Steps:

    def __init__(self, sem):
        self.sem, self.n, self.off = sem, 0, None

    def value(self):
        return self.n if self.off is None else self.off + self.n

    def __call__(self, eng, ins):
        ins.then_inc(self.sem, 1)
        self.n += 1
        eng.wait_ge(self.sem, self.value())

    def loop(self, i, per, first=0):
        self.base, self.per = self.n, per
        self.off = (i - first) * per if first else i * per

    def end(self, turns):
        assert self.n == self.base + self.per, (self.n, self.base, self.per)
        self.off, self.n = None, self.base + self.per * turns


class Turn:

    def __init__(self, by=1):
        self.by, self.n = by, {}

    def take(self, eng, sem, times=1):
        self.n[sem.name] = self.n.get(sem.name, 0) + self.by * times
        eng.wait_ge(sem, self.n[sem.name])


def sub_tokens(g, b):
    dil = GROUPS[g][1]
    if dil == 16:
        return b, dil // 2
    per = NPR // P // dil
    return b // per + dil * P * (b % per), dil


def sub_slice(g, b, row0=0):
    first, step = sub_tokens(g, b)
    return slice(first - row0, first - row0 + step * (P - 1) + 1, step)


class Core:

    def __init__(self):
        self.stage_sems = []

    def sem(self, name):
        self.stage_sems.append(self.nc.alloc_semaphore(name))
        return self.stage_sems[-1]

    def end_stage(self):
        self.nc.clear_and_free_semaphores(self.stage_sems)
        self.nc.all_engine_barrier()
        self.stage_sems = []


def setup(nc, c, ctx, IN, OUT):
    def sem(name):
        return ctx.enter_context(nc.semaphore(name))

    def sb(name, shape, dt=F32):
        return ctx.enter_context(nc.sbuf_tensor(name, shape, dt))

    c.nc, c.IN, c.OUT = nc, IN, OUT
    c.ps = [ctx.enter_context(nc.psum_tensor(f"bank{i}", [P, 512], F32)) for i in range(8)]
    c.vstep = Steps(sem("vector_step"))
    c.astep = Steps(sem("scalar_step"))
    c.eps = sb("eps", [P, 1])
    c.mod = sb("mod", [P, ADA, KD, 1 + NSA])
    c.gs = sb("gain_scale", [P, 2, KD, 1 + NSA])
    c.gT = sb("gainsT", [P, 2 * KD + 2 + 1])
    c.dram = {}

    def scratch(name, shape):
        c.dram[name] = nc.dram_tensor(name, shape, F32, kind="Internal").ap()
    scratch("x1_dram", (P, KD, TOK))
    scratch("q_dil_sample", (NG, NSA * GW))
    scratch("o_group", (NG, NPR, GW + 2 * DH))
    scratch("gates_dram", (NK, NK, TOK))


def right_side(c, ctx, tensors):
    return [ctx.enter_context(c.nc.sbuf_tensor(name, shape, F32, side="right")) for name, shape in tensors.items()]


R_KVL, R_QN, R_KN, R_DQ, R_DK = 0, KVL, KVL + QK, KVL + 2 * QK, KVL + 2 * QK + DE
ROWG = R_DK + DE


def product3(pe, out, w, x, start, stop):
    pe.matmul(out, w[0], x[0], start=start, stop=False)
    pe.matmul(out, w[0], x[1], start=False, stop=False)
    return pe.matmul(out, w[1], x[0], start=False, stop=stop)


def low_part(dve, low, full, high):
    return dve.tensor_tensor(low, full, high.bitcast(F32), ALU.subtract)


def sum_squares(pe, c, bank, ones_rows, sq, n, done):
    for k in range(n):
        ins = pe.matmul(bank[:, 0:CH], c.ones[:, :], sq[:, k, :], start=(k == 0), stop=(k == n - 1))
    ins.then_inc(done, 1)


def stage_ada(c):
    nc, IN = c.nc, c.IN
    SL = 4
    with ExitStack() as ctx:
        sb = lambda name, shape: ctx.enter_context(nc.sbuf_tensor(name, shape, F32))
        cT = sb("cT", [P, KD, 1 + NSA])
        sig = sb("sigmoid_c", [P, KD, 1 + NSA])
        sc = sb("silu_c", [P, KD, 1 + NSA])
        bT = sb("b_adaT", [P, ADA * KD])
        w = [sb(f"w_ada{j}", [P, KD, P]) for j in range(SL)]
        w_in = [c.sem(f"ada_w_in{j}") for j in range(SL)]
        c_in, small_in, silu, mm = c.sem("ada_c_in"), c.sem("ada_small_in"), c.sem("ada_silu"), c.sem("ada_mm")
        sig_done, ones_done = c.sem("ada_sig"), c.sem("ada_ones")
        out = c.ps[0][:, 0:ADA * KD * (1 + NSA)]
        turns = ADA * KD // SL
        with nc.Block() as block:
            @block.sync
            def _(sp):
                sp.dma_start(cT[:], IN["cT"]).then_inc(c_in, 16)
                for j in range(SL):
                    sp.dma_start(w[j][:], IN["w_ada"][j]).then_inc(w_in[j], 16)
                with sp.Fori(1, turns) as i:
                    for j in range(SL):
                        sp.wait_ge(mm, (i - 1) * SL + j + 1)
                        sp.dma_start(w[j][:], IN["w_ada"][bass.ds(i * SL + j, 1)]
                                     .rearrange("o p k n -> (o p) k n")).then_inc(w_in[j], 16)

            @block.scalar
            def _(act):
                for dst, src in ((bT, "b_adaT"), (c.gT, "gainsT"), (c.rows, "row_gains"), (c.ident, "ident"),
                                 (c.rot, "rot"), (c.masks, "masks"), (c.iota, "iota")):
                    act.dma_start(dst[:], IN[src]).then_inc(small_in, 16)
                act.wait_ge(c_in, 16)
                act.activation(sig[:], cT[:], ACT.Sigmoid).then_inc(sig_done, 1)

            @block.vector
            def _(dve):
                dve.memset(c.ones[:], 1.0).then_inc(ones_done, 1)
                dve.memset(c.eps[:], EPS).then_inc(ones_done, 1)
                dve.wait_ge(sig_done, 1)
                dve.tensor_tensor(sc[:], sig[:], cT[:], ALU.mult).then_inc(silu, 1)
                dve.wait_ge(mm, ADA * KD)
                dve.wait_ge(small_in, 112)
                c.vstep(dve, dve.tensor_tensor(
                    c.mod[:].rearrange("p a k n -> p (a k) n"), out.rearrange("p (m n) -> p m n", n=1 + NSA),
                    bT[:].unsqueeze(2).to_broadcast([P, ADA * KD, 1 + NSA]), ALU.add))
                for r, w, scale in ((R_QN, QK, MSCALE), (R_DQ, DE, DSCALE)):
                    dve.tensor_scalar(c.rows[:, r:r + w], c.rows[:, r:r + w], scale, None, ALU.mult)
                for n in range(2):
                    g = c.gT[:, n * KD:(n + 1) * KD].unsqueeze(2).to_broadcast([P, KD, 1 + NSA])
                    dve.scalar_tensor_tensor(out=c.gs[:, n], in0=c.mod[:, 3 * n + 1], scalar=1.0,
                                             in1=g, op0=ALU.add, op1=ALU.mult)

            @block.tensor
            def _(pe):
                pe.wait_ge(silu, 1)
                with pe.Fori(0, turns) as i:
                    for j in range(SL):
                        pe.wait_ge(w_in[j], i * 16 + 16)
                        for k in range(KD):
                            ins = pe.matmul(out[:, bass.ds((i * SL + j) * (1 + NSA), 1 + NSA)], w[j][:, k, :],
                                            sc[:, k, :], start=(k == 0), stop=(k == KD - 1))
                        ins.then_inc(mm, 1)


def stage_norm(c, name, src_load, n, parts=None):
    nc = c.nc
    with ExitStack() as ctx:
        sb = lambda t, shape: ctx.enter_context(nc.sbuf_tensor(f"{name}_{t}", shape, F32))
        x = sb("x", [P, KD, TOK])
        sq = [sb(f"sq{i}", [P, KD, CH]) for i in range(2)]
        root = sb("root", [P, TOK])
        inv = sb("inv", [P, TOK])
        tmp = sb("tmp", [P, KD, TOK])
        s = {t: c.sem(f"{name}_{t}") for t in ("x_in", "sq", "sum", "root", "inv", "xn", "h", "hi")}
        gs, sh = c.gs[:, n], c.mod[:, 3 * n]
        h = x if parts else c.hT
        with nc.Block() as block:
            @block.sync
            def _(sp):
                src_load(sp, x, s["x_in"])

            @block.scalar
            def _(act):
                act.wait_ge(s["x_in"], 16)
                for i in range(NCH):
                    if i >= 2:
                        act.wait_ge(s["sum"], i - 1)
                    act.activation(sq[i % 2][:], x[:, :, i * CH:(i + 1) * CH], ACT.Square).then_inc(s["sq"], 1)
                for i in range(NCH):
                    act.wait_ge(s["sum"], i + 1)
                    act.activation(root[:, i * CH:(i + 1) * CH], c.ps[i][:, 0:CH], ACT.Sqrt,
                                   scale=1.0 / D, bias=c.eps[:]).then_inc(s["root"], 1)
                for k in range(KD):
                    act.wait_ge(s["xn"], k + 1)
                    act.activation(h[:, k, 0:NPR], tmp[:, k, 0:NPR], ACT.Identity,
                                   scale=gs[:, k, 0:1], bias=sh[:, k, 0:1]).then_inc(s["h"], 1)
                if parts:
                    act.wait_ge(s["h"], KD + 1)
                    for k in range(KD):
                        act.activation(parts[0][:, k], h[:, k], ACT.Copy).then_inc(s["hi"], 1)

            @block.tensor
            def _(pe):
                for i in range(NCH):
                    pe.wait_ge(s["sq"], i + 1)
                    sum_squares(pe, c, c.ps[i], None, sq[i % 2], KD, s["sum"])

            @block.vector
            def _(dve):
                for i in range(NCH):
                    dve.wait_ge(s["root"], i + 1)
                    dve.reciprocal(inv[:, i * CH:(i + 1) * CH], root[:, i * CH:(i + 1) * CH]).then_inc(s["inv"], 1)
                dve.wait_ge(s["inv"], NCH)
                for k in range(KD):
                    dve.tensor_tensor(tmp[:, k], x[:, k], inv[:], ALU.mult).then_inc(s["xn"], 1)
                dve.wait_ge(s["xn"], KD)
                c.vstep(dve, dve.tensor_tensor(tmp[:, :, NPR:TOK], tmp[:, :, NPR:TOK], gs[:, :, 1:], ALU.mult))
                dve.tensor_tensor(h[:, :, NPR:TOK], tmp[:, :, NPR:TOK], sh[:, :, 1:], ALU.add).then_inc(s["h"], 1)
                if parts:
                    for k in range(KD):
                        dve.wait_ge(s["hi"], k + 1)
                        low_part(dve, parts[1][:, k], h[:, k], parts[0][:, k])


def normed_rows(dve, c, x, ss, root, inv, gain, width, sqrt_done, tn, ss_done):
    n, heads = x.shape[0], x.shape[1]
    tn.take(dve, sqrt_done)
    c.vstep(dve, dve.reciprocal(inv, root))
    c.vstep(dve, dve.tensor_tensor(x, x, inv.unsqueeze(2).to_broadcast([n, heads, width]), ALU.mult))
    c.vstep(dve, dve.tensor_tensor(x, x, gain[0:n].unsqueeze(1).to_broadcast([n, heads, width]), ALU.mult))


def rotate(dve, c, out, x, rot, tmp, done=None):
    n, heads = x.shape[0], x.shape[1]
    if len(rot.shape) == 2:
        rot = rot[0:n].unsqueeze(1).to_broadcast([n, heads, 2 * RH])
    cos, sin = rot[:, :, 0:RH], rot[:, :, RH:2 * RH]
    x1, x2 = x[:, :, 0:RH], x[:, :, RH:2 * RH]
    t = [tmp[0:n, i, 0:heads] for i in range(4)]
    dve.tensor_tensor(t[0], x1, cos, ALU.mult)
    dve.tensor_tensor(t[1], x2, sin, ALU.mult)
    dve.tensor_tensor(t[2], x2, cos, ALU.mult)
    c.vstep(dve, dve.tensor_tensor(t[3], x1, sin, ALU.mult))
    dve.tensor_tensor(out[:, :, 0:RH], t[0], t[1], ALU.subtract)
    ins = dve.tensor_tensor(out[:, :, RH:2 * RH], t[2], t[3], ALU.add)
    if done is None:
        c.vstep(dve, ins)
    else:
        ins.then_inc(done, 1)


def stage_mla_project(c):
    nc, IN, OUT = c.nc, c.IN, c.OUT
    HB = MH // 2
    with ExitStack() as ctx:
        sb = lambda t, shape: ctx.enter_context(nc.sbuf_tensor("mp_" + t, shape, F32))
        w_q = sb("w_q", [P, 2, KD, P])
        w_kv = sb("w_kv", [P, KD, LAT])
        w_uq = sb("w_uq", [P, 2, MH * QK])
        w_uk = sb("w_uk", [P, MH * NOPE])
        w_uv = sb("w_uv", [P, MH * VH])
        zq = sb("zq", [P, 2, TOK])
        sq = [sb(f"sq{i}", [P, 2, CH]) for i in range(2)]
        inv = sb("inv", [P, TOK])
        qs = sb("q", [P, MH, QK])
        qsq = sb("qsq", [P, MH, QK])
        kf = sb("k", [P, MH, QK])
        ksq = sb("ksq", [P, MH, NOPE])
        lat = [sb(f"lat{i}", [P, LAT]) for i in range(2)]
        junk = sb("junk", [P, LAT])
        st = sb("stats", [P, 8, MH])
        krr = sb("krr", [P, 1, ROPE])
        tmp = sb("tmp", [P, 4, MH, RH])
        ckT = sb("ckT", [P, P])
        names = ("w_in zq zcopy zsq zsum root cq cq_free q_mm q_copy kv_mm kv_copy q_ss q_root kv_root lat tr "
                 "trc kn_mm kn_copy v_mm v_copy k_ss k_root q_fin k_fin kT_mm kT_copy qT_mm qT_copy lat_out").split()
        s = {t: c.sem("mp_" + t) for t in names}
        lat_out = [s["lat_out"], c.sem("mp_lat_out1")]
        A, B, KV, TR, KN, V, X0, X1 = c.ps
        ss_q, root_q, inv_q = st[:, 0], st[:, 1], st[:, 2]
        ss_k, root_k, inv_k = st[:, 3], st[:, 4], st[:, 5]
        one = st[:, 6]
        with nc.Block() as block:
            @block.sync
            def _(sp):
                for m in range(2):
                    sp.dma_start(w_q[:, m], IN["w_q"][m]).then_inc(s["w_in"], 16)
                for dst, src in ((w_kv, "w_kv"), (w_uq, "w_uq"), (w_uk, "w_uk"), (w_uv, "w_uv")):
                    sp.dma_start(dst[:], IN[src]).then_inc(s["w_in"], 16)
                for t, (t0, n) in enumerate(TILES):
                    sp.wait_ge(s["lat"], t + 1)
                    dst = OUT["latent_prompt"][t0:t0 + n] if n == P else OUT["latent_sample"]
                    sp.dma_start(dst, lat[t % 2][0:n, :]).then_inc(lat_out[t % 2], 16)
                for i in range(2):
                    sp.wait_ge(lat_out[i], 16 * ((len(TILES) + 1 - i) // 2))

            @block.tensor
            def _(pe):
                tn = Turn()
                pe.wait_ge(s["w_in"], 96)
                for u in range(2 * NCH):
                    m, i = divmod(u, NCH)
                    for k in range(KD):
                        ins = pe.matmul(c.ps[u][:, 0:CH], w_q[:, m, k, :], c.hT[:, k, i * CH:(i + 1) * CH],
                                        start=(k == 0), stop=(k == KD - 1))
                    ins.then_inc(s["zq"], 1)
                for i in range(NCH):
                    tn.take(pe, s["zsq"])
                    if i == 2:
                        pe.wait_ge(s["root"], 1)
                    sum_squares(pe, c, c.ps[6 + i % 2], None, sq[i % 2], 2, s["zsum"])
                tn.take(pe, s["cq"], NCH)

                def project(t):
                    t0, n = TILES[t]
                    if t:
                        pe.wait_ge(s["q_copy"], 4 * t)
                        pe.wait_ge(s["kv_copy"], 2 * t)
                    for half, bank in ((0, A), (1, B)):
                        for k in range(2):
                            ins = pe.matmul(bank[0:n, 0:HB * QK], zq[:, k, t0:t0 + n],
                                            w_uq[:, k, half * HB * QK:(half + 1) * HB * QK],
                                            start=(k == 0), stop=(k == 1))
                        ins.then_inc(s["q_mm"], 1)
                    for k in range(KD):
                        ins = pe.matmul(KV[0:n, 0:LAT], c.hT[:, k, t0:t0 + n], w_kv[:, k, :],
                                        start=(k == 0), stop=(k == KD - 1))
                    ins.then_inc(s["kv_mm"], 1)

                def turn_heads(t, x, mm, copied, fin):
                    n = TILES[t][1]
                    pe.wait_ge(fin, t + 1)
                    for half, bank in ((0, X0), (1, X1)):
                        if fin is s["q_fin"]:
                            pe.wait_ge(s["kT_copy"], 2 * t + half + 1)
                        elif t:
                            pe.wait_ge(s["qT_copy"], 2 * t - 1 + half)
                        for h in range(HB):
                            ins = pe.transpose(bank[0:QK, h * P:h * P + n], x[0:n, half * HB + h, :],
                                               c.ident[0:n, 0:n])
                        ins.then_inc(mm, 1)

                project(0)
                for t, (t0, n) in enumerate(TILES):
                    pe.wait_ge(s["lat"], t + 1)
                    if t:
                        pe.wait_ge(s["trc"], t)
                    pe.transpose(TR[:, 0:n], lat[t % 2][0:n, 0:KVL], c.ident[0:n, 0:n]).then_inc(s["tr"], 1)
                    pe.wait_ge(s["trc"], t + 1)
                    if t:
                        pe.wait_ge(s["kn_copy"], 2 * t)
                        pe.wait_ge(s["v_copy"], t)
                    pe.matmul(KN[0:n, :], ckT[:, 0:n], w_uk[:], start=True, stop=True).then_inc(s["kn_mm"], 1)
                    pe.matmul(V[0:n, :], ckT[:, 0:n], w_uv[:], start=True, stop=True).then_inc(s["v_mm"], 1)
                    if t + 1 < len(TILES):
                        project(t + 1)
                    turn_heads(t, kf, s["kT_mm"], s["kT_copy"], s["k_fin"])
                    turn_heads(t, qs, s["qT_mm"], s["qT_copy"], s["q_fin"])

            @block.scalar
            def _(act):
                for i in range(NCH):
                    for m in range(2):
                        act.wait_ge(s["zq"], m * NCH + i + 1)
                        act.activation(zq[:, m, i * CH:(i + 1) * CH], c.ps[m * NCH + i][:, 0:CH], ACT.Copy)\
                           .then_inc(s["zcopy"], 1)
                        if i >= 2:
                            act.wait_ge(s["zsum"], i - 1)
                        ins = act.activation(sq[i % 2][:, m, :], c.ps[m * NCH + i][:, 0:CH], ACT.Square)
                    ins.then_inc(s["zsq"], 1)
                for i in range(NCH):
                    act.wait_ge(s["zsum"], i + 1)
                    act.activation(inv[:, i * CH:(i + 1) * CH], c.ps[6 + i % 2][:, 0:CH], ACT.Sqrt,
                                   scale=1.0 / QL, bias=c.eps[:]).then_inc(s["root"], 1)
                for t, (t0, n) in enumerate(TILES):
                    if t:
                        act.wait_ge(s["qT_mm"], 2 * t)
                    for half, bank in ((0, A), (1, B)):
                        act.wait_ge(s["q_mm"], 2 * t + half + 1)
                        hs = slice(half * HB, (half + 1) * HB)
                        src = bank[0:n, 0:HB * QK].rearrange("p (h d) -> p h d", d=QK)
                        act.activation(qs[0:n, hs, :], src, ACT.Copy).then_inc(s["q_copy"], 1)
                        if t and half == 0:
                            act.wait_ge(s["q_ss"], t)
                        act.activation(qsq[0:n, hs, :], src, ACT.Square).then_inc(s["q_copy"], 1)
                    act.wait_ge(s["kv_mm"], t + 1)
                    if t >= 2:
                        act.wait_ge(s["tr"], t - 1)
                        act.wait_ge(lat_out[t % 2], 16 * (t // 2))
                    if t:
                        act.wait_ge(s["k_fin"], t)
                    act.activation(lat[t % 2][0:n, :], KV[0:n, 0:LAT], ACT.Copy).then_inc(s["kv_copy"], 1)
                    c.astep(act, act.activation(junk[0:n, 0:KVL], KV[0:n, 0:KVL], ACT.Square,
                                                accum_out=one[0:n, 0:1]))
                    act.activation(one[0:n, 1:2], one[0:n, 0:1], ACT.Sqrt, scale=1.0 / KVL,
                                   bias=c.eps[0:n]).then_inc(s["kv_root"], 1)
                    act.activation(junk[0:n, KVL:LAT], KV[0:n, KVL:LAT], ACT.Square,
                                   accum_out=one[0:n, 3:4]).then_inc(s["kv_copy"], 1)
                    act.wait_ge(s["q_ss"], t + 1)
                    act.activation(root_q[0:n], ss_q[0:n], ACT.Sqrt, scale=1.0 / QK, bias=c.eps[0:n])\
                       .then_inc(s["q_root"], 1)
                    act.wait_ge(s["tr"], t + 1)
                    act.activation(ckT[:, 0:n], TR[:, 0:n], ACT.Copy).then_inc(s["trc"], 1)
                    act.wait_ge(s["kn_mm"], t + 1)
                    if t:
                        act.wait_ge(s["kT_mm"], 2 * t)
                    src = KN[0:n, :].rearrange("p (h d) -> p h d", d=NOPE)
                    act.activation(kf[0:n, :, 0:NOPE], src, ACT.Copy).then_inc(s["kn_copy"], 1)
                    act.activation(ksq[0:n], src, ACT.Square).then_inc(s["kn_copy"], 1)
                    act.wait_ge(s["v_mm"], t + 1)
                    if n == P:
                        act.activation(c.Vm[:, t, :], V[:, :], ACT.Copy).then_inc(s["v_copy"], 1)
                    act.wait_ge(s["k_ss"], t + 1)
                    act.activation(root_k[0:n], ss_k[0:n], ACT.Sqrt, scale=1.0 / QK, bias=c.eps[0:n])\
                       .then_inc(s["k_root"], 1)
                    for half, bank in ((0, X0), (1, X1)):
                        act.wait_ge(s["kT_mm"], 2 * t + half + 1)
                        dst = c.KT[:, :, t0:t0 + n] if n == P else c.KTs
                        act.activation(dst[:, half * HB:(half + 1) * HB, :],
                                       bank[0:QK, :].rearrange("p (h q) -> p h q", q=P)[:, :, 0:n],
                                       ACT.Copy).then_inc(s["kT_copy"], 1)

            @block.vector
            def _(dve):
                tn = Turn()
                for i in range(NCH):
                    tn.take(dve, s["root"])
                    cols = slice(i * CH, (i + 1) * CH)
                    c.vstep(dve, dve.reciprocal(inv[:, cols], inv[:, cols]))
                    dve.wait_ge(s["zcopy"], 2 * i + 2)
                    for m in range(2):
                        ins = dve.scalar_tensor_tensor(out=zq[:, m, cols], in0=zq[:, m, cols],
                                                       scalar=c.gT[:, 2 * KD + m:2 * KD + m + 1],
                                                       in1=inv[:, cols], op0=ALU.mult, op1=ALU.mult)
                    ins.then_inc(s["cq"], 1)
                for t, (t0, n) in enumerate(TILES):
                    L = lat[t % 2]
                    dve.wait_ge(s["q_copy"], 4 * t + 4)
                    dve.tensor_reduce(ss_q[0:n], qsq[0:n], AX.X, ALU.add).then_inc(s["q_ss"], 1)
                    dve.wait_ge(s["kv_root"], t + 1)
                    dve.wait_ge(s["kv_copy"], 2 * t + 2)
                    c.vstep(dve, dve.reciprocal(one[0:n, 2:3], one[0:n, 1:2]))
                    dve.scalar_tensor_tensor(out=L[0:n, 0:KVL], in0=L[0:n, 0:KVL], scalar=one[0:n, 2:3],
                                             in1=c.rows[0:n, R_KVL:R_KVL + KVL], op0=ALU.mult,
                                             op1=ALU.mult).then_inc(s["lat"], 1)
                    c.vstep(dve, dve.tensor_tensor(krr[0:n, 0], L[0:n, KVL:LAT],
                                                   c.rows[0:n, R_KN + NOPE:R_KN + QK], ALU.mult))
                    rotate(dve, c, krr[0:n], krr[0:n], c.rot[:, 0, t], tmp)
                    normed_rows(dve, c, qs[0:n], ss_q[0:n], root_q[0:n], inv_q[0:n],
                                c.rows[:, R_QN:R_QN + QK], QK, s["q_root"], tn, None)
                    rotate(dve, c, qs[0:n, :, NOPE:QK], qs[0:n, :, NOPE:QK], c.rot[:, 0, t], tmp,
                           s["q_fin"])
                    dve.wait_ge(s["kn_copy"], 2 * t + 2)
                    c.vstep(dve, dve.tensor_reduce(ss_k[0:n], ksq[0:n], AX.X, ALU.add))
                    dve.tensor_scalar(ss_k[0:n], ss_k[0:n], one[0:n, 3:4], None, ALU.add).then_inc(s["k_ss"], 1)
                    kn = kf[0:n, :, 0:NOPE]
                    normed_rows(dve, c, kn, ss_k[0:n], root_k[0:n], inv_k[0:n],
                                c.rows[:, R_KN:R_KN + NOPE], NOPE, s["k_root"], tn, None)
                    dve.tensor_tensor(kf[0:n, :, NOPE:QK], krr[0:n].to_broadcast([n, MH, ROPE]),
                                      inv_k[0:n].unsqueeze(2).to_broadcast([n, MH, ROPE]),
                                      ALU.mult).then_inc(s["k_fin"], 1)
                    for half, bank in ((0, X0), (1, X1)):
                        dve.wait_ge(s["qT_mm"], 2 * t + half + 1)
                        dst = c.QT[:, :, t0:t0 + n] if n == P else c.QTs
                        dve.tensor_copy(dst[:, half * HB:(half + 1) * HB, :],
                                        bank[0:QK, :].rearrange("p (h q) -> p h q", q=P)[:, :, 0:n])\
                           .then_inc(s["qT_copy"], 1)
                dve.wait_ge(s["lat"], len(TILES))
                dve.tensor_copy(c.lat_s[:], lat[(len(TILES) - 1) % 2][0:NSA, :])


def stage_attention(c, name, heads, width, QT, KT, V, span, finish, normed):
    nc = c.nc
    NT = NPR // P
    units = [(b, h) for b in range(NT) for h in range(heads)]
    U = len(units)
    HW = heads * width
    turns = []
    for u, (b, h) in enumerate(units):
        nb = span(b)[1]
        turns += [(u, j, min(4, nb - j)) for j in range(0, nb, 4)]
    ends = [max(i for i, g in enumerate(turns) if g[0] == u) + 1 for u in range(U)]
    kd = QT.shape[0]
    with ExitStack() as ctx:
        sb = lambda t, shape: ctx.enter_context(nc.sbuf_tensor(f"{name}_{t}", shape, F32))
        prob = [sb(f"prob{i}", [P, NPR if normed else 2 * P]) for i in range(2)]
        pT = [sb(f"pT{i}", [P, NT if normed else 2, P]) for i in range(2)]
        o = [sb(f"o{i}", [P, HW + 2 * heads]) for i in range(2)]
        rs = sb("rs", [P, 4])
        s = {t: c.sem(f"{name}_{t}") for t in "mm nmax exp turn copy pv out tile".split()}
        S = [c.ps[0:2], c.ps[2:4]]
        PT = c.ps[4:6]
        O = c.ps[6]

        def scores(pe, u):
            b, h = units[u]
            k0, nb, _, _ = span(b)
            if u >= 2:
                pe.wait_ge(s["exp"], u - 1)
            for j in range(0, nb, 4):
                w = min(4, nb - j) * P
                ins = pe.matmul(S[u % 2][j // 4][:, 0:w], QT[:, h, b * P:(b + 1) * P],
                                KT[:, h, (k0 + j) * P:(k0 + j) * P + w], start=True, stop=True)
            ins.then_inc(s["mm"], 1)

        with nc.Block() as block:
            @block.tensor
            def _(pe):
                scores(pe, 0)
                scores(pe, 1)
                for u, (b, h) in enumerate(units):
                    k0, nb, _, _ = span(b)
                    pe.wait_ge(s["exp"], u + 1)
                    for i, (v, j0, n) in enumerate(turns):
                        if v == u:
                            if i >= 2:
                                pe.wait_ge(s["copy"], i - 1)
                            for j in range(n):
                                ins = pe.transpose(PT[i % 2][:, j * P:(j + 1) * P],
                                                   prob[u % 2][:, (j0 + j) * P:(j0 + j + 1) * P], c.ident[:, :])
                            ins.then_inc(s["turn"], 1)
                    if u + 2 < U:
                        scores(pe, u + 2)
                    pe.wait_ge(s["copy"], ends[u])
                    if u:
                        pe.wait_ge(s["out"], u)
                    for j in range(nb):
                        ins = pe.matmul(O[:, h * width:(h + 1) * width], pT[u % 2][:, j, :],
                                        V[:, k0 + j, h * width:(h + 1) * width],
                                        start=(j == 0), stop=(j == nb - 1))
                    ins.then_inc(s["pv"], 1)
                    if h == heads - 1:
                        finish.tensor(pe, b, o[b % 2], s)

            @block.scalar
            def _(act):
                def exps(u):
                    b, h = units[u]
                    w = span(b)[1] * P
                    act.wait_ge(s["nmax"], u + 1)
                    if u >= 2:
                        act.wait_ge(s["turn"], ends[u - 2])
                        act.wait_ge(s["exp"], u - 1)
                    ot = o[b % 2]
                    for j in range(0, w, 512):
                        n = min(512, w - j)
                        acc = ot[:, HW + heads + h:HW + heads + h + 1] if j == 0 else rs[:, 2 + u % 2:3 + u % 2]
                        ins = act.activation(prob[u % 2][:, j:j + n], S[u % 2][j // 512][:, 0:n], ACT.Exp,
                                             bias=ot[:, HW + h:HW + h + 1], accum_out=acc)
                    if w > 512:
                        c.astep(act, ins)
                        acc = ot[:, HW + heads + h:HW + heads + h + 1]
                        ins = act.activation(acc, rs[:, 2 + u % 2:3 + u % 2], ACT.Identity, bias=acc)
                    ins.then_inc(s["exp"], 1)

                exps(0)
                for u, (b, h) in enumerate(units):
                    if u + 1 < U:
                        exps(u + 1)
                    for i, (v, j0, n) in enumerate(turns):
                        if v == u:
                            act.wait_ge(s["turn"], i + 1)
                            if u >= 2:
                                act.wait_ge(s["pv"], u - 1)
                            act.activation(pT[u % 2][:, j0:j0 + n, :],
                                           PT[i % 2][:, 0:n * P].rearrange("p (j q) -> p j q", q=P),
                                           ACT.Copy).then_inc(s["copy"], 1)
                    if h == heads - 1:
                        finish.scalar(act, b, o[b % 2], s)

            @block.vector
            def _(dve):
                def maxima(u):
                    b, h = units[u]
                    k0, nb, m0, mask = span(b)
                    dve.wait_ge(s["mm"], u + 1)
                    if h == 0 and b >= 2:
                        dve.wait_ge(finish.used, finish.per_tile * (b - 1))
                    bank = S[u % 2][m0 // 4]
                    at = (m0 % 4) * P
                    w = mask.shape[1]
                    c.vstep(dve, dve.tensor_tensor(bank[:, at:at + w], bank[:, at:at + w], mask, ALU.add))
                    ot = o[b % 2]
                    nm = ot[:, HW + h:HW + h + 1]
                    if nb <= 4:
                        ins = dve.tensor_reduce(nm, S[u % 2][0][:, 0:nb * P], AX.X, ALU.max, negate=True)
                    else:
                        dve.tensor_reduce(nm, S[u % 2][0][:, :], AX.X, ALU.max, negate=True)
                        c.vstep(dve, dve.tensor_reduce(rs[:, 0:1], S[u % 2][1][:, 0:(nb - 4) * P], AX.X,
                                                       ALU.max, negate=True))
                        ins = dve.tensor_tensor(nm, nm, rs[:, 0:1], ALU.min)
                    ins.then_inc(s["nmax"], 1)

                maxima(0)
                maxima(1)
                for u, (b, h) in enumerate(units):
                    if u + 2 < U:
                        maxima(u + 2)
                    ot = o[b % 2]
                    dst = ot[:, h * width:(h + 1) * width]
                    src = O[:, h * width:(h + 1) * width]
                    sm = ot[:, HW + heads + h:HW + heads + h + 1]
                    dve.wait_ge(s["exp"], u + 1)
                    if normed:
                        c.vstep(dve, dve.reciprocal(sm, sm))
                        dve.wait_ge(s["pv"], u + 1)
                        ins = dve.tensor_scalar(dst, src, sm, None, ALU.mult)
                    else:
                        dve.wait_ge(s["pv"], u + 1)
                        ins = dve.tensor_copy(dst, src)
                    ins.then_inc(s["out"], 1)

            @block.sync
            def _(sp):
                finish.sync(sp, o, s)


class TurnOutput:
    per_tile = 1

    def __init__(self, c, dst):
        self.c, self.dst = c, dst
        self.used, self.copied = c.sem("mo_turned"), c.sem("mo_copied")

    def tensor(self, pe, b, o, s):
        pe.wait_ge(s["out"], MH * (b + 1))
        if b:
            pe.wait_ge(self.copied, b)
        for k in range(MH * VH // P):
            ins = pe.transpose(self.c.ps[7][:, k * P:(k + 1) * P], o[:, k * P:(k + 1) * P], self.c.ident[:, :])
        ins.then_inc(self.used, 1)

    def scalar(self, act, b, o, s):
        act.wait_ge(self.used, b + 1)
        act.activation(self.dst[:, :, b * P:(b + 1) * P], self.c.ps[7][:].rearrange("p (k q) -> p k q", q=P),
                       ACT.Copy).then_inc(self.copied, 1)

    def sync(self, sp, o, s):
        pass


def stage_mla_sample(c):
    nc, IN = c.nc, c.IN
    R = MH * NSA
    Z = R + 1
    HALF = NPAGE // 2
    NQ = 2 * NSA
    with ExitStack() as ctx:
        sb = lambda t, shape, dt=F32: ctx.enter_context(nc.sbuf_tensor("ms_" + t, shape, dt))
        table = sb("page_table", [1, NSA * NPAGE], I32)
        rows = sb("rows", [P, NSA * NPAGE, LAT])
        w_ukT = sb("w_ukT", [NOPE, MH, KVL])
        w_uk = sb("w_uk", [P, MH * NOPE])
        w_uv = sb("w_uv", [P, MH * VH])
        diag = sb("diag", [R, NSA])
        qg = sb("qg", [NOPE, R])
        qwz = sb("qw_padded", [P, NSA * Z])
        qrz = sb("qr_padded", [ROPE, NSA * Z])
        qz = sb("q_padded", [QK, MH * (R + NSA)])
        krs = sb("krs", [P, NSA * NPAGE])
        krq = sb("krq", [P, NPAGE, ROPE])
        krr = [sb(f"krr{i}", [P, NPAGE, ROPE]) for i in range(2)]
        tmp = sb("tmp", [P, 4, NPAGE, RH])
        cT = [sb(f"cT{i}", [P, HALF * P]) for i in range(2)]
        krT = [sb(f"krT{i}", [ROPE, HALF * P]) for i in range(2)]
        ksq = [sb(f"ksq{i}", [P, MH, NOPE]) for i in range(2)]
        ms = sb("ms", [P, NPAGE, MH, NSA])
        invT = sb("invT", [R, PAST])
        sc = sb("scores", [R, PAST + NSA])
        st = sb("stats", [R, 4])
        pT = sb("pT", [P, NPAGE, R])
        pTn = sb("pT_new", [NSA, R])
        cx = sb("ctx", [P, R])
        s = {t: c.sem("ms_" + t) for t in ("w_in table prep qw kr tr trc kn sq red sc root inv invt invc new nmax "
                                           "exp norm pt ptc ctx ctxc out zero").split()}
        pages_in = [c.sem(f"ms_pages{b}") for b in range(NSA)]
        S = c.ps[6:8]
        with nc.Block() as block:
            @block.sync
            def _(sp):
                sp.dma_start(table[:], IN["page_table"]).then_inc(s["table"], 16)
                sp.wait_ge(s["table"], 16)
                for b in range(NSA):
                    with sp.Fori(b * NPAGE, (b + 1) * NPAGE) as i:
                        page = sp.value_load(table[0:1, bass.ds(i, 1)], min_val=0, max_val=IN["cache"].shape[0] - 1)
                        sp.dma_start(rows[:, bass.ds(i, 1), :].rearrange("p o d -> p (o d)"),
                                     IN["cache"][bass.ds(page, 1)].rearrange("o p d -> (o p) d"))\
                          .then_inc(pages_in[b], 16)

            @block.tensor
            def _(pe):
                pe.wait_ge(s["w_in"], 64)
                pe.wait_ge(s["prep"], 1)
                for h in range(MH):
                    ins = pe.matmul(c.ps[4][:, h * NSA:(h + 1) * NSA], w_ukT[:, h, :],
                                    qg[:, h * NSA:(h + 1) * NSA], start=True, stop=True)
                ins.then_inc(s["qw"], 1)

                def turn(q):
                    b, half = divmod(q, 2)
                    if half == 0:
                        pe.wait_ge(pages_in[b], 16 * NPAGE)
                        pe.wait_ge(s["kr"], b + 1)
                    if q >= 2:
                        pe.wait_ge(s["trc"], 2 * (q - 1))
                    for j in range(HALF):
                        pe.transpose(c.ps[q % 2][:, j * P:(j + 1) * P], rows[:, q * HALF + j, 0:KVL], c.ident[:, :])
                    for j in range(HALF):
                        ins = pe.transpose(c.ps[2 + q % 2][0:ROPE, j * P:(j + 1) * P],
                                           krr[b % 2][:, half * HALF + j, :], c.ident[:, :])
                    ins.then_inc(s["tr"], 1)

                turn(0)
                for q in range(NQ):
                    b, half = divmod(q, 2)
                    if q + 1 < NQ:
                        turn(q + 1)
                    pe.wait_ge(s["trc"], 2 * q + 2)
                    pe.wait_ge(s["prep"], 4)
                    for j in range(HALF):
                        n = q * HALF + j
                        if n >= 2:
                            pe.wait_ge(s["sq"], n - 1)
                        pe.matmul(c.ps[4 + n % 2][:, :], cT[q % 2][:, j * P:(j + 1) * P], w_uk[:],
                                  start=True, stop=True).then_inc(s["kn"], 1)
                    pe.matmul(S[half][0:R, :], qwz[:, b * R:(b + 1) * R], cT[q % 2][:, :],
                              start=(b == 0), stop=False)
                    pe.matmul(S[half][0:R, :], qrz[:, b * R:(b + 1) * R], krT[q % 2][:, :],
                              start=False, stop=(b == NSA - 1)).then_inc(s["sc"], 1)
                pe.wait_ge(s["inv"], 1)
                for j in range(NPAGE):
                    ins = pe.transpose(c.ps[j // HALF][0:R, (j % HALF) * P:(j % HALF + 1) * P],
                                       ms[:, j].rearrange("p h b -> p (h b)"), c.ident[:, :])
                ins.then_inc(s["invt"], 1)
                for h in range(MH):
                    ins = pe.matmul(c.ps[2][0:R, 0:NSA], qz[:, h * R:(h + 1) * R], c.KTs[:, h, :],
                                    start=(h == 0), stop=(h == MH - 1))
                ins.then_inc(s["new"], 1)
                pe.wait_ge(s["norm"], 1)
                for j in range(NPAGE):
                    ins = pe.transpose(c.ps[4][:, j * R:(j + 1) * R], sc[:, j * P:(j + 1) * P], c.ident[0:R, 0:R])
                pe.transpose(c.ps[5][0:NSA, 0:R], sc[:, PAST:PAST + NSA], c.ident[0:R, 0:R]).then_inc(s["pt"], 1)
                pe.wait_ge(s["ptc"], 2)
                pe.matmul(c.ps[3][:, 0:R], c.lat_s[:, 0:KVL], pTn[:], start=True, stop=False)
                for b in range(NSA):
                    for j in range(NPAGE):
                        last = b == NSA - 1 and j == NPAGE - 1
                        ins = pe.matmul(c.ps[3][:, b:R:NSA], rows[:, b * NPAGE + j, 0:KVL], pT[:, j, b:R:NSA],
                                        start=False, stop=last)
                ins.then_inc(s["ctx"], 1)
                pe.wait_ge(s["ctxc"], 1)
                for h in range(MH):
                    p0, k = VH * (h % 2), h // 2
                    ins = pe.matmul(c.ps[2][p0:p0 + VH, k * NSA:(k + 1) * NSA], w_uv[:, h * VH:(h + 1) * VH],
                                    cx[:, h * NSA:(h + 1) * NSA], start=True, stop=True)
                ins.then_inc(s["out"], 1)

            @block.scalar
            def _(act):
                for dst, src in ((w_ukT, "w_ukT"), (w_uk, "w_uk"), (w_uv, "w_uv"), (diag, "diag")):
                    act.dma_start(dst[:], IN[src]).then_inc(s["w_in"], 16)

                def copies(q):
                    act.wait_ge(s["tr"], q + 1)
                    if q >= 2:
                        act.wait_ge(s["sc"], q - 1)
                    act.activation(cT[q % 2][:], c.ps[q % 2][:], ACT.Copy).then_inc(s["trc"], 1)
                    act.activation(krT[q % 2][:], c.ps[2 + q % 2][0:ROPE, :], ACT.Copy).then_inc(s["trc"], 1)

                copies(0)
                for q in range(NQ):
                    if q + 1 < NQ:
                        copies(q + 1)
                    for j in range(HALF):
                        n = q * HALF + j
                        act.wait_ge(s["kn"], n + 1)
                        if n >= 2:
                            act.wait_ge(s["red"], n - 1)
                        act.activation(ksq[n % 2][:], c.ps[4 + n % 2][:].rearrange("p (h d) -> p h d", d=NOPE),
                                       ACT.Square).then_inc(s["sq"], 1)
                act.wait_ge(s["root"], 1)
                act.activation(ms[:], ms[:], ACT.Sqrt, scale=1.0 / QK, bias=c.eps[:]).then_inc(s["root"], 1)
                act.wait_ge(s["invt"], 1)
                for i in range(2):
                    act.activation(invT[:, i * 512:(i + 1) * 512], c.ps[i][0:R, :], ACT.Copy).then_inc(s["invc"], 1)
                act.wait_ge(s["nmax"], 1)
                act.activation(sc[:], sc[:], ACT.Exp, bias=st[:, 0:1], accum_out=st[:, 1:2]).then_inc(s["exp"], 1)
                act.wait_ge(s["pt"], 1)
                act.activation(pT[:], c.ps[4][:].rearrange("p (j r) -> p j r", r=R), ACT.Copy).then_inc(s["ptc"], 1)
                act.activation(pTn[:], c.ps[5][0:NSA, 0:R], ACT.Copy).then_inc(s["ptc"], 1)

            @block.vector
            def _(dve):
                for t in (qwz, qrz, qz):
                    ins = dve.memset(t[:], 0.0)
                c.vstep(dve, ins)
                dve.tensor_scalar(qg[:], c.QTs[0:NOPE].rearrange("p h b -> p (h b)"), c.gT[0:NOPE, 18:19], None,
                                  ALU.mult).then_inc(s["prep"], 1)
                dve.tensor_copy(qrz[:].rearrange("p (b x) -> p b x", x=Z)[:, :, 0:R:NSA],
                                c.QTs[NOPE:QK].rearrange("p h b -> p b h")).then_inc(s["prep"], 1)
                dve.tensor_copy(qz[:].rearrange("p (h x) -> p h x", x=R + NSA)[:, :, 0:NSA], c.QTs[:])\
                   .then_inc(s["prep"], 1)
                dve.wait_ge(s["qw"], 1)
                dve.tensor_copy(qwz[:].rearrange("p (b x) -> p b x", x=Z)[:, :, 0:R:NSA],
                                c.ps[4][:, 0:R].rearrange("p (h b) -> p b h", b=NSA)).then_inc(s["prep"], 1)

                def rope_keys(b):
                    pg = slice(b * NPAGE, (b + 1) * NPAGE)
                    dve.wait_ge(pages_in[b], 16 * NPAGE)
                    if b >= 2:
                        dve.wait_ge(s["tr"], 2 * (b - 1))
                    kr = rows[:, pg, KVL:LAT]
                    gain = c.rows[:, R_KN + NOPE:R_KN + QK].unsqueeze(1).to_broadcast([P, NPAGE, ROPE])
                    dve.tensor_tensor(krr[b % 2][:], kr, gain, ALU.mult)
                    c.vstep(dve, dve.tensor_tensor(krq[:], kr, kr, ALU.mult))
                    dve.tensor_reduce(krs[:, pg], krq[:], AX.X, ALU.add)
                    rotate(dve, c, krr[b % 2], krr[b % 2], c.rot[:, 0, 0:NPAGE, :], tmp, s["kr"])

                rope_keys(0)
                for b in range(NSA):
                    if b + 1 < NSA:
                        rope_keys(b + 1)
                    for j in range(NPAGE):
                        n = b * NPAGE + j
                        dve.wait_ge(s["sq"], n + 1)
                        dve.tensor_reduce(ms[:, j, :, b], ksq[n % 2][:], AX.X, ALU.add).then_inc(s["red"], 1)
                dve.wait_ge(s["red"], NSA * NPAGE)
                ins = dve.tensor_tensor(ms[:], ms[:], krs[:].rearrange("p (b j) -> p j b", j=NPAGE).unsqueeze(2)
                                        .to_broadcast([P, NPAGE, MH, NSA]), ALU.add)
                ins.then_inc(s["root"], 1)
                dve.wait_ge(s["root"], 2)
                dve.reciprocal(ms[:], ms[:]).then_inc(s["inv"], 1)
                dve.wait_ge(s["new"], 1)
                dve.wait_ge(s["w_in"], 64)
                dve.tensor_tensor(sc[:, PAST:PAST + NSA], c.ps[2][0:R, 0:NSA], diag[:], ALU.add)
                for i in range(2):
                    dve.wait_ge(s["sc"], 2 * NSA)
                    dve.wait_ge(s["invc"], i + 1)
                    cols = slice(i * 512, (i + 1) * 512)
                    ins = dve.tensor_tensor(sc[:, cols], S[i][0:R, :], invT[:, cols], ALU.mult)
                c.vstep(dve, ins)
                dve.tensor_reduce(st[:, 0:1], sc[:], AX.X, ALU.max, negate=True).then_inc(s["nmax"], 1)
                dve.wait_ge(s["exp"], 1)
                c.vstep(dve, dve.reciprocal(st[:, 2:3], st[:, 1:2]))
                dve.tensor_scalar(sc[:], sc[:], st[:, 2:3], None, ALU.mult).then_inc(s["norm"], 1)
                dve.wait_ge(s["ctx"], 1)
                dve.tensor_copy(cx[:], c.ps[3][:, 0:R]).then_inc(s["ctxc"], 1)
                dve.wait_ge(s["out"], 1)
                dve.tensor_copy(c.o_mlaT[:, :, NPR:TOK], c.ps[2][:, 0:MH // 2 * NSA]
                                .rearrange("p (k b) -> p k b", b=NSA))


def tail_rows(OUT, g, b, kv):
    keep = min(GROUPS[g][0], NPR)
    out = OUT[f"dil{g}_prompt"][:, kv, :]
    if g == 0 and b < NPR // P - keep // P or g == 1 and b % 2 == 0:
        return []
    return [(slice(0, P), out[sub_slice(g, b, NPR - keep)])]


def stage_dilated_project(c, g, w, sb):
    nc, IN, OUT = c.nc, c.IN, c.OUT
    NB = len(TILES)
    if True:
        z = [sb(f"z{i}", [P, DH, DE]) for i in range(3)]
        sq = [sb(f"zsq{i}", [P, DH, DE]) for i in range(2)]
        st = [sb(f"zst{i}", [P, 3, DH]) for i in range(2)]
        tmp = sb("ztmp", [P, 4, DH, RH])
        s = {t: c.sem(f"dp{g}_{t}") for t in
             "mm zcopy zsq ss root fin tr trc vcopy k_out v_out".split()}
        w_in = [c.sem(f"dp{g}_w{i}") for i in range(3)]
        k_out = [c.sem(f"dp{g}_k_out{i}") for i in range(3)]
        units = [(ch, b) for ch in range(3) for b in range(NB)]
        n_norm = 2 * NB
        stores = [[], [], []]

        def z_stores(v):
            ch, b = units[v]
            if b == NB - 1:
                dst = c.dram["q_dil_sample"][g].rearrange("(b f) -> b f", f=GW) if ch == 0 \
                    else OUT[f"dil{g}_sample"][:, 0, :]
                return [(slice(0, NSA), dst)]
            return tail_rows(OUT, g, b, 0) if ch == 1 else []

        def stored(v):
            return 16 * sum(len(z_stores(x)) for x in range(v % 3, v + 1, 3))

        with nc.Block() as block:
            @block.gpsimd
            def _(pool):
                for ch in range(3):
                    if ch == 2:
                        pool.wait_ge(s["mm"], NB)
                    pool.dma_start(w[ch % 2][:], IN["w_dil"][ch * NG + g]).then_inc(w_in[ch], 16)

            @block.sync
            def _(sp):
                for v in range(n_norm):
                    lots = z_stores(v)
                    if lots:
                        sp.wait_ge(s["fin"], v + 1)
                    for rows, dst in lots:
                        sp.dma_start(dst, z[v % 3][rows].rearrange("p h d -> p (h d)")).then_inc(k_out[v % 3], 16)
                count = 0
                for b in range(NB):
                    lots = tail_rows(OUT, g, b, 1) if b < NB - 1 else [(slice(0, NSA), OUT[f"dil{g}_sample"][:, 1, :])]
                    if lots:
                        sp.wait_ge(s["vcopy"], b + 1)
                    for rows, dst in lots:
                        src = c.dV[rows, b, :] if b < NB - 1 else c.dvs[:, g, :]
                        sp.dma_start(dst, src).then_inc(s["v_out"], 16)
                        count += 1
                sp.wait_ge(s["v_out"], 16 * count)
                for i in range(3):
                    sp.wait_ge(k_out[i], stored(n_norm - 3 + i))

            @block.tensor
            def _(pe):
                def turn(v):
                    n = TILES[units[v][1]][1]
                    pe.wait_ge(s["fin"], v + 1)
                    if v >= 2:
                        pe.wait_ge(s["trc"], v - 1)
                    bank = c.ps[4 + v % 2]
                    for h in range(DH):
                        ins = pe.transpose(bank[:, h * P:h * P + n], z[v % 3][0:n, h, :], c.ident[0:n, 0:n])
                    ins.then_inc(s["tr"], 1)

                for v, (ch, b) in enumerate(units):
                    if b == 0:
                        pe.wait_ge(w_in[ch], 16)
                    if v >= 4:
                        x = v - 4
                        pe.wait_ge(s["zsq"], min(x, n_norm - 1) + 1)
                        if x >= n_norm:
                            pe.wait_ge(s["vcopy"], x - n_norm + 1)
                    n = TILES[b][1]
                    for k in range(KD):
                        tok = c.hT[:, k, NPR:TOK] if n == NSA else c.hT[:, k, sub_slice(g, b)]
                        ins = pe.matmul(c.ps[v % 4][0:n, :], tok, w[ch % 2][:, k, :],
                                        start=(k == 0), stop=(k == KD - 1))
                    ins.then_inc(s["mm"], 1)
                    if 1 <= v <= n_norm:
                        turn(v - 1)

            @block.scalar
            def _(act):
                def turned(v):
                    ch, b = units[v]
                    n = TILES[b][1]
                    act.wait_ge(s["tr"], v + 1)
                    if b == NB - 1:
                        dst = (c.dqs, c.dks)[ch][:, g]
                    else:
                        dst = (c.dQ, c.dK)[ch][:, :, b * P:(b + 1) * P]
                    act.activation(dst, c.ps[4 + v % 2][:].rearrange("p (h q) -> p h q", q=P)[:, :, 0:n],
                                   ACT.Copy).then_inc(s["trc"], 1)

                for v, (ch, b) in enumerate(units):
                    n = TILES[b][1]
                    act.wait_ge(s["mm"], v + 1)
                    src = c.ps[v % 4][0:n, :]
                    if ch == 2:
                        dst = c.dV[:, b, :] if b < NB - 1 else c.dvs[:, g, :]
                        act.activation(dst, src, ACT.Copy).then_inc(s["vcopy"], 1)
                    else:
                        if v >= 3:
                            act.wait_ge(s["tr"], v - 2)
                            if stored(v - 3):
                                act.wait_ge(k_out[v % 3], stored(v - 3))
                        src = src.rearrange("p (h d) -> p h d", d=DE)
                        act.activation(z[v % 3][0:n], src, ACT.Copy).then_inc(s["zcopy"], 1)
                        if v >= 2:
                            act.wait_ge(s["ss"], v - 1)
                        act.activation(sq[v % 2][0:n], src, ACT.Square).then_inc(s["zsq"], 1)
                        act.wait_ge(s["ss"], v + 1)
                        act.activation(st[v % 2][0:n, 1], st[v % 2][0:n, 0], ACT.Sqrt, scale=1.0 / DE,
                                       bias=c.eps[0:n]).then_inc(s["root"], 1)
                    if 1 <= v <= n_norm:
                        turned(v - 1)

            @block.vector
            def _(dve):
                tn = Turn()
                for v in range(n_norm):
                    ch, b = units[v]
                    n = TILES[b][1]
                    gain = c.rows[:, R_DQ:R_DQ + DE] if ch == 0 else c.rows[:, R_DK:R_DK + DE]
                    x, t = z[v % 3][0:n], st[v % 2]
                    dve.wait_ge(s["zsq"], v + 1)
                    dve.tensor_reduce(t[0:n, 0], sq[v % 2][0:n], AX.X, ALU.add).then_inc(s["ss"], 1)
                    normed_rows(dve, c, x, t[0:n, 0], t[0:n, 1], t[0:n, 2], gain, DE, s["root"], tn, None)
                    rotate(dve, c, x[:, :, 0:ROPE], x[:, :, 0:ROPE], c.rot[:, 1 + g, b], tmp, s["fin"])


def dilated_span(c, g, b):
    if g == 2:
        return b, 1, 0, c.masks[:, 2, :]
    if b == 0 or g == 1 and b % 2 == 0:
        return b, 1, 0, c.masks[:, 1, :]
    return b - 1, 2, 0, c.masks[:, 0:2, :].rearrange("p m k -> p (m k)")


class StoreOutput:

    def __init__(self, c, g):
        self.c, self.g = c, g
        self.used = c.sem(f"da{g}_stored")
        self.per_tile = 16

    def tensor(self, pe, b, o, s):
        pass

    def scalar(self, act, b, o, s):
        pass

    def sync(self, sp, o, s):
        for b in range(NPR // P):
            sp.wait_ge(s["out"], DH * (b + 1))
            sp.dma_start(self.c.dram["o_group"][self.g][sub_slice(self.g, b)], o[b % 2][:]).then_inc(self.used, 16)
        sp.wait_ge(self.used, self.per_tile * (NPR // P))


def stage_dilated_combine(c):
    nc = c.nc
    W = GW + 2 * DH
    with ExitStack() as ctx:
        sb = lambda t, shape: ctx.enter_context(nc.sbuf_tensor("dc_" + t, shape, F32))
        x = [sb(f"x{i}", [P, NG, W]) for i in range(2)]
        e = sb("e", [P, NG, DH])
        den = sb("den", [P, NG, DH])
        m = sb("m", [P, DH])
        y = [sb(f"y{i}", [P, GW]) for i in range(2)]
        x_in = [c.sem(f"dc_x_in{i}") for i in range(2)]
        s = {t: c.sem("dc_" + t) for t in "diff exp y turn copy".split()}
        NT = NPR // P
        with nc.Block() as block:
            @block.sync
            def _(sp):
                for t in range(NT):
                    if t >= 2:
                        sp.wait_ge(s["y"], t - 1)
                    sp.dma_start(x[t % 2][:], c.dram["o_group"][:, t * P:(t + 1) * P, :]
                                 .rearrange("g p w -> p g w")).then_inc(x_in[t % 2], 16)

            @block.vector
            def _(dve):
                for t in range(NT):
                    X = x[t % 2]
                    nm, sm = X[:, :, GW:GW + DH], X[:, :, GW + DH:W]
                    dve.wait_ge(x_in[t % 2], 16 * (t // 2 + 1))
                    c.vstep(dve, dve.tensor_tensor(m[:], nm[:, 0], nm[:, 1], ALU.min))
                    c.vstep(dve, dve.tensor_tensor(m[:], m[:], nm[:, 2], ALU.min))
                    dve.tensor_tensor(e[:], m[:].unsqueeze(1).to_broadcast([P, NG, DH]), nm,
                                      ALU.subtract).then_inc(s["diff"], 1)
                    dve.wait_ge(s["exp"], t + 1)
                    c.vstep(dve, dve.tensor_tensor(den[:], e[:], sm, ALU.mult))
                    c.vstep(dve, dve.tensor_tensor(den[:, 0], den[:, 0], den[:, 1], ALU.add))
                    c.vstep(dve, dve.tensor_tensor(den[:, 0], den[:, 0], den[:, 2], ALU.add))
                    c.vstep(dve, dve.reciprocal(den[:, 1], den[:, 0]))
                    c.vstep(dve, dve.tensor_tensor(e[:], e[:], den[:, 1:2].to_broadcast([P, NG, DH]), ALU.mult))
                    if t >= 2:
                        dve.wait_ge(s["turn"], t - 1)
                    Y = y[t % 2]
                    for g in range(NG):
                        for h in range(DH):
                            cols = slice(h * DE, (h + 1) * DE)
                            if g == 0:
                                ins = dve.tensor_scalar(Y[:, cols], X[:, g, cols], e[:, g, h:h + 1], None, ALU.mult)
                            else:
                                ins = dve.scalar_tensor_tensor(out=Y[:, cols], in0=X[:, g, cols],
                                                               scalar=e[:, g, h:h + 1], in1=Y[:, cols],
                                                               op0=ALU.mult, op1=ALU.add)
                        if g < NG - 1:
                            c.vstep(dve, ins)
                    ins.then_inc(s["y"], 1)

            @block.scalar
            def _(act):
                for t in range(NT):
                    act.wait_ge(s["diff"], t + 1)
                    act.activation(e[:], e[:], ACT.Exp).then_inc(s["exp"], 1)
                    act.wait_ge(s["turn"], t + 1)
                    act.activation(c.o_dilT[:, :, t * P:(t + 1) * P],
                                   c.ps[t % 2][:].rearrange("p (k q) -> p k q", q=P), ACT.Copy).then_inc(s["copy"], 1)

            @block.tensor
            def _(pe):
                for t in range(NT):
                    pe.wait_ge(s["y"], t + 1)
                    if t >= 2:
                        pe.wait_ge(s["copy"], t - 1)
                    for k in range(GW // P):
                        ins = pe.transpose(c.ps[t % 2][:, k * P:(k + 1) * P], y[t % 2][:, k * P:(k + 1) * P],
                                           c.ident[:, :])
                    ins.then_inc(s["turn"], 1)


def stage_dilated_sample(c):
    nc, IN = c.nc, c.IN
    R = DH * NSA
    KROWS = [128, 128, 64]
    with ExitStack() as ctx:
        sb = lambda t, shape, dt=F32: ctx.enter_context(nc.sbuf_tensor("ds_" + t, shape, dt))
        kv = [sb(f"kv{i}", [P, 2, 2 * GW]) for i in range(3)]
        V = [sb(f"v{g}", [P, NSA, GW]) for g in range(NG)]
        qb = [sb(f"qb{i}", [P, 2, GW]) for i in range(3)]
        prod = sb("prod", [P, 2, GW])
        sT = sb("scoresT", [P, NG, DH, NSA])
        qz = sb("q_padded", [P, NG, DH * (R + NSA)])
        diag = sb("diag", [R, NSA])
        sc = sb("scores", [R, NG, P + NSA])
        st = sb("stats", [R, 4])
        pT = sb("pT", [P, NG, R])
        pTn = sb("pT_new", [NSA, NG, R])
        s = {t: c.sem("ds_" + t) for t in "diag zero kT t new fill nmax exp norm pt ptc out qz vv".split()}
        kv_in = [c.sem(f"ds_kv_in{i}") for i in range(3)]
        pairs = [(g, b) for g in range(NG) for b in range(0, NSA, 2)]
        with nc.Block() as block:
            @block.sync
            def _(sp):
                sp.dma_start(diag[:], IN["diag"][0:R]).then_inc(s["diag"], 16)
                for i, (g, b) in enumerate(pairs):
                    if i >= 3:
                        sp.wait_ge(s["kT"], i - 2)
                        sp.wait_ge(s["vv"], i - 2)
                    n, step = KROWS[g], GROUPS[g][1]
                    src = IN[f"state{g}"][b:b + 2, 0:step * (n - 1) + 1:step, :].rearrange("b p f -> p b f")
                    sp.dma_start(kv[i % 3][0:n], src).then_inc(kv_in[i % 3], 16)
                    q = c.dram["q_dil_sample"][g, b * GW:(b + 2) * GW].unsqueeze(0).to_broadcast([n, 2 * GW])
                    sp.dma_start(qb[i % 3][0:n].rearrange("p b f -> p (b f)"), q).then_inc(kv_in[i % 3], 16)

            @block.gpsimd
            def _(pool):
                pool.memset(sT[:], NEG).then_inc(s["zero"], 1)

            @block.scalar
            def _(act):
                for i, (g, b) in enumerate(pairs):
                    n = KROWS[g]
                    act.wait_ge(kv_in[i % 3], 32 * (i // 3 + 1))
                    act.activation(V[g][0:n, b:b + 2, :], kv[i % 3][0:n, :, GW:], ACT.Copy).then_inc(s["vv"], 1)
                act.wait_ge(s["nmax"], 1)
                act.activation(sc[:], sc[:], ACT.Exp, bias=st[:, 0:1], accum_out=st[:, 1:2]).then_inc(s["exp"], 1)
                act.wait_ge(s["pt"], 1)
                act.activation(pT[:], c.ps[2][:, 0:NG * R].rearrange("p (g r) -> p g r", r=R), ACT.Copy)\
                   .then_inc(s["ptc"], 1)
                act.activation(pTn[:], c.ps[3][0:NSA, 0:NG * R].rearrange("p (g r) -> p g r", r=R), ACT.Copy)\
                   .then_inc(s["ptc"], 1)

            @block.vector
            def _(dve):
                c.vstep(dve, dve.memset(qz[:], 0.0))
                for g in range(NG):
                    ins = dve.tensor_copy(qz[:, g].rearrange("p (h x) -> p h x", x=R + NSA)[:, :, 0:NSA], c.dqs[:, g])
                ins.then_inc(s["qz"], 1)
                dve.wait_ge(s["zero"], 1)
                for i, (g, b) in enumerate(pairs):
                    n = KROWS[g]
                    dve.wait_ge(kv_in[i % 3], 32 * (i // 3 + 1))
                    if i:
                        dve.wait_ge(s["kT"], i)
                    c.vstep(dve, dve.tensor_tensor(prod[0:n], kv[i % 3][0:n, :, 0:GW], qb[i % 3][0:n], ALU.mult))
                    dve.tensor_reduce(sT[0:n, g, :, b:b + 2], prod[0:n].rearrange("p b (h e) -> p h b e", e=DE),
                                      AX.X, ALU.add).then_inc(s["kT"], 1)
                dve.wait_ge(s["new"], 1)
                dve.wait_ge(s["diag"], 16)
                dve.tensor_copy(sc[:, :, 0:P], c.ps[0][0:R, 0:NG * P].rearrange("p (g k) -> p g k", k=P))
                c.vstep(dve, dve.tensor_tensor(
                    sc[:, :, P:], c.ps[1][0:R, 0:NG * NSA].rearrange("p (g k) -> p g k", k=NSA),
                    diag[:].unsqueeze(1).to_broadcast([R, NG, NSA]), ALU.add))
                dve.tensor_reduce(st[:, 0:1], sc[:].rearrange("p g k -> p (g k)"), AX.X, ALU.max, negate=True)\
                   .then_inc(s["nmax"], 1)
                dve.wait_ge(s["exp"], 1)
                c.vstep(dve, dve.reciprocal(st[:, 2:3], st[:, 1:2]))
                dve.tensor_scalar(sc[:], sc[:], st[:, 2:3], None, ALU.mult).then_inc(s["norm"], 1)
                dve.wait_ge(s["out"], 1)
                dve.tensor_copy(c.o_dilT[:, :, NPR:TOK], c.ps[4][:, 0:R].rearrange("p (h b) -> p h b", b=NSA))

            @block.tensor
            def _(pe):
                pe.wait_ge(s["qz"], 1)
                pe.wait_ge(s["kT"], len(pairs))
                for g in range(NG):
                    pe.transpose(c.ps[0][0:R, g * P:(g + 1) * P], sT[:, g].rearrange("p h b -> p (h b)"), c.ident[:, :])
                for g in range(NG):
                    for h in range(DH):
                        ins = pe.matmul(c.ps[1][0:R, g * NSA:(g + 1) * NSA], qz[:, g, h * R:(h + 1) * R],
                                        c.dks[:, g, h, :], start=(h == 0), stop=(h == DH - 1))
                ins.then_inc(s["new"], 1)
                pe.wait_ge(s["norm"], 1)
                for g in range(NG):
                    pe.transpose(c.ps[2][:, g * R:(g + 1) * R], sc[:, g, 0:P], c.ident[0:R, 0:R])
                for g in range(NG):
                    ins = pe.transpose(c.ps[3][0:NSA, g * R:(g + 1) * R], sc[:, g, P:P + NSA], c.ident[0:R, 0:R])
                ins.then_inc(s["pt"], 1)
                pe.wait_ge(s["ptc"], 2)
                pe.wait_ge(s["vv"], len(pairs))
                for h in range(DH):
                    out = c.ps[4][:, h * NSA:(h + 1) * NSA]
                    for g in range(NG):
                        pe.matmul(out, c.dvs[:, g, h * DE:(h + 1) * DE], pTn[:, g, h * NSA:(h + 1) * NSA],
                                  start=(g == 0), stop=False)
                    for g in range(NG):
                        n = KROWS[g]
                        for b in range(NSA):
                            ins = pe.matmul(out[:, b:b + 1], V[g][0:n, b, h * DE:(h + 1) * DE],
                                            pT[0:n, g, h * NSA + b:h * NSA + b + 1],
                                            start=False, stop=(g == NG - 1 and b == NSA - 1))
                ins.then_inc(s["out"], 1)


def stage_mix(c):
    nc, IN = c.nc, c.IN
    KO = GW // P
    with ExitStack() as ctx:
        sb = lambda t, shape: ctx.enter_context(nc.sbuf_tensor("mx_" + t, shape, F32))
        w = [sb(f"w{i}", [P, 2 * KO + 2 * KD, P]) for i in range(2)]
        wo = [sb(f"w_out{i}", [P, KD, P]) for i in range(2)]
        x = sb("x", [P, KD, TOK])
        y = sb("y", [P, KD, TOK])
        sg = [sb(f"sig{i}", [P, 2, CH]) for i in range(2)]
        t = [sb(f"t{i}", [P, 2, CH]) for i in range(2)]
        ts = sb("ts", [P, KD, NSA])
        s = {n: c.sem("mx_" + n) for n in "x_in mm sig y out_mm out stored".split()}
        w_in = [c.sem(f"mx_w_in{i}") for i in range(2)]
        wo_in = [c.sem(f"mx_wo_in{i}") for i in range(2)]
        gate1 = c.mod[:, 2]
        units = [(m, i) for m in range(KD) for i in range(NCH)]
        with nc.Block() as block:
            @block.sync
            def _(sp):
                for m in range(KD):
                    if m >= 2:
                        sp.wait_ge(s["mm"], NCH * (m - 1))
                    for at, n, src in ((0, KO, IN["w_mla"][m]), (KO, KO, IN["w_dilb"][m]),
                                       (2 * KO, KD, IN["w_gate"][m]), (2 * KO + KD, KD, IN["w_gate"][KD + m])):
                        sp.dma_start(w[m % 2][:, at:at + n], src).then_inc(w_in[m % 2], 16)
                sp.dma_start(x[:], IN["xT"]).then_inc(s["x_in"], 16)
                for m in range(KD):
                    if m >= 2:
                        sp.wait_ge(s["out_mm"], NCH * (m - 1))
                    sp.dma_start(wo[m % 2][:], IN["w_out"][m]).then_inc(wo_in[m % 2], 16)
                for m in range(KD):
                    sp.wait_ge(s["out"], NCH * (m + 1))
                    sp.dma_start(c.dram["x1_dram"][:, m], x[:, m]).then_inc(s["stored"], 16)
                sp.wait_ge(s["stored"], 16 * KD)

            @block.tensor
            def _(pe):
                for u, (m, i) in enumerate(units):
                    cols = slice(i * CH, (i + 1) * CH)
                    if i == 0:
                        pe.wait_ge(w_in[m % 2], 64 * (m // 2 + 1))
                    if u >= 2:
                        pe.wait_ge(s["y"], u - 1)
                    bank = c.ps[4 * (u % 2):4 * (u % 2) + 4]
                    W = w[m % 2]
                    for n, (src, at, num) in enumerate(((c.hT, 2 * KO, KD), (c.hT, 2 * KO + KD, KD),
                                                        (c.o_mlaT, 0, KO), (c.o_dilT, KO, KO))):
                        for k in range(num):
                            ins = pe.matmul(bank[n][:, 0:CH], W[:, at + k, :], src[:, k, cols],
                                            start=(k == 0), stop=(k == num - 1))
                    ins.then_inc(s["mm"], 1)
                pe.wait_ge(s["y"], len(units))
                for u, (m, i) in enumerate(units):
                    if i == 0:
                        pe.wait_ge(wo_in[m % 2], 16 * (m // 2 + 1))
                    if u >= 4:
                        pe.wait_ge(s["out"], u - 3)
                    for k in range(KD):
                        ins = pe.matmul(c.ps[u % 4][:, 0:CH], wo[m % 2][:, k, :], y[:, k, i * CH:(i + 1) * CH],
                                        start=(k == 0), stop=(k == KD - 1))
                    ins.then_inc(s["out_mm"], 1)

            @block.scalar
            def _(act):
                for u in range(len(units)):
                    act.wait_ge(s["mm"], u + 1)
                    if u >= 2:
                        act.wait_ge(s["y"], u - 1)
                    for n in range(2):
                        ins = act.activation(sg[u % 2][:, n], c.ps[4 * (u % 2) + n][:, 0:CH], ACT.Sigmoid)
                    ins.then_inc(s["sig"], 1)

            @block.vector
            def _(dve):
                for u, (m, i) in enumerate(units):
                    dve.wait_ge(s["sig"], u + 1)
                    for n in range(2):
                        ins = dve.tensor_tensor(t[u % 2][:, n], sg[u % 2][:, n], c.ps[4 * (u % 2) + 2 + n][:, 0:CH],
                                                ALU.mult)
                    c.vstep(dve, ins)
                    dve.tensor_tensor(y[:, m, i * CH:(i + 1) * CH], t[u % 2][:, 0], t[u % 2][:, 1], ALU.add)\
                       .then_inc(s["y"], 1)
                dve.wait_ge(s["x_in"], 16)
                for u, (m, i) in enumerate(units):
                    a, e = i * CH, min((i + 1) * CH, NPR)
                    dve.wait_ge(s["out_mm"], u + 1)
                    ps = c.ps[u % 4]
                    ins = dve.scalar_tensor_tensor(out=x[:, m, a:e], in0=ps[:, 0:e - a], scalar=gate1[:, m, 0:1],
                                                   in1=x[:, m, a:e], op0=ALU.mult, op1=ALU.add)
                    if i == NCH - 1:
                        c.vstep(dve, dve.tensor_tensor(ts[:, m], ps[:, e - a:CH], gate1[:, m, 1:], ALU.mult))
                        ins = dve.tensor_tensor(x[:, m, NPR:TOK], x[:, m, NPR:TOK], ts[:, m], ALU.add)
                    ins.then_inc(s["out"], 1)


def stage_route(c):
    nc, IN = c.nc, c.IN
    NT = len(TILES)
    HP = 2 * PH
    with ExitStack() as ctx:
        sb = lambda t, shape, dt=F32: ctx.enter_context(nc.sbuf_tensor("rt_" + t, shape, dt))
        w = [sb(f"w{i}", [P, KD, P]) for i in range(2)]
        wp = [[sb(f"w_{t}{i}", [P, KD, P], F32R) for t in ("high", "low")] for i in range(2)]
        keys = sb("keysT", [P, HP, NK])
        qT = [sb(f"qT{i}", [P, TOK]) for i in range(2)]
        sc = [sb(f"sc{i}", [P, NT, NK]) for i in range(2)]
        sc2 = sb("sc_rest", [P, NT, NK])
        top = sb("top", [P, NT, PH, 2, TOPK])
        topi = sb("topi", [P, NT, PH, 2, TOPK], U32)
        topf = sb("topf", [P, PH, 2, TOPK])
        cand = [sb(f"cand{i}", [P, PH, TOPK * TOPK]) for i in range(2)]
        rest = sb("cand_rest", [P, PH, TOPK * TOPK])
        best = sb("best", [P, PH, TOPK])
        besti = sb("besti", [P, PH, TOPK], U32)
        part = sb("part", [P, 2, PH, TOPK], U32)
        partf = sb("partf", [P, 2, PH, TOPK])
        eq = [sb(f"eq{i}", [P, PH, TOPK, TOPK]) for i in range(2)]
        res = [sb(f"res{i}", [P, 3, PH * TOPK]) for i in range(2)]
        st = sb("stats", [P, 2, PH])
        s = {n: c.sem("rt_" + n) for n in "keys_in w_hi w_lo mm copy sc_mm sc_copy top diff exp res turn turned".split()}
        w_in = [c.sem(f"rt_w_in{i}") for i in range(2)]
        with nc.Block() as block:
            @block.sync
            def _(sp):
                sp.dma_start(keys[:], IN["keysT"]).then_inc(s["keys_in"], 16)
                for hp in range(HP):
                    if hp >= 2:
                        sp.wait_ge(s["w_lo"], hp - 1)
                    sp.dma_start(w[hp % 2][:], IN["w_pq"][hp]).then_inc(w_in[hp % 2], 16)

            @block.tensor
            def _(pe):
                def queries(hp):
                    pe.wait_ge(s["w_lo"], hp + 1)
                    for i in range(NCH):
                        if hp:
                            pe.wait_ge(s["copy"], NCH * (hp - 1) + i + 1)
                        for k in range(KD):
                            ins = product3(pe, c.ps[i][:, 0:CH], [x[:, k, :] for x in wp[hp % 2]],
                                           [x[:, k, i * CH:(i + 1) * CH] for x in c.hT2], k == 0, k == KD - 1)
                        ins.then_inc(s["mm"], 1)

                pe.wait_ge(s["keys_in"], 16)
                queries(0)
                for hp in range(HP):
                    if hp + 1 < HP:
                        queries(hp + 1)
                    pe.wait_ge(s["copy"], NCH * (hp + 1))
                    for t, (t0, n) in enumerate(TILES):
                        if hp and t % 4 == 0:
                            pe.wait_ge(s["sc_copy"], NCH * (hp - 1) + t // 4 + 1)
                        ins = pe.matmul(c.ps[3 + t // 4][0:n, (t % 4) * NK:(t % 4 + 1) * NK], qT[hp % 2][:, t0:t0 + n],
                                        keys[:, hp, :], start=True, stop=True)
                        if t % 4 == 3 or t == NT - 1:
                            ins.then_inc(s["sc_mm"], 1)
                for t, (t0, n) in enumerate(TILES):
                    pe.wait_ge(s["res"], t + 1)
                    if t:
                        pe.wait_ge(s["turned"], t)
                    for j in range(3):
                        ins = pe.transpose(c.ps[6][:, j * P:j * P + n], res[t % 2][0:n, j, :], c.ident[0:n, 0:n])
                    ins.then_inc(s["turn"], 1)

            @block.scalar
            def _(act):
                def queries(hp):
                    if hp >= 2:
                        act.wait_ge(s["sc_mm"], NCH * (hp - 1))
                    for i in range(NCH):
                        act.wait_ge(s["mm"], NCH * hp + i + 1)
                        act.activation(qT[hp % 2][:, i * CH:(i + 1) * CH], c.ps[i][:, 0:CH], ACT.Copy)\
                           .then_inc(s["copy"], 1)

                def high(hp):
                    act.wait_ge(w_in[hp % 2], 16 * (hp // 2 + 1))
                    if hp >= 2:
                        act.wait_ge(s["mm"], NCH * (hp - 1))
                    act.activation(wp[hp % 2][0][:], w[hp % 2][:], ACT.Copy).then_inc(s["w_hi"], 1)

                high(0)
                high(1)
                queries(0)
                for hp in range(HP):
                    if hp + 1 < HP:
                        queries(hp + 1)
                    if hp + 2 < HP:
                        high(hp + 2)
                    if hp >= 2:
                        act.wait_ge(s["top"], hp - 1)
                    for i in range(NCH):
                        act.wait_ge(s["sc_mm"], NCH * hp + i + 1)
                        if i < 2:
                            dst, src = sc[hp % 2][:, 4 * i:4 * i + 4], c.ps[3 + i][:]
                            act.activation(dst, src.rearrange("p (t k) -> p t k", k=NK), ACT.Copy)\
                               .then_inc(s["sc_copy"], 1)
                        else:
                            act.activation(sc[hp % 2][0:NSA, 8], c.ps[5][0:NSA, 0:NK], ACT.Copy)\
                               .then_inc(s["sc_copy"], 1)
                for t, (t0, n) in enumerate(TILES):
                    act.wait_ge(s["diff"], t + 1)
                    act.activation(best[0:n], best[0:n], ACT.Exp).then_inc(s["exp"], 1)
                    act.wait_ge(s["turn"], t + 1)
                    act.activation(c.pick[:, :, t0:t0 + n], c.ps[6][:, 0:3 * P].rearrange("p (j n) -> p j n", n=P)
                                   [:, :, 0:n], ACT.Copy).then_inc(s["turned"], 1)

            @block.vector
            def _(dve):
                def low(hp):
                    dve.wait_ge(s["w_hi"], hp + 1)
                    low_part(dve, wp[hp % 2][1][:], w[hp % 2][:], wp[hp % 2][0][:]).then_inc(s["w_lo"], 1)

                low(0)
                low(1)
                for hp in range(HP):
                    if hp + 2 < HP:
                        low(hp + 2)
                    S = sc[hp % 2]
                    T = lambda t, a: top[0:TILES[t][1], t, hp // 2, hp % 2, a:a + 8]
                    I = lambda t, a: topi[0:TILES[t][1], t, hp // 2, hp % 2, a:a + 8]
                    dve.wait_ge(s["sc_copy"], NCH * (hp + 1))
                    for t, (_, n) in enumerate(TILES):
                        ins = dve.max(T(t, 0), S[0:n, t])
                    c.vstep(dve, ins)
                    for t, (_, n) in enumerate(TILES):
                        dve.max_index(I(t, 0), T(t, 0), S[0:n, t])
                        ins = dve.match_replace(sc2[0:n, t], T(t, 0), S[0:n, t], NEG)
                    c.vstep(dve, ins)
                    for t, (_, n) in enumerate(TILES):
                        ins = dve.max(T(t, 8), sc2[0:n, t])
                    c.vstep(dve, ins)
                    for t, (_, n) in enumerate(TILES):
                        ins = dve.max_index(I(t, 8), T(t, 8), sc2[0:n, t])
                    c.vstep(dve, ins)
                    dve.engine_nop().then_inc(s["top"], 1)
                for t, (t0, n) in enumerate(TILES):
                    C, R = cand[t % 2], res[t % 2]
                    four = [n, PH, TOPK, TOPK]
                    c.vstep(dve, dve.tensor_tensor(C[0:n].rearrange("p h (a b) -> p h a b", b=TOPK),
                                                   top[0:n, t, :, 0].unsqueeze(3).to_broadcast(four),
                                                   top[0:n, t, :, 1].unsqueeze(2).to_broadcast(four), ALU.add))
                    if t:
                        dve.wait_ge(s["exp"], t)
                    for h in range(PH):
                        ins = dve.max(best[0:n, h, 0:8], C[0:n, h])
                    c.vstep(dve, ins)
                    for h in range(PH):
                        dve.max_index(besti[0:n, h, 0:8], best[0:n, h, 0:8], C[0:n, h])
                        ins = dve.match_replace(rest[0:n, h], best[0:n, h, 0:8], C[0:n, h], NEG)
                    c.vstep(dve, ins)
                    for h in range(PH):
                        ins = dve.max(best[0:n, h, 8:16], rest[0:n, h])
                    c.vstep(dve, ins)
                    for h in range(PH):
                        ins = dve.max_index(besti[0:n, h, 8:16], best[0:n, h, 8:16], rest[0:n, h])
                    c.vstep(dve, dve.tensor_copy(st[0:n, 0], best[0:n, :, 0]))
                    dve.tensor_tensor(best[0:n], best[0:n], st[0:n, 0].unsqueeze(2).to_broadcast([n, PH, TOPK]),
                                      ALU.subtract).then_inc(s["diff"], 1)
                    dve.tensor_scalar(part[0:n, 0], besti[0:n], 4, None, ALU.logical_shift_right)
                    dve.tensor_scalar(part[0:n, 1], besti[0:n], 15, None, ALU.bitwise_and)
                    c.vstep(dve, dve.tensor_copy(topf[0:n], topi[0:n, t]))
                    c.vstep(dve, dve.tensor_copy(partf[0:n], part[0:n]))
                    if t >= 2:
                        dve.wait_ge(s["turn"], t - 1)
                    for j in range(2):
                        c.vstep(dve, dve.tensor_tensor(
                            eq[j][0:n], partf[0:n, j].unsqueeze(3).to_broadcast(four),
                            c.iota[0:n, 0:TOPK].unsqueeze(1).unsqueeze(1).to_broadcast(four), ALU.is_equal))
                        c.vstep(dve, dve.tensor_tensor(
                            eq[j][0:n], eq[j][0:n], topf[0:n, :, j].unsqueeze(2).to_broadcast(four), ALU.mult))
                        dve.tensor_reduce(R[0:n, j].rearrange("p (h k) -> p h k", k=TOPK), eq[j][0:n], AX.X, ALU.add)
                    dve.wait_ge(s["exp"], t + 1)
                    c.vstep(dve, dve.tensor_reduce(st[0:n, 0], best[0:n], AX.X, ALU.add))
                    c.vstep(dve, dve.reciprocal(st[0:n, 1], st[0:n, 0]))
                    dve.tensor_tensor(R[0:n, 2].rearrange("p (h k) -> p h k", k=TOPK), best[0:n],
                                      st[0:n, 1].unsqueeze(2).to_broadcast([n, PH, TOPK]), ALU.mult)\
                       .then_inc(s["res"], 1)


def stage_gates(c):
    nc = c.nc
    QB, RQ = 8, 4
    BLK = 64
    TURNS = BLK // 4 // QB
    NBLK = NPR // BLK
    with ExitStack() as ctx:
        sb = lambda t, shape: ctx.enter_context(nc.sbuf_tensor("gt_" + t, shape, F32))
        first = [sb(f"first{i}", [P, 4, NK]) for i in range(RQ)]
        second = [sb(f"second{i}", [P, 4, NK]) for i in range(RQ)]
        stage = [sb(f"stage{i}", [P, NK, BLK]) for i in range(2)]
        s = {n: c.sem("gt_" + n) for n in "hot mm copy".split()}
        out = [c.sem(f"gt_out{i}") for i in range(2)]
        gates = c.dram["gates_dram"].rearrange("a b n -> b a n")
        NQ = TOK // 4
        TAIL = NSA // 4

        def hots(dve, r, quad, token):
            for i in range(4):
                pick = [c.pick[:, j, bass.ds(token + i, 1)] for j in range(3)]
                dve.tensor_scalar(first[r][:, i], c.iota[:], pick[0], pick[2], ALU.is_equal, ALU.mult)
                ins = dve.tensor_scalar(second[r][:, i], c.iota[:], pick[1], None, ALU.is_equal)
            ins.then_inc(s["hot"], 1)

        def products(pe, r, bank):
            for i in range(4):
                ins = pe.matmul(bank[:, i * NK:(i + 1) * NK], second[r][:, i], first[r][:, i], start=True, stop=True)
            ins.then_inc(s["mm"], 1)

        def to_stage(act, bank, buf, at):
            act.activation(buf[:, :, bass.ds(at, 4)].rearrange("p a n -> p n a"),
                           bank[:].rearrange("p (n a) -> p n a", a=NK), ACT.Copy).then_inc(s["copy"], 1)

        with nc.Block() as block:
            @block.vector
            def _(dve):
                for q in range(QB):
                    if q >= RQ:
                        dve.wait_ge(s["mm"], q - RQ + 1)
                    hots(dve, q % RQ, q, 4 * q)
                with dve.Fori(1, NPR // 4 // QB) as i:
                    for q in range(QB):
                        dve.wait_ge(s["mm"], i * QB + (q - RQ + 1))
                        hots(dve, q % RQ, i * QB + q, i * (4 * QB) + 4 * q)
                for q in range(NPR // 4, NQ):
                    dve.wait_ge(s["mm"], q - RQ + 1)
                    hots(dve, q % RQ, q, 4 * q)

            @block.tensor
            def _(pe):
                for q in range(QB):
                    pe.wait_ge(s["hot"], q + 1)
                    products(pe, q % RQ, c.ps[q])
                with pe.Fori(1, NPR // 4 // QB) as i:
                    for q in range(QB):
                        pe.wait_ge(s["hot"], i * QB + q + 1)
                        pe.wait_ge(s["copy"], (i - 1) * QB + q + 1)
                        products(pe, q % RQ, c.ps[q])
                for q in range(NPR // 4, NQ):
                    pe.wait_ge(s["hot"], q + 1)
                    pe.wait_ge(s["copy"], q - QB + 1)
                    products(pe, q % RQ, c.ps[q % QB])

            @block.scalar
            def _(act):
                for b in range(NBLK):
                    if b >= 2:
                        act.wait_ge(out[b % 2], 16 * (b // 2))
                    with act.Fori(0, TURNS) as i:
                        for q in range(QB):
                            act.wait_ge(s["mm"], i * QB + b * TURNS * QB + q + 1)
                            to_stage(act, c.ps[q], stage[b % 2], i * (4 * QB) + 4 * q)
                act.wait_ge(out[0], 16 * (NBLK // 2))
                for q in range(TAIL):
                    act.wait_ge(s["mm"], NPR // 4 + q + 1)
                    to_stage(act, c.ps[q], stage[0], 4 * q)

            @block.sync
            def _(sp):
                for b in range(NBLK):
                    sp.wait_ge(s["copy"], (b + 1) * BLK // 4)
                    sp.dma_start(gates[:, :, b * BLK:(b + 1) * BLK], stage[b % 2][:]).then_inc(out[b % 2], 16)
                sp.wait_ge(s["copy"], NQ)
                sp.dma_start(gates[:, :, NPR:TOK], stage[0][:, :, 0:NSA]).then_inc(out[0], 16)
                sp.wait_ge(out[0], 16 * (NBLK // 2 + 1))
                sp.wait_ge(out[1], 16 * (NBLK // 2))


def stage_experts(c):
    nc, IN = c.nc, c.IN
    GR = 2
    SL = 2 * GR
    UG = GR * NCH
    YG = KD * NCH
    NB = 4
    NGE = 3
    SPLIT_AT = (2, 7, 12, 18)
    turns = NK // SL
    with ExitStack() as ctx:
        sb = lambda t, shape, dt=F32: ctx.enter_context(nc.sbuf_tensor("ex_" + t, shape, dt))
        u = [sb(f"u{i}", [P, KD, P]) for i in range(GR)]
        v = [sb(f"v{i}", [P, D]) for i in range(GR)]
        g = [sb(f"g{i}", [P, TOK]) for i in range(GR)]
        up = [[sb(f"u_{t}{i}", [P, KD, P], F32R) for t in ("high", "low")] for i in range(GR)]
        vp = [[sb(f"v_{t}{i}", [P, D], F32R) for t in ("high", "low")] for i in range(SL)]
        ap = [[sb(f"a_{t}{i}", [P, TOK], F32R) for t in ("high", "low")] for i in range(SL)]
        ge = [sb(f"gelu{i}", [P, CH]) for i in range(NGE)]
        u_in, v_in, g_in = ([c.sem(f"ex_{t}_in{i}") for i in range(GR)] for t in "uvg")
        s = {n: c.sem("ex_" + n) for n in "s_mm gelu prod a_hi a_lo u_hi u_lo v_hi v_lo y_mm y".split()}
        SB, YB = c.ps[0:NB], c.ps[NB:2 * NB]

        def scores(pe, i, grp):
            for j in range(GR):
                pe.wait_ge(s["u_lo"], i * SL + grp * GR + j + 1)
                for ch in range(NCH):
                    unit = grp * UG + j * NCH + ch
                    if not (isinstance(i, int) and i == 0 and unit < NB):
                        pe.wait_ge(s["gelu"], i * (2 * UG) + unit - NB + 1)
                    for k in range(KD):
                        ins = product3(pe, SB[unit % NB][:, 0:CH], [x[:, k, :] for x in up[j]],
                                       [x[:, k, ch * CH:(ch + 1) * CH] for x in c.hT2], k == 0, k == KD - 1)
                    ins.then_inc(s["s_mm"], 1)

        def sums(pe, i, grp):
            pe.wait_ge(s["v_lo"], i * SL + (grp + 1) * GR)
            pe.wait_ge(s["a_lo"], i * (2 * UG) + (grp + 1) * UG)
            for n in range(YG):
                m, ch = divmod(n, NCH)
                unit = grp * YG + n
                if not (isinstance(i, int) and i == 0 and unit < NB):
                    pe.wait_ge(s["y"], i * (2 * YG) + unit - NB + 1)
                for j in range(GR):
                    sl = grp * GR + j
                    ins = product3(pe, YB[n % NB][:, 0:CH], [x[:, m * P:(m + 1) * P] for x in vp[sl]],
                                   [x[:, ch * CH:(ch + 1) * CH] for x in ap[sl]], j == 0, j == GR - 1)
                ins.then_inc(s["y_mm"], 1)

        def u_high(act, i, grp):
            for j in range(GR):
                act.wait_ge(u_in[j], i * 32 + grp * 16 + 16)
                if not (isinstance(i, int) and i == 0 and grp == 0):
                    act.wait_ge(s["s_mm"], i * (2 * UG) + (grp - 1) * UG + (j + 1) * NCH)
                act.activation(up[j][0][:], u[j][:], ACT.Copy).then_inc(s["u_hi"], 1)

        def v_high(act, i, grp):
            for j in range(GR):
                act.wait_ge(v_in[j], i * 32 + grp * 16 + 16)
                act.activation(vp[grp * GR + j][0][:], v[j][:], ACT.Copy).then_inc(s["v_hi"], 1)

        def gelus(act, i, grp):
            for r in range(UG + 1):
                unit = grp * UG + r
                if r < UG:
                    act.wait_ge(s["s_mm"], i * (2 * UG) + unit + 1)
                    if not (isinstance(i, int) and i == 0 and unit < NGE):
                        act.wait_ge(s["a_lo"], i * (2 * UG) + unit - NGE + 1)
                    act.activation(ge[r % NGE][:], SB[unit % NB][:, 0:CH], ACT.Gelu).then_inc(s["gelu"], 1)
                if r:
                    j, ch = divmod(r - 1, NCH)
                    act.wait_ge(s["prod"], i * (2 * UG) + unit)
                    if r == 1 and not (isinstance(i, int) and i == 0):
                        act.wait_ge(s["y_mm"], i * (2 * YG) + (grp - 1) * YG)
                    act.activation(ap[grp * GR + j][0][:, ch * CH:(ch + 1) * CH], ge[(r - 1) % NGE][:], ACT.Copy)\
                       .then_inc(s["a_hi"], 1)

        def gating(dve, i, grp):
            for r in range(UG + 1):
                unit = grp * UG + r
                if r < UG:
                    j, ch = divmod(r, NCH)
                    if ch == 0:
                        dve.wait_ge(g_in[j], i * 32 + grp * 16 + 16)
                    dve.wait_ge(s["gelu"], i * (2 * UG) + unit + 1)
                    x = ge[r % NGE][:]
                    dve.tensor_tensor(x, x, g[j][:, ch * CH:(ch + 1) * CH], ALU.mult).then_inc(s["prod"], 1)
                if r:
                    j, ch = divmod(r - 1, NCH)
                    cols = slice(ch * CH, (ch + 1) * CH)
                    dve.wait_ge(s["a_hi"], i * (2 * UG) + unit)
                    low_part(dve, ap[grp * GR + j][1][:, cols], ge[(r - 1) % NGE][:],
                             ap[grp * GR + j][0][:, cols]).then_inc(s["a_lo"], 1)

        def low_of(dve, i, grp, n):
            j = n % GR
            if n < GR:
                dve.wait_ge(s["u_hi"], i * SL + (grp + 1) * GR + j + 1)
                low_part(dve, up[j][1][:], u[j][:], up[j][0][:]).then_inc(s["u_lo"], 1)
            else:
                sl = grp * GR + j
                dve.wait_ge(s["v_hi"], i * SL + sl + 1)
                low_part(dve, vp[sl][1][:], v[j][:], vp[sl][0][:]).then_inc(s["v_lo"], 1)

        def adding(dve, i, grp, lows):
            for n in range(YG):
                m, ch = divmod(n, NCH)
                dve.wait_ge(s["y_mm"], i * (2 * YG) + grp * YG + n + 1)
                if n == 0:
                    dve.wait_ge(s["y"], i * (2 * YG) + grp * YG)
                at = c.acc[:, m, ch * CH:(ch + 1) * CH]
                dve.tensor_tensor(at, at, YB[n % NB][:, 0:CH], ALU.add).then_inc(s["y"], 1)
                if n in SPLIT_AT and SPLIT_AT.index(n) in lows:
                    lows[SPLIT_AT.index(n)]()

        with nc.Block() as block:
            @block.sync
            def _(sp):
                def load(i, grp):
                    for j in range(GR):
                        tile = bass.ds(i * SL + grp * GR + j, 1)
                        one = lambda ap: ap[tile].rearrange("o p n -> (o p) n")
                        later = not (isinstance(i, int) and i == 0 and grp == 0)
                        if later:
                            sp.wait_ge(s["u_lo"], (i * SL + grp * GR + j) - GR + 1)
                        sp.dma_start(u[j][:].rearrange("p k e -> p (k e)"),
                                     one(IN["uT"].rearrange("t p k e -> t p (k e)"))).then_inc(u_in[j], 16)
                        if later:
                            sp.wait_ge(s["prod"], (i * (2 * UG) + grp * UG) + (j + 1) * NCH - UG)
                        sp.dma_start(g[j][:], one(c.dram["gates_dram"])).then_inc(g_in[j], 16)
                    for j in range(GR):
                        tile = bass.ds(i * SL + grp * GR + j, 1)
                        if later:
                            sp.wait_ge(s["v_lo"], (i * SL + grp * GR + j) - GR + 1)
                        sp.dma_start(v[j][:], IN["v"][tile].rearrange("o p n -> (o p) n")).then_inc(v_in[j], 16)

                load(0, 0)
                load(0, 1)
                with sp.Fori(1, turns) as i:
                    load(i, 0)
                    load(i, 1)

            @block.tensor
            def _(pe):
                scores(pe, 0, 0)
                scores(pe, 0, 1)
                sums(pe, 0, 0)
                with pe.Fori(1, turns) as i:
                    scores(pe, i, 0)
                    sums(pe, i - 1, 1)
                    scores(pe, i, 1)
                    sums(pe, i, 0)
                sums(pe, turns - 1, 1)

            @block.scalar
            def _(act):
                def step(i, grp, more=True):
                    gelus(act, i, grp)
                    if more and grp == 0:
                        u_high(act, i, 1)
                    elif more:
                        u_high(act, i + 1, 0)
                    v_high(act, i, grp)

                u_high(act, 0, 0)
                step(0, 0)
                step(0, 1)
                with act.Fori(1, turns - 1) as i:
                    step(i, 0)
                    step(i, 1)
                step(turns - 1, 0)
                step(turns - 1, 1, more=False)

            @block.vector
            def _(dve):
                def step(i, grp, before=True, more=True):
                    gating(dve, i, grp)
                    todo = [n for n in range(2 * GR) if more or n >= GR]
                    lows = {n: (lambda n=n: low_of(dve, i, grp, n)) for n in todo}
                    if not before:
                        for n in todo:
                            lows[n]()
                    elif grp == 0:
                        adding(dve, i - 1, 1, lows)
                    else:
                        adding(dve, i, 0, lows)

                for j in range(GR):
                    dve.wait_ge(s["u_hi"], j + 1)
                    low_part(dve, up[j][1][:], u[j][:], up[j][0][:]).then_inc(s["u_lo"], 1)
                c.vstep(dve, dve.memset(c.acc[:], 0.0))
                step(0, 0, before=False)
                step(0, 1)
                with dve.Fori(1, turns - 1) as i:
                    step(i, 0)
                    step(i, 1)
                step(turns - 1, 0)
                step(turns - 1, 1, more=False)
                adding(dve, turns - 1, 1, {})


def stage_output(c):
    nc, OUT = c.nc, c.OUT
    with ExitStack() as ctx:
        x1 = ctx.enter_context(nc.sbuf_tensor("out_x1", [P, KD, TOK], F32))
        s = {n: c.sem("out_" + n) for n in "x_in y stored".split()}
        gate2, acc = c.mod[:, 5], c.acc
        with nc.Block() as block:
            @block.sync
            def _(sp):
                sp.dma_start(x1[:], c.dram["x1_dram"]).then_inc(s["x_in"], 16)
                for m in range(KD):
                    sp.wait_ge(s["y"], m + 1)
                    sp.dma_start(OUT["yT"][:, m], x1[:, m]).then_inc(s["stored"], 16)
                sp.wait_ge(s["stored"], 16 * KD)

            @block.vector
            def _(dve):
                dve.wait_ge(s["x_in"], 16)
                c.vstep(dve, dve.tensor_tensor(acc[:, :, NPR:TOK], acc[:, :, NPR:TOK], gate2[:, :, 1:], ALU.mult))
                c.vstep(dve, dve.tensor_tensor(x1[:, :, NPR:TOK], x1[:, :, NPR:TOK], acc[:, :, NPR:TOK], ALU.add))
                for m in range(KD):
                    dve.scalar_tensor_tensor(out=x1[:, m, 0:NPR], in0=acc[:, m, 0:NPR], scalar=gate2[:, m, 0:1],
                                             in1=x1[:, m, 0:NPR], op0=ALU.mult, op1=ALU.add).then_inc(s["y"], 1)


def build_program(nc, IN, OUT, upto=99, dbg=None):
    with ExitStack() as ctx:
        c = Core()
        setup(nc, c, ctx, IN, OUT)
        late = ctx.enter_context(ExitStack())
        c.ident, c.ones, c.iota = right_side(c, late, dict(ident=[P, P], ones=[P, P], iota=[P, NK]))
        with ExitStack() as outs, ExitStack() as early:
            c.rows, c.rot, c.masks, c.QTs, c.KTs, c.lat_s, c.hT = right_side(c, early, dict(
                rows=[P, ROWG], rot=[P, NG + 1, len(TILES), 2 * RH], masks=[P, 3, P],
                QTs=[QK, MH, NSA], KTs=[QK, MH, NSA], lat_s=[NSA, LAT], hT=[P, KD, TOK]))
            c.o_mlaT = outs.enter_context(nc.sbuf_tensor("o_mlaT", [P, MH * VH // P, TOK], F32))
            stage_ada(c)
            stage_norm(c, "norm1", lambda e, x, sem: e.dma_start(x[:], IN["xT"]).then_inc(sem, 16), 0)
            with ExitStack() as mla:
                c.QT = mla.enter_context(nc.sbuf_tensor("QT", [QK, MH, NPR], F32))
                c.KT = mla.enter_context(nc.sbuf_tensor("KT", [QK, MH, NPR], F32))
                c.Vm = mla.enter_context(nc.sbuf_tensor("Vm", [P, NPR // P, MH * VH], F32))
                stage_mla_project(c)
                c.end_stage()
                stage_attention(c, "ma", MH, VH, c.QT, c.KT, c.Vm, lambda b: (0, b + 1, b, c.masks[:, 1, :]),
                                TurnOutput(c, c.o_mlaT), True)
                c.end_stage()
            stage_mla_sample(c)
            c.end_stage()
            c.o_dilT = outs.enter_context(nc.sbuf_tensor("o_dilT", [P, GW // P, TOK], F32))
            with ExitStack() as dil:
                dsb = lambda t, shape: dil.enter_context(nc.sbuf_tensor("d_" + t, shape, F32))
                c.dqs, c.dks = (dsb(t, [P, NG, DH, NSA]) for t in ("qs", "ks"))
                c.dvs = dsb("vs", [NSA, NG, GW])
                with ExitStack() as work:
                    wsb = lambda t, shape: work.enter_context(nc.sbuf_tensor("d_" + t, shape, F32))
                    c.dQ, c.dK = (wsb(t, [P, DH, NPR]) for t in ("Q", "K"))
                    c.dV = wsb("V", [P, NPR // P, GW])
                    w = [wsb(f"w{i}", [P, KD, GW]) for i in range(2)]
                    for g in range(NG):
                        with ExitStack() as one:
                            stage_dilated_project(c, g, w, lambda t, shape: one.enter_context(
                                nc.sbuf_tensor(f"d{g}_{t}", shape, F32)))
                        stage_attention(c, f"da{g}", DH, DE, c.dQ, c.dK, c.dV, lambda b: dilated_span(c, g, b),
                                        StoreOutput(c, g), False)
                        c.end_stage()
                stage_dilated_combine(c)
                stage_dilated_sample(c)
                c.end_stage()
            if upto == 5:
                dump(nc, c, dbg)
                return
            stage_mix(c)
        c.hT2 = [ctx.enter_context(nc.sbuf_tensor(f"h_{t}", [P, KD, TOK], F32R)) for t in ("high", "low")]
        stage_norm(c, "norm2", lambda e, x, sem: e.dma_start(x[:], c.dram["x1_dram"]).then_inc(sem, 16), 1, c.hT2)
        c.end_stage()
        if upto == 6:
            dump(nc, c, dbg)
            return
        with ExitStack() as route:
            c.pick = route.enter_context(nc.sbuf_tensor("pick", [P, 3, TOK], F32))
            stage_route(c)
            c.end_stage()
            if upto == 7:
                dump(nc, c, dbg)
                return
            stage_gates(c)
            c.end_stage()
        late.close()
        c.acc = ctx.enter_context(nc.sbuf_tensor("experts_out", [P, KD, TOK], F32))
        with ExitStack() as experts:
            stage_experts(c)
        stage_output(c)


def dump(nc, c, dbg):
    s = c.sem("dbg")
    with nc.Block() as block:
        @block.sync
        def _(sp):
            for i, (dst, src) in enumerate(dbg(c)):
                sp.dma_start(dst, src).then_inc(s, 16)
                sp.wait_ge(s, 16 * i + 16)


def feature_tiles(a, inner):
    r, n = a.shape
    return np.ascontiguousarray(a.reshape(r // P, P, n // inner, inner).transpose(2, 1, 0, 3))


def angles(pos, half):
    inv = (np.float32(THETA) ** (-np.arange(half, dtype=np.float32) / np.float32(half))).astype(np.float32)
    ang = pos.astype(np.float32)[:, None] * inv[None]
    return np.cos(ang), np.sin(ang)


OUTS = dict(yT=(P, KD, TOK), latent_prompt=(NPR, LAT), latent_sample=(NSA, LAT))
for _g, (_w, _) in enumerate(GROUPS):
    OUTS[f"dil{_g}_prompt"] = (min(_w, NPR), 2, GW)
    OUTS[f"dil{_g}_sample"] = (NSA, 2, GW)


def lay_out(x):
    a = {k: np.asarray(v) for k, v in x.items()}
    w = {k: a[k][0] for k in a if a[k].shape[:1] == (1,) and k not in ("x_prompt", "c_prompt")}
    col = lambda v: v.reshape(-1, P).T
    fm = lambda t: np.ascontiguousarray(t.T.reshape(KD, P, -1).transpose(1, 0, 2))
    out = {}
    out["xT"] = fm(np.concatenate([a["x_prompt"][0], a["x_sample"][:, 0]]))
    out["cT"] = fm(np.concatenate([a["c_prompt"], a["c_sample"]]))
    out["w_ada"] = feature_tiles(w["w_ada"], P)
    out["b_adaT"] = np.ascontiguousarray(col(w["b_ada"]))
    kn = np.zeros((P, 1), np.float32)
    kn[0:NOPE, 0] = w["g_mla_kn"][0:NOPE]
    out["gainsT"] = np.concatenate([col(w["norm_mix_g"]), col(w["norm_ffn_g"]), col(w["g_q_lora"]), kn], 1)
    rg = np.concatenate([w["g_kv_lora"], w["g_mla_qn"], w["g_mla_kn"], w["g_dil_qn"], w["g_dil_kn"]])
    out["row_gains"] = np.ascontiguousarray(np.broadcast_to(rg, (P, ROWG)))
    out["ident"] = np.eye(P, dtype=np.float32)
    w_in = w["w_in"]
    out["w_q"] = feature_tiles(w_in[:, 0:QL], P)
    out["w_kv"] = feature_tiles(w_in[:, QL:O_DIL], LAT)[0]
    out["w_dil"] = feature_tiles(w_in[:, O_DIL:O_GATE], GW)
    out["w_gate"] = feature_tiles(w_in[:, O_GATE:], P)
    out["w_uq"] = feature_tiles(w["w_uq"].reshape(QL, MH * QK), MH * QK)[0]
    out["w_uk"] = np.ascontiguousarray(w["w_uk"].reshape(KVL, MH * NOPE))
    out["w_uv"] = np.ascontiguousarray(w["w_uv"].reshape(KVL, MH * VH))
    out["w_ukT"] = np.ascontiguousarray(w["w_uk"].transpose(2, 1, 0))
    out["w_mla"] = feature_tiles(w["w_branch_mla"], P)
    out["w_dilb"] = feature_tiles(w["w_branch_dil"], P)
    out["w_out"] = feature_tiles(w["w_out"], P)
    out["w_pq"] = feature_tiles(w["w_pq"], P)
    out["keysT"] = np.ascontiguousarray(w["sub_keys"].transpose(3, 0, 1, 2).reshape(P, 2 * PH, NK))
    u = w["expert_u"].reshape(NK, NK, KD, P)
    out["uT"] = np.ascontiguousarray(u.transpose(0, 3, 2, 1))
    out["v"] = w["expert_v"].reshape(NK, NK, D)
    out["cache"] = w["cache_latent"]
    out["page_table"] = a["page_table"].reshape(1, -1)
    for g in range(NG):
        out[f"state{g}"] = w[f"state_dil{g}"].reshape(NSA, -1, 2 * GW)
    pos = np.arange(NPR)
    orders = [pos] + [np.concatenate([pos[sub_slice(g, b)] for b in range(NPR // P)]) for g in range(NG)]
    rot = np.zeros((P, 4, len(TILES), 2 * RH), np.float32)
    for n, o in enumerate(orders):
        cs = np.concatenate(angles(o, RH), 1).reshape(-1, P, 2 * RH)
        rot[:, n, 0:8] = cs.transpose(1, 0, 2)
        rot[:, n, 8] = np.concatenate(angles(np.array([PAST]), RH), 1)
    out["rot"] = rot
    q, k = np.arange(P)[:, None], np.arange(P)[None]
    causal = np.where(k <= q, 0, NEG)
    prev = np.where(k >= q, 0, NEG)
    pair = np.where((k <= q) & (k % 2 == q % 2), 0, NEG)
    out["iota"] = np.broadcast_to(np.arange(NK, dtype=np.float32), (P, NK))
    hb = np.arange(MH * NSA)[:, None]
    out["diag"] = np.where(hb % NSA == np.arange(NSA)[None], 0, NEG).astype(np.float32)
    out["masks"] = np.stack([prev, causal, pair], 1).astype(np.float32)
    return {k: np.ascontiguousarray(v) for k, v in out.items()}


def kernel(**inputs):
    from concourse import bacc
    from concourse.bass_utils import run_bass_kernel_spmd

    nc = bacc.Bacc("TRN2", target_bir_lowering=False, num_devices=1)
    arrays = lay_out(inputs)
    IN = {k: nc.dram_tensor("in_" + k, v.shape, mybir.dt.from_np(v.dtype), kind="ExternalInput").ap()
          for k, v in arrays.items()}
    OUT = {k: nc.dram_tensor("out_" + k, shape, F32, kind="ExternalOutput").ap() for k, shape in OUTS.items()}
    build_program(nc, IN, OUT)
    res = run_bass_kernel_spmd(nc, [{"in_" + k: v for k, v in arrays.items()}], core_ids=[0]).results[0]
    r = {k: res["out_" + k] for k in OUTS}
    y = r["yT"].transpose(2, 1, 0).reshape(TOK, D)
    dil = [r[f"dil{g}_prompt"].reshape(1, 1, -1, 2, DH, DE) for g in range(NG)]
    dil += [r[f"dil{g}_sample"].reshape(1, NSA, 1, 2, DH, DE) for g in range(NG)]
    return (y[0:NPR].reshape(1, NPR, D), y[NPR:].reshape(NSA, 1, D), r["latent_prompt"].reshape(1, 1, NPR, LAT),
            r["latent_sample"].reshape(1, NSA, 1, LAT), *dil)
```

```python
from contextlib import ExitStack

import concourse.bass as bass
import numpy as np
from concourse import mybir

F32 = mybir.dt.float32
F32R = mybir.dt.float32r
I32 = mybir.dt.int32
U32 = mybir.dt.uint32
ACT = mybir.ActivationFunctionType
ALU = mybir.AluOpType
AX = mybir.AxisListType

P = 128
D = 1024
KD = D // P
NPR = 1024
NSA = 8
TOK = NPR + NSA
GBLK = 64
CH = TOK // 3
NCH = 3
TILES = [(t * P, P) for t in range(NPR // P)] + [(NPR, NSA)]
EPS = 1e-6
NEG = -1e30
THETA = 500000.0

QL, KVL, ROPE, NOPE = 256, 128, 32, 64
QK = NOPE + ROPE
LAT = KVL + ROPE
MH, VH = 8, 64
GROUPS = ((128, 1), (512, 4), (2048, 16))
NG, DH, DE = 3, 4, 128
GW = DH * DE
RH = 16
PAGE, NPAGE, PAST = 128, 8, 1024
PH, NK, TOPK = 8, 128, 16
ADA = 6
MSCALE = QK ** -0.5
DSCALE = DE ** -0.5

O_KVL = QL
O_DIL = QL + LAT
O_GATE = O_DIL + 3 * NG * GW


class Steps:

    def __init__(self, sem):
        self.sem, self.n, self.off = sem, 0, None

    def value(self):
        return self.n if self.off is None else self.off + self.n

    def __call__(self, eng, ins):
        ins.then_inc(self.sem, 1)
        self.n += 1
        eng.wait_ge(self.sem, self.value())

    def loop(self, i, per, first=0):
        self.base, self.per = self.n, per
        self.off = (i - first) * per if first else i * per

    def end(self, turns):
        assert self.n == self.base + self.per, (self.n, self.base, self.per)
        self.off, self.n = None, self.base + self.per * turns


class Turn:

    def __init__(self, by=1):
        self.by, self.n = by, {}

    def take(self, eng, sem, times=1):
        self.n[sem.name] = self.n.get(sem.name, 0) + self.by * times
        eng.wait_ge(sem, self.n[sem.name])


def sub_tokens(g, b):
    dil = GROUPS[g][1]
    if dil == 16:
        return b, dil // 2
    per = NPR // P // dil
    return b // per + dil * P * (b % per), dil


def sub_slice(g, b, row0=0):
    first, step = sub_tokens(g, b)
    return slice(first - row0, first - row0 + step * (P - 1) + 1, step)


class Core:

    def __init__(self):
        self.stage_sems = []

    def sem(self, name):
        self.stage_sems.append(self.nc.alloc_semaphore(name))
        return self.stage_sems[-1]

    def end_stage(self):
        self.nc.clear_and_free_semaphores(self.stage_sems)
        self.nc.all_engine_barrier()
        self.stage_sems = []


def setup(nc, c, ctx, IN, OUT):
    def sem(name):
        return ctx.enter_context(nc.semaphore(name))

    def sb(name, shape, dt=F32):
        return ctx.enter_context(nc.sbuf_tensor(name, shape, dt))

    c.nc, c.IN, c.OUT = nc, IN, OUT
    c.ps = [ctx.enter_context(nc.psum_tensor(f"bank{i}", [P, 512], F32)) for i in range(8)]
    c.vstep = Steps(sem("vector_step"))
    c.astep = Steps(sem("scalar_step"))
    c.eps = sb("eps", [P, 1])
    c.mod = sb("mod", [P, ADA, KD, 1 + NSA])
    c.gs = sb("gain_scale", [P, 2, KD, 1 + NSA])
    c.gT = sb("gainsT", [P, 2 * KD + 2 + 1])
    c.dram = {}

    def scratch(name, shape):
        c.dram[name] = nc.dram_tensor(name, shape, F32, kind="Internal").ap()
    scratch("x1_dram", (P, KD, TOK))
    scratch("q_dil_sample", (NG, NSA * GW))
    scratch("o_group", (NG, NPR, GW + 2 * DH))
    scratch("gates_dram", (NPR // GBLK, P, NK, GBLK))
    scratch("gates_tail_dram", (P, NK, NSA))
    scratch("gelu_dram", (Ahead.TILES, P, TOK))


def right_side(c, ctx, tensors):
    return [ctx.enter_context(c.nc.sbuf_tensor(name, shape, F32, side="right")) for name, shape in tensors.items()]


def same_place(c, ctx, shape, tensors, **side):
    found = []
    for name, dt in tensors[:-1]:
        with c.nc.sbuf_tensor(name, shape, dt, **side) as t:
            found.append(t)
    return found + [ctx.enter_context(c.nc.sbuf_tensor(tensors[-1][0], shape, tensors[-1][1], **side))]


R_KVL, R_QN, R_KN, R_DQ, R_DK = 0, KVL, KVL + QK, KVL + 2 * QK, KVL + 2 * QK + DE
ROWG = R_DK + DE


def product3(pe, out, w, x, start, stop):
    pe.matmul(out, w[0], x[0], start=start, stop=False)
    pe.matmul(out, w[0], x[1], start=False, stop=False)
    return pe.matmul(out, w[1], x[0], start=False, stop=stop)


def low_part(dve, low, full, high):
    return dve.tensor_tensor(low, full, high.bitcast(F32), ALU.subtract)


def sum_squares(pe, c, bank, ones_rows, sq, n, done):
    for k in range(n):
        ins = pe.matmul(bank[:, 0:CH], c.ones[:, :], sq[:, k, :], start=(k == 0), stop=(k == n - 1))
    ins.then_inc(done, 1)


def add_bias(dve, c, first, products):
    tiles = slice(first * KD, (first + 2) * KD)
    c.vstep(dve, dve.tensor_tensor(
        c.mod[:].rearrange("p a k n -> p (a k) n")[:, tiles], products.rearrange("p (m n) -> p m n", n=1 + NSA),
        c.b_adaT[:, tiles].unsqueeze(2).to_broadcast([P, 2 * KD, 1 + NSA]), ALU.add))


def gain_scale(dve, c, n):
    g = c.gT[:, n * KD:(n + 1) * KD].unsqueeze(2).to_broadcast([P, KD, 1 + NSA])
    dve.scalar_tensor_tensor(out=c.gs[:, n], in0=c.mod[:, 3 * n + 1], scalar=1.0,
                             in1=g, op0=ALU.add, op1=ALU.mult)


def stage_ada(c):
    nc, IN = c.nc, c.IN
    SL = 4
    with ExitStack() as ctx:
        sb = lambda name, shape: ctx.enter_context(nc.sbuf_tensor(name, shape, F32))
        cT = sb("cT", [P, KD, 1 + NSA])
        sig = sb("sigmoid_c", [P, KD, 1 + NSA])
        sc, bT = c.silu_c, c.b_adaT
        w = [sb(f"w_ada{j}", [P, KD, P]) for j in range(SL)]
        w_in = [c.sem(f"ada_w_in{j}") for j in range(SL)]
        c_in, small_in, silu, mm = c.sem("ada_c_in"), c.sem("ada_small_in"), c.sem("ada_silu"), c.sem("ada_mm")
        sig_done, ones_done = c.sem("ada_sig"), c.sem("ada_ones")
        NOW = 2 * KD
        out = c.ps[0][:, 0:NOW * (1 + NSA)]
        turns = NOW // SL
        with nc.Block() as block:
            @block.sync
            def _(sp):
                sp.dma_start(cT[:], IN["cT"]).then_inc(c_in, 16)
                for j in range(SL):
                    sp.dma_start(w[j][:], IN["w_ada"][j]).then_inc(w_in[j], 16)
                with sp.Fori(1, turns) as i:
                    for j in range(SL):
                        sp.wait_ge(mm, (i - 1) * SL + j + 1)
                        sp.dma_start(w[j][:], IN["w_ada"][bass.ds(i * SL + j, 1)]
                                     .rearrange("o p k n -> (o p) k n")).then_inc(w_in[j], 16)

            @block.scalar
            def _(act):
                for dst, src in ((bT, "b_adaT"), (c.gT, "gainsT"), (c.rows, "row_gains"), (c.ident, "ident"),
                                 (c.rot, "rot"), (c.masks, "masks"), (c.iota, "iota")):
                    act.dma_start(dst[:], IN[src]).then_inc(small_in, 16)
                act.wait_ge(c_in, 16)
                act.activation(sig[:], cT[:], ACT.Sigmoid).then_inc(sig_done, 1)

            @block.vector
            def _(dve):
                dve.memset(c.ones[:], 1.0).then_inc(ones_done, 1)
                dve.memset(c.eps[:], EPS).then_inc(ones_done, 1)
                dve.wait_ge(sig_done, 1)
                dve.tensor_tensor(sc[:], sig[:], cT[:], ALU.mult).then_inc(silu, 1)
                dve.wait_ge(mm, NOW)
                dve.wait_ge(small_in, 112)
                add_bias(dve, c, 0, out)
                for r, w, scale in ((R_QN, QK, MSCALE), (R_DQ, DE, DSCALE)):
                    dve.tensor_scalar(c.rows[:, r:r + w], c.rows[:, r:r + w], scale, None, ALU.mult)
                gain_scale(dve, c, 0)

            @block.tensor
            def _(pe):
                pe.wait_ge(silu, 1)
                with pe.Fori(0, turns) as i:
                    for j in range(SL):
                        pe.wait_ge(w_in[j], i * 16 + 16)
                        for k in range(KD):
                            ins = pe.matmul(out[:, bass.ds((i * SL + j) * (1 + NSA), 1 + NSA)], w[j][:, k, :],
                                            sc[:, k, :], start=(k == 0), stop=(k == KD - 1))
                        ins.then_inc(mm, 1)


def stage_norm(c, name, src, n, parts=None):
    nc = c.nc
    with ExitStack() as ctx:
        sb = lambda t, shape: ctx.enter_context(nc.sbuf_tensor(f"{name}_{t}", shape, F32))
        x = sb("x", [P, KD, TOK])
        sq = [sb(f"sq{i}", [P, TOK]) for i in range(2)]
        root = sb("root", [P, TOK])
        inv = sb("inv", [P, TOK])
        tmp = sb("tmp", [P, KD, TOK])
        s = {t: c.sem(f"{name}_{t}") for t in ("sq", "sum", "root", "inv", "xn", "h", "h_sample", "hi")}
        x_in = [c.sem(f"{name}_x_in{k}") for k in range(KD)]
        gs, sh = c.gs[:, n], c.mod[:, 3 * n]
        h = x if parts else c.hT
        with nc.Block() as block:
            @block.sync
            def _(sp):
                for k in range(KD):
                    sp.dma_start(x[:, k], src[:, k]).then_inc(x_in[k], 16)

            @block.scalar
            def _(act):
                for k in range(KD):
                    act.wait_ge(x_in[k], 16)
                    if k >= 2:
                        act.wait_ge(s["sum"], k - 1)
                    act.activation(sq[k % 2][:], x[:, k], ACT.Square).then_inc(s["sq"], 1)
                act.wait_ge(s["sum"], KD)
                for i in range(NCH):
                    act.activation(root[:, i * CH:(i + 1) * CH], c.ps[i][:, 0:CH], ACT.Sqrt,
                                   scale=1.0 / D, bias=c.eps[:]).then_inc(s["root"], 1)
                act.wait_ge(s["h_sample"], 1)
                for k in range(KD):
                    act.wait_ge(s["xn"], k + 1)
                    act.activation(h[:, k, 0:NPR], tmp[:, k, 0:NPR], ACT.Identity,
                                   scale=gs[:, k, 0:1], bias=sh[:, k, 0:1]).then_inc(s["h"], 1)
                    if parts:
                        act.wait_ge(s["h"], k + 1)
                        act.activation(parts[0][:, k], h[:, k], ACT.Copy).then_inc(s["hi"], 1)

            @block.tensor
            def _(pe):
                for k in range(KD):
                    pe.wait_ge(s["sq"], k + 1)
                    for i in range(NCH):
                        ins = pe.matmul(c.ps[i][:, 0:CH], c.ones[:, :], sq[k % 2][:, i * CH:(i + 1) * CH],
                                        start=(k == 0), stop=(k == KD - 1))
                    ins.then_inc(s["sum"], 1)

            @block.vector
            def _(dve):
                for k in range(KD):
                    dve.wait_ge(x_in[k], 16)
                for i in range(NCH):
                    dve.wait_ge(s["root"], i + 1)
                    ins = dve.reciprocal(inv[:, i * CH:(i + 1) * CH], root[:, i * CH:(i + 1) * CH])
                ins.then_inc(s["inv"], 1)
                dve.wait_ge(s["inv"], 1)
                ts = tmp[:, :, NPR:TOK]
                c.vstep(dve, dve.tensor_tensor(ts, x[:, :, NPR:TOK], inv[:, NPR:TOK].unsqueeze(1)
                                               .to_broadcast([P, KD, NSA]), ALU.mult))
                c.vstep(dve, dve.tensor_tensor(ts, ts, gs[:, :, 1:], ALU.mult))
                dve.tensor_tensor(h[:, :, NPR:TOK], ts, sh[:, :, 1:], ALU.add).then_inc(s["h_sample"], 1)
                for k in range(KD):
                    dve.tensor_tensor(tmp[:, k, 0:NPR], x[:, k, 0:NPR], inv[:, 0:NPR], ALU.mult).then_inc(s["xn"], 1)
                if parts:
                    for k in range(KD):
                        dve.wait_ge(s["hi"], k + 1)
                        low_part(dve, parts[1][:, k], h[:, k], parts[0][:, k])


def normed_rows(dve, c, x, ss, root, inv, gain, width, sqrt_done, tn, ss_done):
    n, heads = x.shape[0], x.shape[1]
    tn.take(dve, sqrt_done)
    c.vstep(dve, dve.reciprocal(inv, root))
    c.vstep(dve, dve.tensor_tensor(x, x, inv.unsqueeze(2).to_broadcast([n, heads, width]), ALU.mult))
    c.vstep(dve, dve.tensor_tensor(x, x, gain[0:n].unsqueeze(1).to_broadcast([n, heads, width]), ALU.mult))


def rotate(dve, c, out, x, rot, tmp, done=None):
    n, heads = x.shape[0], x.shape[1]
    if len(rot.shape) == 2:
        rot = rot[0:n].unsqueeze(1).to_broadcast([n, heads, 2 * RH])
    cos, sin = rot[:, :, 0:RH], rot[:, :, RH:2 * RH]
    x1, x2 = x[:, :, 0:RH], x[:, :, RH:2 * RH]
    t = [tmp[0:n, i, 0:heads] for i in range(4)]
    dve.tensor_tensor(t[0], x1, cos, ALU.mult)
    dve.tensor_tensor(t[1], x2, sin, ALU.mult)
    dve.tensor_tensor(t[2], x2, cos, ALU.mult)
    c.vstep(dve, dve.tensor_tensor(t[3], x1, sin, ALU.mult))
    dve.tensor_tensor(out[:, :, 0:RH], t[0], t[1], ALU.subtract)
    ins = dve.tensor_tensor(out[:, :, RH:2 * RH], t[2], t[3], ALU.add)
    if done is None:
        c.vstep(dve, ins)
    else:
        ins.then_inc(done, 1)


def stage_mla_project(c):
    nc, IN, OUT = c.nc, c.IN, c.OUT
    HB = MH // 2
    with ExitStack() as ctx:
        sb = lambda t, shape: ctx.enter_context(nc.sbuf_tensor("mp_" + t, shape, F32))
        w_q = sb("w_q", [P, 2, KD, P])
        w_kv = sb("w_kv", [P, KD, LAT])
        w_uq = sb("w_uq", [P, 2, MH * QK])
        w_uk = sb("w_uk", [P, MH * NOPE])
        w_uv = sb("w_uv", [P, MH * VH])
        zq = sb("zq", [P, 2, TOK])
        sq = [sb(f"sq{i}", [P, 2, CH]) for i in range(2)]
        inv = sb("inv", [P, TOK])
        qs = sb("q", [P, MH, QK])
        qsq = sb("qsq", [P, MH, QK])
        kf = sb("k", [P, MH, QK])
        ksq = sb("ksq", [P, MH, NOPE])
        lat = [sb(f"lat{i}", [P, LAT]) for i in range(2)]
        junk = sb("junk", [P, LAT])
        st = sb("stats", [P, 8, MH])
        krr = sb("krr", [P, 1, ROPE])
        tmp = sb("tmp", [P, 4, MH, RH])
        ckT = sb("ckT", [P, P])
        names = ("w_in zq zcopy zsq zsum root cq cq_free q_mm q_copy kv_mm kv_copy q_ss q_root kv_root lat tr "
                 "trc kn_mm kn_copy v_mm v_copy k_ss k_root q_fin k_fin kT_mm kT_copy qT_mm qT_copy lat_out").split()
        s = {t: c.sem("mp_" + t) for t in names}
        lat_out = [s["lat_out"], c.sem("mp_lat_out1")]
        A, B, KV, TR, KN, V, X0, X1 = c.ps
        ss_q, root_q, inv_q = st[:, 0], st[:, 1], st[:, 2]
        ss_k, root_k, inv_k = st[:, 3], st[:, 4], st[:, 5]
        one = st[:, 6]
        with nc.Block() as block:
            @block.sync
            def _(sp):
                for m in range(2):
                    sp.dma_start(w_q[:, m], IN["w_q"][m]).then_inc(s["w_in"], 16)
                for dst, src in ((w_kv, "w_kv"), (w_uq, "w_uq"), (w_uk, "w_uk"), (w_uv, "w_uv")):
                    sp.dma_start(dst[:], IN[src]).then_inc(s["w_in"], 16)
                for t, (t0, n) in enumerate(TILES):
                    sp.wait_ge(s["lat"], t + 1)
                    dst = OUT["latent_prompt"][t0:t0 + n] if n == P else OUT["latent_sample"]
                    sp.dma_start(dst, lat[t % 2][0:n, :]).then_inc(lat_out[t % 2], 16)
                for i in range(2):
                    sp.wait_ge(lat_out[i], 16 * ((len(TILES) + 1 - i) // 2))

            @block.tensor
            def _(pe):
                tn = Turn()
                pe.wait_ge(s["w_in"], 96)
                for u in range(2 * NCH):
                    m, i = divmod(u, NCH)
                    for k in range(KD):
                        ins = pe.matmul(c.ps[u][:, 0:CH], w_q[:, m, k, :], c.hT[:, k, i * CH:(i + 1) * CH],
                                        start=(k == 0), stop=(k == KD - 1))
                    ins.then_inc(s["zq"], 1)
                for i in range(NCH):
                    tn.take(pe, s["zsq"])
                    if i == 2:
                        pe.wait_ge(s["root"], 1)
                    sum_squares(pe, c, c.ps[6 + i % 2], None, sq[i % 2], 2, s["zsum"])
                tn.take(pe, s["cq"], NCH)

                def project(t):
                    t0, n = TILES[t]
                    if t:
                        pe.wait_ge(s["q_copy"], 4 * t)
                        pe.wait_ge(s["kv_copy"], 2 * t)
                    for half, bank in ((0, A), (1, B)):
                        for k in range(2):
                            ins = pe.matmul(bank[0:n, 0:HB * QK], zq[:, k, t0:t0 + n],
                                            w_uq[:, k, half * HB * QK:(half + 1) * HB * QK],
                                            start=(k == 0), stop=(k == 1))
                        ins.then_inc(s["q_mm"], 1)
                    for k in range(KD):
                        ins = pe.matmul(KV[0:n, 0:LAT], c.hT[:, k, t0:t0 + n], w_kv[:, k, :],
                                        start=(k == 0), stop=(k == KD - 1))
                    ins.then_inc(s["kv_mm"], 1)

                def turn_heads(t, x, mm, copied, fin):
                    n = TILES[t][1]
                    pe.wait_ge(fin, t + 1)
                    for half, bank in ((0, X0), (1, X1)):
                        if fin is s["q_fin"]:
                            pe.wait_ge(s["kT_copy"], 2 * t + half + 1)
                        elif t:
                            pe.wait_ge(s["qT_copy"], 2 * t - 1 + half)
                        for h in range(HB):
                            ins = pe.transpose(bank[0:QK, h * P:h * P + n], x[0:n, half * HB + h, :],
                                               c.ident[0:n, 0:n])
                        ins.then_inc(mm, 1)

                project(0)
                for t, (t0, n) in enumerate(TILES):
                    pe.wait_ge(s["lat"], t + 1)
                    if t:
                        pe.wait_ge(s["trc"], t)
                    pe.transpose(TR[:, 0:n], lat[t % 2][0:n, 0:KVL], c.ident[0:n, 0:n]).then_inc(s["tr"], 1)
                    pe.wait_ge(s["trc"], t + 1)
                    if t:
                        pe.wait_ge(s["kn_copy"], 2 * t)
                        pe.wait_ge(s["v_copy"], t)
                    pe.matmul(KN[0:n, :], ckT[:, 0:n], w_uk[:], start=True, stop=True).then_inc(s["kn_mm"], 1)
                    pe.matmul(V[0:n, :], ckT[:, 0:n], w_uv[:], start=True, stop=True).then_inc(s["v_mm"], 1)
                    if t + 1 < len(TILES):
                        project(t + 1)
                    turn_heads(t, kf, s["kT_mm"], s["kT_copy"], s["k_fin"])
                    turn_heads(t, qs, s["qT_mm"], s["qT_copy"], s["q_fin"])

            @block.scalar
            def _(act):
                for i in range(NCH):
                    for m in range(2):
                        act.wait_ge(s["zq"], m * NCH + i + 1)
                        act.activation(zq[:, m, i * CH:(i + 1) * CH], c.ps[m * NCH + i][:, 0:CH], ACT.Copy)\
                           .then_inc(s["zcopy"], 1)
                        if i >= 2:
                            act.wait_ge(s["zsum"], i - 1)
                        ins = act.activation(sq[i % 2][:, m, :], c.ps[m * NCH + i][:, 0:CH], ACT.Square)
                    ins.then_inc(s["zsq"], 1)
                for i in range(NCH):
                    act.wait_ge(s["zsum"], i + 1)
                    act.activation(inv[:, i * CH:(i + 1) * CH], c.ps[6 + i % 2][:, 0:CH], ACT.Sqrt,
                                   scale=1.0 / QL, bias=c.eps[:]).then_inc(s["root"], 1)
                for t, (t0, n) in enumerate(TILES):
                    if t:
                        act.wait_ge(s["qT_mm"], 2 * t)
                    for half, bank in ((0, A), (1, B)):
                        act.wait_ge(s["q_mm"], 2 * t + half + 1)
                        hs = slice(half * HB, (half + 1) * HB)
                        src = bank[0:n, 0:HB * QK].rearrange("p (h d) -> p h d", d=QK)
                        act.activation(qs[0:n, hs, :], src, ACT.Copy).then_inc(s["q_copy"], 1)
                        if t and half == 0:
                            act.wait_ge(s["q_ss"], t)
                        act.activation(qsq[0:n, hs, :], src, ACT.Square).then_inc(s["q_copy"], 1)
                    act.wait_ge(s["kv_mm"], t + 1)
                    if t >= 2:
                        act.wait_ge(s["tr"], t - 1)
                        act.wait_ge(lat_out[t % 2], 16 * (t // 2))
                    if t:
                        act.wait_ge(s["k_fin"], t)
                    act.activation(lat[t % 2][0:n, :], KV[0:n, 0:LAT], ACT.Copy).then_inc(s["kv_copy"], 1)
                    c.astep(act, act.activation(junk[0:n, 0:KVL], KV[0:n, 0:KVL], ACT.Square,
                                                accum_out=one[0:n, 0:1]))
                    act.activation(one[0:n, 1:2], one[0:n, 0:1], ACT.Sqrt, scale=1.0 / KVL,
                                   bias=c.eps[0:n]).then_inc(s["kv_root"], 1)
                    act.activation(junk[0:n, KVL:LAT], KV[0:n, KVL:LAT], ACT.Square,
                                   accum_out=one[0:n, 3:4]).then_inc(s["kv_copy"], 1)
                    act.wait_ge(s["q_ss"], t + 1)
                    act.activation(root_q[0:n], ss_q[0:n], ACT.Sqrt, scale=1.0 / QK, bias=c.eps[0:n])\
                       .then_inc(s["q_root"], 1)
                    act.wait_ge(s["tr"], t + 1)
                    act.activation(ckT[:, 0:n], TR[:, 0:n], ACT.Copy).then_inc(s["trc"], 1)
                    act.wait_ge(s["kn_mm"], t + 1)
                    if t:
                        act.wait_ge(s["kT_mm"], 2 * t)
                    src = KN[0:n, :].rearrange("p (h d) -> p h d", d=NOPE)
                    act.activation(kf[0:n, :, 0:NOPE], src, ACT.Copy).then_inc(s["kn_copy"], 1)
                    act.activation(ksq[0:n], src, ACT.Square).then_inc(s["kn_copy"], 1)
                    act.wait_ge(s["v_mm"], t + 1)
                    if n == P:
                        act.activation(c.Vm[:, t, :], V[:, :], ACT.Copy).then_inc(s["v_copy"], 1)
                    act.wait_ge(s["k_ss"], t + 1)
                    act.activation(root_k[0:n], ss_k[0:n], ACT.Sqrt, scale=1.0 / QK, bias=c.eps[0:n])\
                       .then_inc(s["k_root"], 1)
                    for half, bank in ((0, X0), (1, X1)):
                        act.wait_ge(s["kT_mm"], 2 * t + half + 1)
                        dst = c.KT[:, :, t0:t0 + n] if n == P else c.KTs
                        act.activation(dst[:, half * HB:(half + 1) * HB, :],
                                       bank[0:QK, :].rearrange("p (h q) -> p h q", q=P)[:, :, 0:n],
                                       ACT.Copy).then_inc(s["kT_copy"], 1)

            @block.vector
            def _(dve):
                tn = Turn()
                for i in range(NCH):
                    tn.take(dve, s["root"])
                    cols = slice(i * CH, (i + 1) * CH)
                    c.vstep(dve, dve.reciprocal(inv[:, cols], inv[:, cols]))
                    dve.wait_ge(s["zcopy"], 2 * i + 2)
                    for m in range(2):
                        ins = dve.scalar_tensor_tensor(out=zq[:, m, cols], in0=zq[:, m, cols],
                                                       scalar=c.gT[:, 2 * KD + m:2 * KD + m + 1],
                                                       in1=inv[:, cols], op0=ALU.mult, op1=ALU.mult)
                    ins.then_inc(s["cq"], 1)
                for t, (t0, n) in enumerate(TILES):
                    L = lat[t % 2]
                    dve.wait_ge(s["q_copy"], 4 * t + 4)
                    dve.tensor_reduce(ss_q[0:n], qsq[0:n], AX.X, ALU.add).then_inc(s["q_ss"], 1)
                    dve.wait_ge(s["kv_root"], t + 1)
                    dve.wait_ge(s["kv_copy"], 2 * t + 2)
                    c.vstep(dve, dve.reciprocal(one[0:n, 2:3], one[0:n, 1:2]))
                    dve.scalar_tensor_tensor(out=L[0:n, 0:KVL], in0=L[0:n, 0:KVL], scalar=one[0:n, 2:3],
                                             in1=c.rows[0:n, R_KVL:R_KVL + KVL], op0=ALU.mult,
                                             op1=ALU.mult).then_inc(s["lat"], 1)
                    c.vstep(dve, dve.tensor_tensor(krr[0:n, 0], L[0:n, KVL:LAT],
                                                   c.rows[0:n, R_KN + NOPE:R_KN + QK], ALU.mult))
                    rotate(dve, c, krr[0:n], krr[0:n], c.rot[:, 0, t], tmp)
                    normed_rows(dve, c, qs[0:n], ss_q[0:n], root_q[0:n], inv_q[0:n],
                                c.rows[:, R_QN:R_QN + QK], QK, s["q_root"], tn, None)
                    rotate(dve, c, qs[0:n, :, NOPE:QK], qs[0:n, :, NOPE:QK], c.rot[:, 0, t], tmp,
                           s["q_fin"])
                    dve.wait_ge(s["kn_copy"], 2 * t + 2)
                    c.vstep(dve, dve.tensor_reduce(ss_k[0:n], ksq[0:n], AX.X, ALU.add))
                    dve.tensor_scalar(ss_k[0:n], ss_k[0:n], one[0:n, 3:4], None, ALU.add).then_inc(s["k_ss"], 1)
                    kn = kf[0:n, :, 0:NOPE]
                    normed_rows(dve, c, kn, ss_k[0:n], root_k[0:n], inv_k[0:n],
                                c.rows[:, R_KN:R_KN + NOPE], NOPE, s["k_root"], tn, None)
                    dve.tensor_tensor(kf[0:n, :, NOPE:QK], krr[0:n].to_broadcast([n, MH, ROPE]),
                                      inv_k[0:n].unsqueeze(2).to_broadcast([n, MH, ROPE]),
                                      ALU.mult).then_inc(s["k_fin"], 1)
                    for half, bank in ((0, X0), (1, X1)):
                        dve.wait_ge(s["qT_mm"], 2 * t + half + 1)
                        dst = c.QT[:, :, t0:t0 + n] if n == P else c.QTs
                        dve.tensor_copy(dst[:, half * HB:(half + 1) * HB, :],
                                        bank[0:QK, :].rearrange("p (h q) -> p h q", q=P)[:, :, 0:n])\
                           .then_inc(s["qT_copy"], 1)
                dve.wait_ge(s["lat"], len(TILES))
                dve.tensor_copy(c.lat_s[:], lat[(len(TILES) - 1) % 2][0:NSA, :])


def stage_attention(c, name, heads, width, QT, KT, V, span, finish, normed):
    nc = c.nc
    NT = NPR // P
    units = [(b, h) for b in range(NT) for h in range(heads)]
    U = len(units)
    HW = heads * width
    turns = []
    for u, (b, h) in enumerate(units):
        nb = span(b)[1]
        turns += [(u, j, min(4, nb - j)) for j in range(0, nb, 4)]
    ends = [max(i for i, g in enumerate(turns) if g[0] == u) + 1 for u in range(U)]
    kd = QT.shape[0]
    with ExitStack() as ctx:
        sb = lambda t, shape: ctx.enter_context(nc.sbuf_tensor(f"{name}_{t}", shape, F32))
        prob = [sb(f"prob{i}", [P, NPR if normed else 2 * P]) for i in range(2)]
        pT = [sb(f"pT{i}", [P, NT if normed else 2, P]) for i in range(2)]
        o = [sb(f"o{i}", [P, HW + 2 * heads]) for i in range(2)]
        rs = sb("rs", [P, 4])
        s = {t: c.sem(f"{name}_{t}") for t in "mm nmax exp turn copy pv out tile".split()}
        S = [c.ps[0:2], c.ps[2:4]]
        PT = c.ps[4:6]
        O = c.ps[6]

        def scores(pe, u):
            b, h = units[u]
            k0, nb, _, _ = span(b)
            if u >= 2:
                pe.wait_ge(s["exp"], u - 1)
            for j in range(0, nb, 4):
                w = min(4, nb - j) * P
                ins = pe.matmul(S[u % 2][j // 4][:, 0:w], QT[:, h, b * P:(b + 1) * P],
                                KT[:, h, (k0 + j) * P:(k0 + j) * P + w], start=True, stop=True)
            ins.then_inc(s["mm"], 1)

        def values(pe, u):
            b, h = units[u]
            k0, nb, _, _ = span(b)
            pe.wait_ge(s["copy"], ends[u])
            if u:
                pe.wait_ge(s["out"], u)
            for j in range(nb):
                ins = pe.matmul(O[:, h * width:(h + 1) * width], pT[u % 2][:, j, :],
                                V[:, k0 + j, h * width:(h + 1) * width], start=(j == 0), stop=(j == nb - 1))
            ins.then_inc(s["pv"], 1)

        with nc.Block() as block:
            @block.tensor
            def _(pe):
                scores(pe, 0)
                scores(pe, 1)
                for u, (b, h) in enumerate(units):
                    k0, nb, _, _ = span(b)
                    pe.wait_ge(s["exp"], u + 1)
                    for i, (v, j0, n) in enumerate(turns):
                        if v == u:
                            if i >= 2:
                                pe.wait_ge(s["copy"], i - 1)
                            for j in range(n):
                                ins = pe.transpose(PT[i % 2][:, j * P:(j + 1) * P],
                                                   prob[u % 2][:, (j0 + j) * P:(j0 + j + 1) * P], c.ident[:, :])
                            ins.then_inc(s["turn"], 1)
                    if u + 2 < U:
                        scores(pe, u + 2)
                    finish.beside(pe, u)
                    if u:
                        values(pe, u - 1)
                    if u > heads and h == 1:
                        finish.tensor(pe, b - 1, o[(b - 1) % 2], s)
                values(pe, U - 1)
                finish.tensor(pe, NT - 1, o[(NT - 1) % 2], s)

            @block.scalar
            def _(act):
                def exps(u):
                    b, h = units[u]
                    w = span(b)[1] * P
                    act.wait_ge(s["nmax"], u + 1)
                    if u >= 2:
                        act.wait_ge(s["turn"], ends[u - 2])
                        act.wait_ge(s["exp"], u - 1)
                    ot = o[b % 2]
                    for j in range(0, w, 512):
                        n = min(512, w - j)
                        acc = ot[:, HW + heads + h:HW + heads + h + 1] if j == 0 else rs[:, 2 + u % 2:3 + u % 2]
                        ins = act.activation(prob[u % 2][:, j:j + n], S[u % 2][j // 512][:, 0:n], ACT.Exp,
                                             bias=ot[:, HW + h:HW + h + 1], accum_out=acc)
                    if w > 512:
                        c.astep(act, ins)
                        acc = ot[:, HW + heads + h:HW + heads + h + 1]
                        ins = act.activation(acc, rs[:, 2 + u % 2:3 + u % 2], ACT.Identity, bias=acc)
                    ins.then_inc(s["exp"], 1)

                exps(0)
                for u, (b, h) in enumerate(units):
                    if u + 1 < U:
                        exps(u + 1)
                    for i, (v, j0, n) in enumerate(turns):
                        if v == u:
                            act.wait_ge(s["turn"], i + 1)
                            if u >= 2:
                                act.wait_ge(s["pv"], u - 1)
                            act.activation(pT[u % 2][:, j0:j0 + n, :],
                                           PT[i % 2][:, 0:n * P].rearrange("p (j q) -> p j q", q=P),
                                           ACT.Copy).then_inc(s["copy"], 1)
                    if u > heads and h == 2:
                        finish.scalar(act, b - 1, o[(b - 1) % 2], s)
                finish.scalar(act, NT - 1, o[(NT - 1) % 2], s)

            @block.vector
            def _(dve):
                def maxima(u):
                    b, h = units[u]
                    k0, nb, m0, mask = span(b)
                    dve.wait_ge(s["mm"], u + 1)
                    if h == 0 and b >= 2:
                        dve.wait_ge(finish.used, finish.per_tile * (b - 1))
                    bank = S[u % 2][m0 // 4]
                    at = (m0 % 4) * P
                    w = mask.shape[1]
                    c.vstep(dve, dve.tensor_tensor(bank[:, at:at + w], bank[:, at:at + w], mask, ALU.add))
                    ot = o[b % 2]
                    nm = ot[:, HW + h:HW + h + 1]
                    if nb <= 4:
                        ins = dve.tensor_reduce(nm, S[u % 2][0][:, 0:nb * P], AX.X, ALU.max, negate=True)
                    else:
                        dve.tensor_reduce(nm, S[u % 2][0][:, :], AX.X, ALU.max, negate=True)
                        c.vstep(dve, dve.tensor_reduce(rs[:, 0:1], S[u % 2][1][:, 0:(nb - 4) * P], AX.X,
                                                       ALU.max, negate=True))
                        ins = dve.tensor_tensor(nm, nm, rs[:, 0:1], ALU.min)
                    ins.then_inc(s["nmax"], 1)

                def outputs(u):
                    b, h = units[u]
                    ot = o[b % 2]
                    dst = ot[:, h * width:(h + 1) * width]
                    src = O[:, h * width:(h + 1) * width]
                    sm = ot[:, HW + heads + h:HW + heads + h + 1]
                    dve.wait_ge(s["exp"], u + 1)
                    if normed:
                        c.vstep(dve, dve.reciprocal(sm, sm))
                        dve.wait_ge(s["pv"], u + 1)
                        ins = dve.tensor_scalar(dst, src, sm, None, ALU.mult)
                    else:
                        dve.wait_ge(s["pv"], u + 1)
                        ins = dve.tensor_copy(dst, src)
                    ins.then_inc(s["out"], 1)

                maxima(0)
                maxima(1)
                for u in range(U):
                    if u + 2 < U:
                        maxima(u + 2)
                    if u:
                        outputs(u - 1)
                outputs(U - 1)
                finish.vector(dve)

            @block.sync
            def _(sp):
                finish.sync(sp, o, s)

            @block.gpsimd
            def _(pool):
                finish.gpsimd(pool)


class TurnOutput:
    per_tile = 1

    def __init__(self, c, dst):
        self.c, self.dst = c, dst
        self.used, self.copied = c.sem("mo_turned"), c.sem("mo_copied")

    def tensor(self, pe, b, o, s):
        pe.wait_ge(s["out"], MH * (b + 1))
        if b:
            pe.wait_ge(self.copied, b)
        for k in range(MH * VH // P):
            ins = pe.transpose(self.c.ps[7][:, k * P:(k + 1) * P], o[:, k * P:(k + 1) * P], self.c.ident[:, :])
        ins.then_inc(self.used, 1)

    def scalar(self, act, b, o, s):
        act.wait_ge(self.used, b + 1)
        act.activation(self.dst[:, :, b * P:(b + 1) * P], self.c.ps[7][:].rearrange("p (k q) -> p k q", q=P),
                       ACT.Copy).then_inc(self.copied, 1)

    def beside(self, pe, u):
        pass

    def vector(self, dve):
        pass

    def gpsimd(self, pool):
        pass

    def sync(self, sp, o, s):
        pass


def stage_mla_sample(c):
    nc, IN = c.nc, c.IN
    R = MH * NSA
    Z = R + 1
    HALF = NPAGE // 2
    NQ = 2 * NSA
    with ExitStack() as ctx:
        sb = lambda t, shape, dt=F32: ctx.enter_context(nc.sbuf_tensor("ms_" + t, shape, dt))
        table = sb("page_table", [1, NSA * NPAGE], I32)
        rows = sb("rows", [P, NSA * NPAGE, LAT])
        w_ukT = sb("w_ukT", [NOPE, MH, KVL])
        w_uk = sb("w_uk", [P, MH * NOPE])
        w_uv = sb("w_uv", [P, MH * VH])
        diag = sb("diag", [R, NSA])
        qg = sb("qg", [NOPE, R])
        qwz = sb("qw_padded", [P, NSA * Z])
        qrz = sb("qr_padded", [ROPE, NSA * Z])
        qz = sb("q_padded", [QK, MH * (R + NSA)])
        krs = sb("krs", [P, NSA * NPAGE])
        krq = sb("krq", [P, NPAGE, ROPE])
        krr = [sb(f"krr{i}", [P, NPAGE, ROPE]) for i in range(2)]
        tmp = sb("tmp", [P, 4, NPAGE, RH])
        cT = [sb(f"cT{i}", [P, HALF * P]) for i in range(2)]
        krT = [sb(f"krT{i}", [ROPE, HALF * P]) for i in range(2)]
        ksq = [sb(f"ksq{i}", [P, MH, NOPE]) for i in range(2)]
        ms = sb("ms", [P, NPAGE, MH, NSA])
        invT = sb("invT", [R, PAST])
        sc = sb("scores", [R, PAST + NSA])
        st = sb("stats", [R, 4])
        pT = sb("pT", [P, NPAGE, R])
        pTn = sb("pT_new", [NSA, R])
        cx = sb("ctx", [P, R])
        s = {t: c.sem("ms_" + t) for t in ("w_in table prep qw kr tr trc kn sq red sc root inv invt invc new nmax "
                                           "exp norm pt ptc ctx ctxc out zero").split()}
        pages_in = [c.sem(f"ms_pages{b}") for b in range(NSA)]
        S = c.ps[6:8]
        with nc.Block() as block:
            @block.sync
            def _(sp):
                sp.dma_start(table[:], IN["page_table"]).then_inc(s["table"], 16)
                sp.wait_ge(s["table"], 16)
                for b in range(NSA):
                    with sp.Fori(b * NPAGE, (b + 1) * NPAGE) as i:
                        page = sp.value_load(table[0:1, bass.ds(i, 1)], min_val=0, max_val=IN["cache"].shape[0] - 1)
                        sp.dma_start(rows[:, bass.ds(i, 1), :].rearrange("p o d -> p (o d)"),
                                     IN["cache"][bass.ds(page, 1)].rearrange("o p d -> (o p) d"))\
                          .then_inc(pages_in[b], 16)

            @block.tensor
            def _(pe):
                pe.wait_ge(s["w_in"], 64)
                pe.wait_ge(s["prep"], 1)
                for h in range(MH):
                    ins = pe.matmul(c.ps[4][:, h * NSA:(h + 1) * NSA], w_ukT[:, h, :],
                                    qg[:, h * NSA:(h + 1) * NSA], start=True, stop=True)
                ins.then_inc(s["qw"], 1)

                def turn(q):
                    b, half = divmod(q, 2)
                    if half == 0:
                        pe.wait_ge(pages_in[b], 16 * NPAGE)
                        pe.wait_ge(s["kr"], b + 1)
                    if q >= 2:
                        pe.wait_ge(s["trc"], 2 * (q - 1))
                    for j in range(HALF):
                        pe.transpose(c.ps[q % 2][:, j * P:(j + 1) * P], rows[:, q * HALF + j, 0:KVL], c.ident[:, :])
                    for j in range(HALF):
                        ins = pe.transpose(c.ps[2 + q % 2][0:ROPE, j * P:(j + 1) * P],
                                           krr[b % 2][:, half * HALF + j, :], c.ident[:, :])
                    ins.then_inc(s["tr"], 1)

                turn(0)
                for q in range(NQ):
                    b, half = divmod(q, 2)
                    if q + 1 < NQ:
                        turn(q + 1)
                    pe.wait_ge(s["trc"], 2 * q + 2)
                    pe.wait_ge(s["prep"], 4)
                    for j in range(HALF):
                        n = q * HALF + j
                        if n >= 2:
                            pe.wait_ge(s["sq"], n - 1)
                        pe.matmul(c.ps[4 + n % 2][:, :], cT[q % 2][:, j * P:(j + 1) * P], w_uk[:],
                                  start=True, stop=True).then_inc(s["kn"], 1)
                    pe.matmul(S[half][0:R, :], qwz[:, b * R:(b + 1) * R], cT[q % 2][:, :],
                              start=(b == 0), stop=False)
                    pe.matmul(S[half][0:R, :], qrz[:, b * R:(b + 1) * R], krT[q % 2][:, :],
                              start=False, stop=(b == NSA - 1)).then_inc(s["sc"], 1)
                pe.wait_ge(s["inv"], 1)
                for j in range(NPAGE):
                    ins = pe.transpose(c.ps[j // HALF][0:R, (j % HALF) * P:(j % HALF + 1) * P],
                                       ms[:, j].rearrange("p h b -> p (h b)"), c.ident[:, :])
                ins.then_inc(s["invt"], 1)
                for h in range(MH):
                    ins = pe.matmul(c.ps[2][0:R, 0:NSA], qz[:, h * R:(h + 1) * R], c.KTs[:, h, :],
                                    start=(h == 0), stop=(h == MH - 1))
                ins.then_inc(s["new"], 1)
                pe.wait_ge(s["norm"], 1)
                for j in range(NPAGE):
                    ins = pe.transpose(c.ps[4][:, j * R:(j + 1) * R], sc[:, j * P:(j + 1) * P], c.ident[0:R, 0:R])
                pe.transpose(c.ps[5][0:NSA, 0:R], sc[:, PAST:PAST + NSA], c.ident[0:R, 0:R]).then_inc(s["pt"], 1)
                pe.wait_ge(s["ptc"], 2)
                pe.matmul(c.ps[3][:, 0:R], c.lat_s[:, 0:KVL], pTn[:], start=True, stop=False)
                for b in range(NSA):
                    for j in range(NPAGE):
                        last = b == NSA - 1 and j == NPAGE - 1
                        ins = pe.matmul(c.ps[3][:, b:R:NSA], rows[:, b * NPAGE + j, 0:KVL], pT[:, j, b:R:NSA],
                                        start=False, stop=last)
                ins.then_inc(s["ctx"], 1)
                pe.wait_ge(s["ctxc"], 1)
                for h in range(MH):
                    p0, k = VH * (h % 2), h // 2
                    ins = pe.matmul(c.ps[2][p0:p0 + VH, k * NSA:(k + 1) * NSA], w_uv[:, h * VH:(h + 1) * VH],
                                    cx[:, h * NSA:(h + 1) * NSA], start=True, stop=True)
                ins.then_inc(s["out"], 1)

            @block.scalar
            def _(act):
                for dst, src in ((w_ukT, "w_ukT"), (w_uk, "w_uk"), (w_uv, "w_uv"), (diag, "diag")):
                    act.dma_start(dst[:], IN[src]).then_inc(s["w_in"], 16)

                def copies(q):
                    act.wait_ge(s["tr"], q + 1)
                    if q >= 2:
                        act.wait_ge(s["sc"], q - 1)
                    act.activation(cT[q % 2][:], c.ps[q % 2][:], ACT.Copy).then_inc(s["trc"], 1)
                    act.activation(krT[q % 2][:], c.ps[2 + q % 2][0:ROPE, :], ACT.Copy).then_inc(s["trc"], 1)

                copies(0)
                for q in range(NQ):
                    if q + 1 < NQ:
                        copies(q + 1)
                    for j in range(HALF):
                        n = q * HALF + j
                        act.wait_ge(s["kn"], n + 1)
                        if n >= 2:
                            act.wait_ge(s["red"], n - 1)
                        act.activation(ksq[n % 2][:], c.ps[4 + n % 2][:].rearrange("p (h d) -> p h d", d=NOPE),
                                       ACT.Square).then_inc(s["sq"], 1)
                act.wait_ge(s["root"], 1)
                act.activation(ms[:], ms[:], ACT.Sqrt, scale=1.0 / QK, bias=c.eps[:]).then_inc(s["root"], 1)
                act.wait_ge(s["invt"], 1)
                for i in range(2):
                    act.activation(invT[:, i * 512:(i + 1) * 512], c.ps[i][0:R, :], ACT.Copy).then_inc(s["invc"], 1)
                act.wait_ge(s["nmax"], 1)
                act.activation(sc[:], sc[:], ACT.Exp, bias=st[:, 0:1], accum_out=st[:, 1:2]).then_inc(s["exp"], 1)
                act.wait_ge(s["pt"], 1)
                act.activation(pT[:], c.ps[4][:].rearrange("p (j r) -> p j r", r=R), ACT.Copy).then_inc(s["ptc"], 1)
                act.activation(pTn[:], c.ps[5][0:NSA, 0:R], ACT.Copy).then_inc(s["ptc"], 1)

            @block.vector
            def _(dve):
                for t in (qwz, qrz, qz):
                    ins = dve.memset(t[:], 0.0)
                c.vstep(dve, ins)
                dve.tensor_scalar(qg[:], c.QTs[0:NOPE].rearrange("p h b -> p (h b)"), c.gT[0:NOPE, 18:19], None,
                                  ALU.mult).then_inc(s["prep"], 1)
                dve.tensor_copy(qrz[:].rearrange("p (b x) -> p b x", x=Z)[:, :, 0:R:NSA],
                                c.QTs[NOPE:QK].rearrange("p h b -> p b h")).then_inc(s["prep"], 1)
                dve.tensor_copy(qz[:].rearrange("p (h x) -> p h x", x=R + NSA)[:, :, 0:NSA], c.QTs[:])\
                   .then_inc(s["prep"], 1)
                dve.wait_ge(s["qw"], 1)
                dve.tensor_copy(qwz[:].rearrange("p (b x) -> p b x", x=Z)[:, :, 0:R:NSA],
                                c.ps[4][:, 0:R].rearrange("p (h b) -> p b h", b=NSA)).then_inc(s["prep"], 1)

                def rope_keys(b):
                    pg = slice(b * NPAGE, (b + 1) * NPAGE)
                    dve.wait_ge(pages_in[b], 16 * NPAGE)
                    if b >= 2:
                        dve.wait_ge(s["tr"], 2 * (b - 1))
                    kr = rows[:, pg, KVL:LAT]
                    gain = c.rows[:, R_KN + NOPE:R_KN + QK].unsqueeze(1).to_broadcast([P, NPAGE, ROPE])
                    dve.tensor_tensor(krr[b % 2][:], kr, gain, ALU.mult)
                    c.vstep(dve, dve.tensor_tensor(krq[:], kr, kr, ALU.mult))
                    dve.tensor_reduce(krs[:, pg], krq[:], AX.X, ALU.add)
                    rotate(dve, c, krr[b % 2], krr[b % 2], c.rot[:, 0, 0:NPAGE, :], tmp, s["kr"])

                rope_keys(0)
                for b in range(NSA):
                    if b + 1 < NSA:
                        rope_keys(b + 1)
                    for j in range(NPAGE):
                        n = b * NPAGE + j
                        dve.wait_ge(s["sq"], n + 1)
                        dve.tensor_reduce(ms[:, j, :, b], ksq[n % 2][:], AX.X, ALU.add).then_inc(s["red"], 1)
                dve.wait_ge(s["red"], NSA * NPAGE)
                ins = dve.tensor_tensor(ms[:], ms[:], krs[:].rearrange("p (b j) -> p j b", j=NPAGE).unsqueeze(2)
                                        .to_broadcast([P, NPAGE, MH, NSA]), ALU.add)
                ins.then_inc(s["root"], 1)
                dve.wait_ge(s["root"], 2)
                dve.reciprocal(ms[:], ms[:]).then_inc(s["inv"], 1)
                dve.wait_ge(s["new"], 1)
                dve.wait_ge(s["w_in"], 64)
                dve.tensor_tensor(sc[:, PAST:PAST + NSA], c.ps[2][0:R, 0:NSA], diag[:], ALU.add)
                for i in range(2):
                    dve.wait_ge(s["sc"], 2 * NSA)
                    dve.wait_ge(s["invc"], i + 1)
                    cols = slice(i * 512, (i + 1) * 512)
                    ins = dve.tensor_tensor(sc[:, cols], S[i][0:R, :], invT[:, cols], ALU.mult)
                c.vstep(dve, ins)
                dve.tensor_reduce(st[:, 0:1], sc[:], AX.X, ALU.max, negate=True).then_inc(s["nmax"], 1)
                dve.wait_ge(s["exp"], 1)
                c.vstep(dve, dve.reciprocal(st[:, 2:3], st[:, 1:2]))
                dve.tensor_scalar(sc[:], sc[:], st[:, 2:3], None, ALU.mult).then_inc(s["norm"], 1)
                dve.wait_ge(s["ctx"], 1)
                dve.tensor_copy(cx[:], c.ps[3][:, 0:R]).then_inc(s["ctxc"], 1)
                dve.wait_ge(s["out"], 1)
                dve.tensor_copy(c.o_mlaT[:, :, NPR:TOK], c.ps[2][:, 0:MH // 2 * NSA]
                                .rearrange("p (k b) -> p k b", b=NSA))


def tail_rows(OUT, g, b, kv):
    keep = min(GROUPS[g][0], NPR)
    out = OUT[f"dil{g}_prompt"][:, kv, :]
    if g == 0 and b < NPR // P - keep // P or g == 1 and b % 2 == 0:
        return []
    return [(slice(0, P), out[sub_slice(g, b, NPR - keep)])]


def stage_dilated_project(c, g, w, wh, wl, sb):
    nc, IN, OUT = c.nc, c.IN, c.OUT
    NB = len(TILES)
    if True:
        z = [sb(f"z{i}", [P, DH, DE]) for i in range(3)]
        sq = sb("zsq", [P, DH, DE])
        st = [sb(f"zst{i}", [P, 3, DH]) for i in range(2)]
        tmp = sb("ztmp", [P, 4, DH, RH])
        s = {t: c.sem(f"dp{g}_{t}") for t in
             "h_hi h_lo w_hi w_lo mm zcopy zsq ss root fin tr trc vcopy k_out v_out".split()}
        w_in = [c.sem(f"dp{g}_w{i}") for i in range(3)]
        k_out = [c.sem(f"dp{g}_k_out{i}") for i in range(3)]
        units = [(ch, b) for ch in range(3) for b in range(NB)]
        n_norm = 2 * NB
        stores = [[], [], []]

        def z_stores(v):
            ch, b = units[v]
            if b == NB - 1:
                dst = c.dram["q_dil_sample"][g].rearrange("(b f) -> b f", f=GW) if ch == 0 \
                    else OUT[f"dil{g}_sample"][:, 0, :]
                return [(slice(0, NSA), dst)]
            return tail_rows(OUT, g, b, 0) if ch == 1 else []

        def stored(v):
            return 16 * sum(len(z_stores(x)) for x in range(v % 3, v + 1, 3))

        def high_parts(act, ch):
            if ch or g == 0:
                act.wait_ge(w_in[ch], 16)
            if ch:
                act.wait_ge(s["mm"], ch * NB)
            for k in range(KD):
                if g == 0 and ch == 0:
                    act.activation(c.hh[:, k], c.hT[:, k], ACT.Copy).then_inc(s["h_hi"], 1)
                act.activation(wh[:, k], w[ch % 2][:, k], ACT.Copy).then_inc(s["w_hi"], 1)

        def low_parts(dve, ch):
            for k in range(KD):
                if g == 0 and ch == 0:
                    dve.wait_ge(s["h_hi"], k + 1)
                    low_part(dve, c.hl[:, k], c.hT[:, k], c.hh[:, k]).then_inc(s["h_lo"], 1)
                dve.wait_ge(s["w_hi"], ch * KD + k + 1)
                low_part(dve, wl[ch % 2][:, k], w[ch % 2][:, k], wh[:, k]).then_inc(s["w_lo"], 1)

        with nc.Block() as block:
            @block.gpsimd
            def _(pool):
                for ch in range(1 if g else 0, 3):
                    if ch == 2:
                        pool.wait_ge(s["mm"], NB)
                    pool.dma_start(w[ch % 2][:], IN["w_dil"][ch * NG + g]).then_inc(w_in[ch], 16)

            @block.sync
            def _(sp):
                for v in range(n_norm):
                    lots = z_stores(v)
                    if lots:
                        sp.wait_ge(s["fin"], v + 1)
                    for rows, dst in lots:
                        sp.dma_start(dst, z[v % 3][rows].rearrange("p h d -> p (h d)")).then_inc(k_out[v % 3], 16)
                count = 0
                for b in range(NB):
                    lots = tail_rows(OUT, g, b, 1) if b < NB - 1 else [(slice(0, NSA), OUT[f"dil{g}_sample"][:, 1, :])]
                    if lots:
                        sp.wait_ge(s["vcopy"], b + 1)
                    for rows, dst in lots:
                        src = c.dV[rows, b, :] if b < NB - 1 else c.dvs[:, g, :]
                        sp.dma_start(dst, src).then_inc(s["v_out"], 16)
                        count += 1
                sp.wait_ge(s["v_out"], 16 * count)
                for i in range(3):
                    sp.wait_ge(k_out[i], stored(n_norm - 3 + i))

            @block.tensor
            def _(pe):
                def turn(v):
                    n = TILES[units[v][1]][1]
                    pe.wait_ge(s["fin"], v + 1)
                    if v >= 2:
                        pe.wait_ge(s["trc"], v - 1)
                    bank = c.ps[4 + v % 2]
                    for h in range(DH):
                        ins = pe.transpose(bank[:, h * P:h * P + n], z[v % 3][0:n, h, :], c.ident[0:n, 0:n])
                    ins.then_inc(s["tr"], 1)

                for v, (ch, b) in enumerate(units):
                    if v >= 4:
                        x = v - 4
                        pe.wait_ge(s["zsq"], min(x, n_norm - 1) + 1)
                        if x >= n_norm:
                            pe.wait_ge(s["vcopy"], x - n_norm + 1)
                    n = TILES[b][1]
                    toks = slice(NPR, TOK) if n == NSA else sub_slice(g, b)
                    for k in range(KD):
                        if v == 0 and g == 0:
                            pe.wait_ge(s["h_lo"], k + 1)
                        if b == 0:
                            pe.wait_ge(s["w_lo"], ch * KD + k + 1)
                        ins = product3(pe, c.ps[v % 4][0:n, :], [a[:, k, toks] for a in (c.hh, c.hl)],
                                       [wh[:, k, :], wl[ch % 2][:, k, :]], k == 0, k == KD - 1)
                    ins.then_inc(s["mm"], 1)
                    if 1 <= v <= n_norm:
                        turn(v - 1)

            @block.scalar
            def _(act):
                def turned(v):
                    ch, b = units[v]
                    n = TILES[b][1]
                    act.wait_ge(s["tr"], v + 1)
                    if b == NB - 1:
                        dst = (c.dqs, c.dks)[ch][:, g]
                    else:
                        dst = (c.dQ, c.dK)[ch][:, :, b * P:(b + 1) * P]
                    act.activation(dst, c.ps[4 + v % 2][:].rearrange("p (h q) -> p h q", q=P)[:, :, 0:n],
                                   ACT.Copy).then_inc(s["trc"], 1)

                high_parts(act, 0)
                for v, (ch, b) in enumerate(units):
                    n = TILES[b][1]
                    if b == NB - 1 and ch < 2:
                        high_parts(act, ch + 1)
                    act.wait_ge(s["mm"], v + 1)
                    src = c.ps[v % 4][0:n, :]
                    if ch == 2:
                        dst = c.dV[:, b, :] if b < NB - 1 else c.dvs[:, g, :]
                        act.activation(dst, src, ACT.Copy).then_inc(s["vcopy"], 1)
                    else:
                        if v >= 3:
                            act.wait_ge(s["tr"], v - 2)
                            if stored(v - 3):
                                act.wait_ge(k_out[v % 3], stored(v - 3))
                        src = src.rearrange("p (h d) -> p h d", d=DE)
                        act.activation(z[v % 3][0:n], src, ACT.Copy).then_inc(s["zcopy"], 1)
                        if v:
                            act.wait_ge(s["ss"], v)
                        act.activation(sq[0:n], src, ACT.Square).then_inc(s["zsq"], 1)
                        act.wait_ge(s["ss"], v + 1)
                        act.activation(st[v % 2][0:n, 1], st[v % 2][0:n, 0], ACT.Sqrt, scale=1.0 / DE,
                                       bias=c.eps[0:n]).then_inc(s["root"], 1)
                    if 1 <= v <= n_norm:
                        turned(v - 1)

            @block.vector
            def _(dve):
                tn = Turn()
                low_parts(dve, 0)
                for v in range(n_norm):
                    ch, b = units[v]
                    n = TILES[b][1]
                    if b == NB - 1:
                        low_parts(dve, ch + 1)
                    gain = c.rows[:, R_DQ:R_DQ + DE] if ch == 0 else c.rows[:, R_DK:R_DK + DE]
                    x, t = z[v % 3][0:n], st[v % 2]
                    dve.wait_ge(s["zsq"], v + 1)
                    dve.tensor_reduce(t[0:n, 0], sq[0:n], AX.X, ALU.add).then_inc(s["ss"], 1)
                    normed_rows(dve, c, x, t[0:n, 0], t[0:n, 1], t[0:n, 2], gain, DE, s["root"], tn, None)
                    rotate(dve, c, x[:, :, 0:ROPE], x[:, :, 0:ROPE], c.rot[:, 1 + g, b], tmp, s["fin"])


def dilated_span(c, g, b):
    if g == 2:
        return b, 1, 0, c.masks[:, 2, :]
    if b == 0 or g == 1 and b % 2 == 0:
        return b, 1, 0, c.masks[:, 1, :]
    return b - 1, 2, 0, c.masks[:, 0:2, :].rearrange("p m k -> p (m k)")


class StoreOutput:

    def __init__(self, c, g, w):
        self.c, self.g = c, g
        self.used = c.sem(f"da{g}_stored")
        self.per_tile = 16
        self.w = w
        self.ada = (2, 4, None)[g]
        self.slots = [w[1][:, :, j * P:(j + 1) * P] for j in range(4)]
        self.w_in = [c.sem(f"da{g}_w_in{j}") for j in range(4)]
        self.ada_mm, self.next_in = c.sem(f"da{g}_ada_mm"), c.sem(f"da{g}_next_in")

    def tensor(self, pe, b, o, s):
        pass

    def scalar(self, act, b, o, s):
        pass

    def beside(self, pe, u):
        if not self.ada or u % 2 == 0:
            return
        m, n = u // 2, 1 + NSA
        pe.wait_ge(self.w_in[m % 4], 16 * (m // 4 + 1))
        for k in range(KD):
            ins = pe.matmul(self.c.ps[7][:, m * n:(m + 1) * n], self.slots[m % 4][:, k, :], self.c.silu_c[:, k, :],
                            start=(k == 0), stop=(k == KD - 1))
        ins.then_inc(self.ada_mm, 1)

    def vector(self, dve):
        if self.ada:
            dve.wait_ge(self.ada_mm, 2 * KD)
            add_bias(dve, self.c, self.ada, self.c.ps[7][:, 0:2 * KD * (1 + NSA)])
            if self.ada == 4:
                gain_scale(dve, self.c, 1)

    def gpsimd(self, pool):
        for m in range(2 * KD if self.ada else 0):
            if m == 4:
                pool.dma_start(self.w[0][:], self.c.IN["w_dil"][self.g + 1]).then_inc(self.next_in, 16)
            if m >= 4:
                pool.wait_ge(self.ada_mm, m - 3)
            pool.dma_start(self.slots[m % 4], self.c.IN["w_ada"][self.ada * KD + m]).then_inc(self.w_in[m % 4], 16)
        if self.ada:
            pool.wait_ge(self.next_in, 16)

    def sync(self, sp, o, s):
        for b in range(NPR // P):
            sp.wait_ge(s["out"], DH * (b + 1))
            sp.dma_start(self.c.dram["o_group"][self.g][sub_slice(self.g, b)], o[b % 2][:]).then_inc(self.used, 16)
        sp.wait_ge(self.used, self.per_tile * (NPR // P))


def stage_dilated_combine(c):
    nc = c.nc
    W = GW + 2 * DH
    with ExitStack() as ctx:
        sb = lambda t, shape: ctx.enter_context(nc.sbuf_tensor("dc_" + t, shape, F32))
        x = [sb(f"x{i}", [P, NG, W]) for i in range(2)]
        e = sb("e", [P, NG, DH])
        den = sb("den", [P, NG, DH])
        m = sb("m", [P, DH])
        y = [sb(f"y{i}", [P, GW]) for i in range(2)]
        x_in = [c.sem(f"dc_x_in{i}") for i in range(2)]
        s = {t: c.sem("dc_" + t) for t in "diff exp y turn copy".split()}
        NT = NPR // P
        with nc.Block() as block:
            @block.sync
            def _(sp):
                for t in range(NT):
                    if t >= 2:
                        sp.wait_ge(s["y"], t - 1)
                    sp.dma_start(x[t % 2][:], c.dram["o_group"][:, t * P:(t + 1) * P, :]
                                 .rearrange("g p w -> p g w")).then_inc(x_in[t % 2], 16)

            @block.vector
            def _(dve):
                for t in range(NT):
                    X = x[t % 2]
                    nm, sm = X[:, :, GW:GW + DH], X[:, :, GW + DH:W]
                    dve.wait_ge(x_in[t % 2], 16 * (t // 2 + 1))
                    c.vstep(dve, dve.tensor_tensor(m[:], nm[:, 0], nm[:, 1], ALU.min))
                    c.vstep(dve, dve.tensor_tensor(m[:], m[:], nm[:, 2], ALU.min))
                    dve.tensor_tensor(e[:], m[:].unsqueeze(1).to_broadcast([P, NG, DH]), nm,
                                      ALU.subtract).then_inc(s["diff"], 1)
                    dve.wait_ge(s["exp"], t + 1)
                    c.vstep(dve, dve.tensor_tensor(den[:], e[:], sm, ALU.mult))
                    c.vstep(dve, dve.tensor_tensor(den[:, 0], den[:, 0], den[:, 1], ALU.add))
                    c.vstep(dve, dve.tensor_tensor(den[:, 0], den[:, 0], den[:, 2], ALU.add))
                    c.vstep(dve, dve.reciprocal(den[:, 1], den[:, 0]))
                    c.vstep(dve, dve.tensor_tensor(e[:], e[:], den[:, 1:2].to_broadcast([P, NG, DH]), ALU.mult))
                    if t >= 2:
                        dve.wait_ge(s["turn"], t - 1)
                    Y = y[t % 2]
                    for g in range(NG):
                        for h in range(DH):
                            cols = slice(h * DE, (h + 1) * DE)
                            if g == 0:
                                ins = dve.tensor_scalar(Y[:, cols], X[:, g, cols], e[:, g, h:h + 1], None, ALU.mult)
                            else:
                                ins = dve.scalar_tensor_tensor(out=Y[:, cols], in0=X[:, g, cols],
                                                               scalar=e[:, g, h:h + 1], in1=Y[:, cols],
                                                               op0=ALU.mult, op1=ALU.add)
                        if g < NG - 1:
                            c.vstep(dve, ins)
                    ins.then_inc(s["y"], 1)

            @block.scalar
            def _(act):
                for t in range(NT):
                    act.wait_ge(s["diff"], t + 1)
                    act.activation(e[:], e[:], ACT.Exp).then_inc(s["exp"], 1)
                    act.wait_ge(s["turn"], t + 1)
                    act.activation(c.o_dilT[:, :, t * P:(t + 1) * P],
                                   c.ps[t % 2][:].rearrange("p (k q) -> p k q", q=P), ACT.Copy).then_inc(s["copy"], 1)

            @block.tensor
            def _(pe):
                for t in range(NT):
                    pe.wait_ge(s["y"], t + 1)
                    if t >= 2:
                        pe.wait_ge(s["copy"], t - 1)
                    for k in range(GW // P):
                        ins = pe.transpose(c.ps[t % 2][:, k * P:(k + 1) * P], y[t % 2][:, k * P:(k + 1) * P],
                                           c.ident[:, :])
                    ins.then_inc(s["turn"], 1)


def stage_dilated_sample(c):
    nc, IN = c.nc, c.IN
    R = DH * NSA
    KROWS = [128, 128, 64]
    with ExitStack() as ctx:
        sb = lambda t, shape, dt=F32: ctx.enter_context(nc.sbuf_tensor("ds_" + t, shape, dt))
        kv = [sb(f"kv{i}", [P, 2, 2 * GW]) for i in range(3)]
        V = [sb(f"v{g}", [P, NSA, GW]) for g in range(NG)]
        qb = [sb(f"qb{i}", [P, 2, GW]) for i in range(3)]
        sT = sb("scoresT", [P, NG, DH, NSA])
        qz = sb("q_padded", [P, NG, DH * (R + NSA)])
        diag = sb("diag", [R, NSA])
        sc = sb("scores", [R, NG, P + NSA])
        st = sb("stats", [R, 4])
        pT = sb("pT", [P, NG, R])
        pTn = sb("pT_new", [NSA, NG, R])
        s = {t: c.sem("ds_" + t) for t in "diag zero kT t new fill nmax exp norm pt ptc out qz vv".split()}
        kv_in = [c.sem(f"ds_kv_in{i}") for i in range(3)]
        pairs = [(g, b) for g in range(NG) for b in range(0, NSA, 2)]
        with nc.Block() as block:
            @block.sync
            def _(sp):
                sp.dma_start(diag[:], IN["diag"][0:R]).then_inc(s["diag"], 16)
                for i, (g, b) in enumerate(pairs):
                    if i >= 3:
                        sp.wait_ge(s["kT"], i - 2)
                        sp.wait_ge(s["vv"], i - 2)
                    n, step = KROWS[g], GROUPS[g][1]
                    src = IN[f"state{g}"][b:b + 2, 0:step * (n - 1) + 1:step, :].rearrange("b p f -> p b f")
                    sp.dma_start(kv[i % 3][0:n], src).then_inc(kv_in[i % 3], 16)
                    q = c.dram["q_dil_sample"][g, b * GW:(b + 2) * GW].unsqueeze(0).to_broadcast([n, 2 * GW])
                    sp.dma_start(qb[i % 3][0:n].rearrange("p b f -> p (b f)"), q).then_inc(kv_in[i % 3], 16)

            @block.gpsimd
            def _(pool):
                pool.memset(sT[:], NEG).then_inc(s["zero"], 1)

            @block.scalar
            def _(act):
                for i, (g, b) in enumerate(pairs):
                    n = KROWS[g]
                    act.wait_ge(kv_in[i % 3], 32 * (i // 3 + 1))
                    act.activation(V[g][0:n, b:b + 2, :], kv[i % 3][0:n, :, GW:], ACT.Copy).then_inc(s["vv"], 1)
                act.wait_ge(s["nmax"], 1)
                act.activation(sc[:], sc[:], ACT.Exp, bias=st[:, 0:1], accum_out=st[:, 1:2]).then_inc(s["exp"], 1)
                act.wait_ge(s["pt"], 1)
                act.activation(pT[:], c.ps[2][:, 0:NG * R].rearrange("p (g r) -> p g r", r=R), ACT.Copy)\
                   .then_inc(s["ptc"], 1)
                act.activation(pTn[:], c.ps[3][0:NSA, 0:NG * R].rearrange("p (g r) -> p g r", r=R), ACT.Copy)\
                   .then_inc(s["ptc"], 1)

            @block.vector
            def _(dve):
                c.vstep(dve, dve.memset(qz[:], 0.0))
                for g in range(NG):
                    ins = dve.tensor_copy(qz[:, g].rearrange("p (h x) -> p h x", x=R + NSA)[:, :, 0:NSA], c.dqs[:, g])
                ins.then_inc(s["qz"], 1)
                dve.wait_ge(s["zero"], 1)
                for i, (g, b) in enumerate(pairs):
                    n = KROWS[g]
                    dve.wait_ge(kv_in[i % 3], 32 * (i // 3 + 1))
                    q = qb[i % 3][0:n]
                    c.vstep(dve, dve.tensor_tensor(q, kv[i % 3][0:n, :, 0:GW], q, ALU.mult))
                    dve.tensor_reduce(sT[0:n, g, :, b:b + 2], q.rearrange("p b (h e) -> p h b e", e=DE),
                                      AX.X, ALU.add).then_inc(s["kT"], 1)
                dve.wait_ge(s["new"], 1)
                dve.wait_ge(s["diag"], 16)
                dve.tensor_copy(sc[:, :, 0:P], c.ps[0][0:R, 0:NG * P].rearrange("p (g k) -> p g k", k=P))
                c.vstep(dve, dve.tensor_tensor(
                    sc[:, :, P:], c.ps[1][0:R, 0:NG * NSA].rearrange("p (g k) -> p g k", k=NSA),
                    diag[:].unsqueeze(1).to_broadcast([R, NG, NSA]), ALU.add))
                dve.tensor_reduce(st[:, 0:1], sc[:].rearrange("p g k -> p (g k)"), AX.X, ALU.max, negate=True)\
                   .then_inc(s["nmax"], 1)
                dve.wait_ge(s["exp"], 1)
                c.vstep(dve, dve.reciprocal(st[:, 2:3], st[:, 1:2]))
                dve.tensor_scalar(sc[:], sc[:], st[:, 2:3], None, ALU.mult).then_inc(s["norm"], 1)
                dve.wait_ge(s["out"], 1)
                dve.tensor_copy(c.o_dilT[:, :, NPR:TOK], c.ps[4][:, 0:R].rearrange("p (h b) -> p h b", b=NSA))

            @block.tensor
            def _(pe):
                pe.wait_ge(s["qz"], 1)
                pe.wait_ge(s["kT"], len(pairs))
                for g in range(NG):
                    pe.transpose(c.ps[0][0:R, g * P:(g + 1) * P], sT[:, g].rearrange("p h b -> p (h b)"), c.ident[:, :])
                for g in range(NG):
                    for h in range(DH):
                        ins = pe.matmul(c.ps[1][0:R, g * NSA:(g + 1) * NSA], qz[:, g, h * R:(h + 1) * R],
                                        c.dks[:, g, h, :], start=(h == 0), stop=(h == DH - 1))
                ins.then_inc(s["new"], 1)
                pe.wait_ge(s["norm"], 1)
                for g in range(NG):
                    pe.transpose(c.ps[2][:, g * R:(g + 1) * R], sc[:, g, 0:P], c.ident[0:R, 0:R])
                for g in range(NG):
                    ins = pe.transpose(c.ps[3][0:NSA, g * R:(g + 1) * R], sc[:, g, P:P + NSA], c.ident[0:R, 0:R])
                ins.then_inc(s["pt"], 1)
                pe.wait_ge(s["ptc"], 2)
                pe.wait_ge(s["vv"], len(pairs))
                for h in range(DH):
                    out = c.ps[4][:, h * NSA:(h + 1) * NSA]
                    for g in range(NG):
                        pe.matmul(out, c.dvs[:, g, h * DE:(h + 1) * DE], pTn[:, g, h * NSA:(h + 1) * NSA],
                                  start=(g == 0), stop=False)
                    for g in range(NG):
                        n = KROWS[g]
                        for b in range(NSA):
                            ins = pe.matmul(out[:, b:b + 1], V[g][0:n, b, h * DE:(h + 1) * DE],
                                            pT[0:n, g, h * NSA + b:h * NSA + b + 1],
                                            start=False, stop=(g == NG - 1 and b == NSA - 1))
                ins.then_inc(s["out"], 1)


def stage_mix(c):
    nc, IN = c.nc, c.IN
    KO = GW // P
    with ExitStack() as ctx:
        sb = lambda t, shape, dt=F32: ctx.enter_context(nc.sbuf_tensor("mx_" + t, shape, dt))
        wb = [sb(f"w_branch{i}", [P, 2 * KO, P]) for i in range(2)]
        wh = [sb(f"w_high{i}", [P, 2 * KD, P], F32R) for i in range(2)]
        w, wl = zip(*(same_place(c, ctx, [P, 2 * KD, P], [(f"mx_w{i}", F32), (f"mx_w_low{i}", F32R)])
                      for i in range(2)))
        y, yl = same_place(c, ctx, [P, KD, TOK], [("mx_y", F32), ("mx_y_low", F32R)])
        x = c.x_mix
        h_parts, y_parts = (c.hh, c.hl), (c.y_high, yl)
        sg = [sb(f"sig{i}", [P, 2, CH]) for i in range(2)]
        t = [sb(f"t{i}", [P, 2, CH]) for i in range(2)]
        ts = sb("ts", [P, KD, NSA])
        s = {n: c.sem("mx_" + n) for n in "w_hi w_lo mm sig y y_hi y_lo out_mm out stored".split()}
        w_in = [c.sem(f"mx_w_in{i}") for i in range(2)]
        x_in = [c.sem(f"mx_x_in{m}") for m in range(KD)]
        gate1 = c.mod[:, 2]
        units = [(m, i) for m in range(KD) for i in range(NCH)]

        def used(w_at):
            return slice(0, 2 * KD if w_at < KD else KD)

        def w_high(act, n):
            act.wait_ge(w_in[n % 2], 64 * (n // 2 + 1) if n < KD else 64 * (KD // 2) + 16 * ((n - KD) // 2 + 1))
            act.activation(wh[n % 2][:, used(n)], w[n % 2][:, used(n)], ACT.Copy).then_inc(s["w_hi"], 1)

        def w_low(dve, n):
            dve.wait_ge(s["w_hi"], n + 1)
            low_part(dve, wl[n % 2][:, used(n)], w[n % 2][:, used(n)], wh[n % 2][:, used(n)])\
                .then_inc(s["w_lo"], 1)

        def w_parts(n, k):
            return [wh[n % 2][:, k, :], wl[n % 2][:, k, :]]

        with nc.Block() as block:
            @block.sync
            def _(sp):
                for m in range(KD):
                    if m >= 2:
                        sp.wait_ge(s["mm"], NCH * (m - 1))
                    for dst, src in ((wb[m % 2][:, 0:KO], IN["w_mla"][m]), (wb[m % 2][:, KO:], IN["w_dilb"][m]),
                                     (w[m % 2][:, 0:KD], IN["w_gate"][m]), (w[m % 2][:, KD:], IN["w_gate"][KD + m])):
                        sp.dma_start(dst, src).then_inc(w_in[m % 2], 16)
                for m in range(KD):
                    if m < 2:
                        sp.wait_ge(s["mm"], NCH * (KD - 1 + m))
                    else:
                        sp.wait_ge(s["out_mm"], NCH * (m - 1))
                    sp.dma_start(w[m % 2][:, 0:KD], IN["w_out"][m]).then_inc(w_in[m % 2], 16)
                    if m == 1:
                        for k in range(KD):
                            sp.dma_start(x[:, k], IN["xT"][:, k]).then_inc(x_in[k], 16)
                for m in range(KD):
                    sp.wait_ge(s["out"], NCH * (m + 1))
                    sp.dma_start(c.dram["x1_dram"][:, m], x[:, m]).then_inc(s["stored"], 16)
                sp.wait_ge(s["stored"], 16 * KD)

            @block.tensor
            def _(pe):
                for u, (m, i) in enumerate(units):
                    cols = slice(i * CH, (i + 1) * CH)
                    if i == 0:
                        pe.wait_ge(w_in[m % 2], 64 * (m // 2 + 1))
                    if u >= 2:
                        pe.wait_ge(s["y"], u - 1)
                    bank = c.ps[4 * (u % 2):4 * (u % 2) + 4]
                    for n, (src, at) in enumerate(((c.o_mlaT, 0), (c.o_dilT, KO))):
                        for k in range(KO):
                            pe.matmul(bank[2 + n][:, 0:CH], wb[m % 2][:, at + k, :], src[:, k, cols],
                                      start=(k == 0), stop=(k == KO - 1))
                    if i == 0:
                        pe.wait_ge(s["w_lo"], m + 1)
                    for n in range(2):
                        for k in range(KD):
                            ins = product3(pe, bank[n][:, 0:CH], w_parts(m, n * KD + k),
                                           [a[:, k, cols] for a in h_parts], k == 0, k == KD - 1)
                    ins.then_inc(s["mm"], 1)
                pe.wait_ge(s["y"], len(units))
                for u, (m, i) in enumerate(units):
                    if i == 0:
                        pe.wait_ge(s["w_lo"], KD + m + 1)
                    if u >= 4:
                        pe.wait_ge(s["out"], u - 3)
                    for k in range(KD):
                        if u == 0:
                            pe.wait_ge(s["y_lo"], k + 1)
                        ins = product3(pe, c.ps[u % 4][:, 0:CH], w_parts(KD + m, k),
                                       [a[:, k, i * CH:(i + 1) * CH] for a in y_parts], k == 0, k == KD - 1)
                    ins.then_inc(s["out_mm"], 1)

            @block.scalar
            def _(act):
                w_high(act, 0)
                w_high(act, 1)
                for u, (m, i) in enumerate(units):
                    act.wait_ge(s["mm"], u + 1)
                    if u >= 2:
                        act.wait_ge(s["y"], u - 1)
                    for n in range(2):
                        ins = act.activation(sg[u % 2][:, n], c.ps[4 * (u % 2) + n][:, 0:CH], ACT.Sigmoid)
                    ins.then_inc(s["sig"], 1)
                    if m and i == 1:
                        w_high(act, m + 1)
                act.wait_ge(s["y"], len(units))
                for k in range(KD):
                    act.activation(y_parts[0][:, k], y[:, k], ACT.Copy).then_inc(s["y_hi"], 1)
                for n in range(KD + 1, 2 * KD):
                    w_high(act, n)

            @block.vector
            def _(dve):
                w_low(dve, 0)
                w_low(dve, 1)
                for u, (m, i) in enumerate(units):
                    dve.wait_ge(s["sig"], u + 1)
                    for n in range(2):
                        ins = dve.tensor_tensor(t[u % 2][:, n], sg[u % 2][:, n], c.ps[4 * (u % 2) + 2 + n][:, 0:CH],
                                                ALU.mult)
                    c.vstep(dve, ins)
                    dve.tensor_tensor(y[:, m, i * CH:(i + 1) * CH], t[u % 2][:, 0], t[u % 2][:, 1], ALU.add)\
                       .then_inc(s["y"], 1)
                    if m and i == 1:
                        w_low(dve, m + 1)
                dve.wait_ge(s["y"], len(units))
                for k in range(KD):
                    dve.wait_ge(s["y_hi"], k + 1)
                    low_part(dve, y_parts[1][:, k], y[:, k], y_parts[0][:, k]).then_inc(s["y_lo"], 1)
                w_low(dve, KD + 1)
                for u, (m, i) in enumerate(units):
                    a, e = i * CH, min((i + 1) * CH, NPR)
                    if i == 0:
                        dve.wait_ge(x_in[m], 16)
                    dve.wait_ge(s["out_mm"], u + 1)
                    ps = c.ps[u % 4]
                    ins = dve.scalar_tensor_tensor(out=x[:, m, a:e], in0=ps[:, 0:e - a], scalar=gate1[:, m, 0:1],
                                                   in1=x[:, m, a:e], op0=ALU.mult, op1=ALU.add)
                    if i == NCH - 1:
                        c.vstep(dve, dve.tensor_tensor(ts[:, m], ps[:, e - a:CH], gate1[:, m, 1:], ALU.mult))
                        ins = dve.tensor_tensor(x[:, m, NPR:TOK], x[:, m, NPR:TOK], ts[:, m], ALU.add)
                    ins.then_inc(s["out"], 1)
                    if m and i == 1 and m + 1 < KD:
                        w_low(dve, KD + m + 1)


class Ahead:
    ROUTE = 28
    TILES = ROUTE + 4 * (NPR // P)

    def __init__(self, c, ctx):
        sb = lambda t, shape, dt=F32: ctx.enter_context(c.nc.sbuf_tensor("ah_" + t, shape, dt))
        self.c = c
        self.u = [sb(f"u{i}", [P, KD, P]) for i in range(2)]
        self.up = [[sb(f"u_{t}{i}", [P, KD, P], F32R) for t in ("high", "low")] for i in range(2)]
        self.g = [sb(f"gelu{i}", [P, TOK]) for i in range(2)]
        self.u_in = [c.sem(f"ah_u_in{i}") for i in range(2)]
        self.out = [c.sem(f"ah_out{i}") for i in range(2)]
        self.u_hi, self.u_lo, self.mm, self.gelu = (c.sem("ah_" + t) for t in ("u_hi", "u_lo", "mm", "gelu"))

    @staticmethod
    def none(i, k, n):
        return isinstance(i, int) and 4 * i + k < n

    def load(self, eng, i, k):
        if not self.none(i, k, 2):
            eng.wait_ge(self.u_lo, i * 4 + (k - 1))
        eng.dma_start(self.u[k % 2][:].rearrange("p k e -> p (k e)"),
                      self.c.IN["uT"].rearrange("t p k e -> t p (k e)")[bass.ds(i * 4 + k, 1)]
                      .rearrange("o p n -> (o p) n")).then_inc(self.u_in[k % 2], 16)

    def high(self, act, i, k):
        act.wait_ge(self.u_in[k % 2], i * 32 + 16 * (k // 2) + 16)
        if not self.none(i, k, 2):
            act.wait_ge(self.mm, i * (4 * NCH) + NCH * (k - 1))
        act.activation(self.up[k % 2][0][:], self.u[k % 2][:], ACT.Copy).then_inc(self.u_hi, 1)

    def low(self, dve, i, k):
        dve.wait_ge(self.u_hi, i * 4 + (k + 1))
        low_part(dve, self.up[k % 2][1][:], self.u[k % 2][:], self.up[k % 2][0][:]).then_inc(self.u_lo, 1)

    def scores(self, pe, i, k, ch):
        if ch == 0:
            pe.wait_ge(self.u_lo, i * 4 + (k + 1))
        unit = NCH * k + ch
        if not (isinstance(i, int) and 4 * NCH * i + unit < 4):
            pe.wait_ge(self.gelu, i * (4 * NCH) + (unit - 3))
        for f in range(KD):
            ins = product3(pe, self.c.ps[unit % 4][:, 0:CH], [x[:, f, :] for x in self.up[k % 2]],
                           [x[:, f, ch * CH:(ch + 1) * CH] for x in self.c.hT2], f == 0, f == KD - 1)
        ins.then_inc(self.mm, 1)

    def gelus(self, act, i, k, ch):
        unit = NCH * k + ch
        if ch == 0 and not self.none(i, k, 2):
            act.wait_ge(self.out[k % 2], i * 32 + 16 * (k // 2))
        act.wait_ge(self.mm, i * (4 * NCH) + (unit + 1))
        act.activation(self.g[k % 2][:, ch * CH:(ch + 1) * CH], self.c.ps[unit % 4][:, 0:CH], ACT.Gelu)\
           .then_inc(self.gelu, 1)

    def store(self, act, i, k):
        act.wait_ge(self.gelu, i * (4 * NCH) + NCH * (k + 1))
        act.dma_start(self.c.dram["gelu_dram"][bass.ds(i * 4 + k, 1)].rearrange("o p n -> (o p) n"),
                      self.g[k % 2][:]).then_inc(self.out[k % 2], 16)


def stage_route(c):
    nc, IN = c.nc, c.IN
    NT = len(TILES)
    HP = 2 * PH

    def ahead_tiles(t):
        return range(3 * t, 3 * t + 3 if t < NT - 1 else Ahead.ROUTE)

    with ExitStack() as ctx:
        sb = lambda t, shape, dt=F32: ctx.enter_context(nc.sbuf_tensor("rt_" + t, shape, dt))
        ah = c.ahead
        w, wp = ah.u, ah.up
        keys = sb("keysT", [P, HP, NK])
        qT = [sb(f"qT{i}", [P, TOK]) for i in range(2)]
        sc = [sb(f"sc{i}", [P, NT, NK]) for i in range(2)]
        sc2 = sb("sc_rest", [P, NT, NK])
        top = sb("top", [P, NT, PH, 2, TOPK])
        topi = sb("topi", [P, NT, PH, 2, TOPK], U32)
        topf = sb("topf", [P, PH, 2, TOPK])
        cand = sb("cand", [P, PH, TOPK * TOPK])
        rest = sb("cand_rest", [P, PH, TOPK * TOPK])
        best = sb("best", [P, PH, TOPK])
        besti = sb("besti", [P, PH, TOPK], U32)
        part = sb("part", [P, 2, PH, TOPK], U32)
        partf = sb("partf", [P, 2, PH, TOPK])
        eq = [sb(f"eq{i}", [P, PH, TOPK, TOPK]) for i in range(2)]
        res = [sb(f"res{i}", [P, 3, PH * TOPK]) for i in range(2)]
        st = sb("stats", [P, 2, PH])
        s = {n: c.sem("rt_" + n) for n in "keys_in w_hi w_lo mm copy sc_mm sc_copy top diff exp res turn turned".split()}
        w_in = [c.sem(f"rt_w_in{i}") for i in range(2)]
        with nc.Block() as block:
            @block.sync
            def _(sp):
                sp.dma_start(keys[:], IN["keysT"]).then_inc(s["keys_in"], 16)
                for hp in range(HP):
                    if hp >= 2:
                        sp.wait_ge(s["w_lo"], hp - 1)
                    sp.dma_start(w[hp % 2][:], IN["w_pq"][hp]).then_inc(w_in[hp % 2], 16)

            @block.tensor
            def _(pe):
                def queries(hp):
                    pe.wait_ge(s["w_lo"], hp + 1)
                    for i in range(NCH):
                        if hp:
                            pe.wait_ge(s["copy"], NCH * (hp - 1) + i + 1)
                        for k in range(KD):
                            ins = product3(pe, c.ps[i][:, 0:CH], [x[:, k, :] for x in wp[hp % 2]],
                                           [x[:, k, i * CH:(i + 1) * CH] for x in c.hT2], k == 0, k == KD - 1)
                        ins.then_inc(s["mm"], 1)

                pe.wait_ge(s["keys_in"], 16)
                queries(0)
                for hp in range(HP):
                    if hp + 1 < HP:
                        queries(hp + 1)
                    pe.wait_ge(s["copy"], NCH * (hp + 1))
                    for t, (t0, n) in enumerate(TILES):
                        if hp and t % 4 == 0:
                            pe.wait_ge(s["sc_copy"], NCH * (hp - 1) + t // 4 + 1)
                        ins = pe.matmul(c.ps[3 + t // 4][0:n, (t % 4) * NK:(t % 4 + 1) * NK], qT[hp % 2][:, t0:t0 + n],
                                        keys[:, hp, :], start=True, stop=True)
                        if t % 4 == 3 or t == NT - 1:
                            ins.then_inc(s["sc_mm"], 1)
                for t, (t0, n) in enumerate(TILES):
                    for x in ahead_tiles(t):
                        for ch in range(NCH):
                            ah.scores(pe, 0, x, ch)
                    pe.wait_ge(s["res"], t + 1)
                    if t:
                        pe.wait_ge(s["turned"], t)
                    for j in range(3):
                        ins = pe.transpose(c.ps[6][:, j * P:j * P + n], res[t % 2][0:n, j, :], c.ident[0:n, 0:n])
                    ins.then_inc(s["turn"], 1)

            @block.scalar
            def _(act):
                def queries(hp):
                    if hp >= 2:
                        act.wait_ge(s["sc_mm"], NCH * (hp - 1))
                    for i in range(NCH):
                        act.wait_ge(s["mm"], NCH * hp + i + 1)
                        act.activation(qT[hp % 2][:, i * CH:(i + 1) * CH], c.ps[i][:, 0:CH], ACT.Copy)\
                           .then_inc(s["copy"], 1)

                def high(hp):
                    act.wait_ge(w_in[hp % 2], 16 * (hp // 2 + 1))
                    if hp >= 2:
                        act.wait_ge(s["mm"], NCH * (hp - 1))
                    act.activation(wp[hp % 2][0][:], w[hp % 2][:], ACT.Copy).then_inc(s["w_hi"], 1)

                high(0)
                high(1)
                queries(0)
                for hp in range(HP):
                    if hp + 1 < HP:
                        queries(hp + 1)
                    if hp + 2 < HP:
                        high(hp + 2)
                    if hp >= 2:
                        act.wait_ge(s["top"], hp - 1)
                    for i in range(NCH):
                        act.wait_ge(s["sc_mm"], NCH * hp + i + 1)
                        if i < 2:
                            dst, src = sc[hp % 2][:, 4 * i:4 * i + 4], c.ps[3 + i][:]
                            act.activation(dst, src.rearrange("p (t k) -> p t k", k=NK), ACT.Copy)\
                               .then_inc(s["sc_copy"], 1)
                        else:
                            act.activation(sc[hp % 2][0:NSA, 8], c.ps[5][0:NSA, 0:NK], ACT.Copy)\
                               .then_inc(s["sc_copy"], 1)
                act.wait_ge(s["w_lo"], HP)
                ah.load(act, 0, 0)
                ah.load(act, 0, 1)
                act.wait_ge(s["mm"], NCH * HP)
                ah.high(act, 0, 0)
                ah.load(act, 0, 2)
                for t, (t0, n) in enumerate(TILES):
                    for x in ahead_tiles(t):
                        ah.high(act, 0, x + 1)
                        for ch in range(NCH):
                            ah.gelus(act, 0, x, ch)
                        ah.store(act, 0, x)
                        ah.load(act, 0, x + 3)
                        if x % 3 == 1:
                            act.wait_ge(s["diff"], t + 1)
                            act.activation(best[0:n], best[0:n], ACT.Exp).then_inc(s["exp"], 1)
                    act.wait_ge(s["turn"], t + 1)
                    act.activation(c.pick[:, :, t0:t0 + n], c.ps[6][:, 0:3 * P].rearrange("p (j n) -> p j n", n=P)
                                   [:, :, 0:n], ACT.Copy).then_inc(s["turned"], 1)

            @block.vector
            def _(dve):
                def low(hp):
                    dve.wait_ge(s["w_hi"], hp + 1)
                    low_part(dve, wp[hp % 2][1][:], w[hp % 2][:], wp[hp % 2][0][:]).then_inc(s["w_lo"], 1)

                low(0)
                low(1)
                for hp in range(HP):
                    if hp + 2 < HP:
                        low(hp + 2)
                    S = sc[hp % 2]
                    T = lambda t, a: top[0:TILES[t][1], t, hp // 2, hp % 2, a:a + 8]
                    I = lambda t, a: topi[0:TILES[t][1], t, hp // 2, hp % 2, a:a + 8]
                    dve.wait_ge(s["sc_copy"], NCH * (hp + 1))
                    for t, (_, n) in enumerate(TILES):
                        ins = dve.max(T(t, 0), S[0:n, t])
                    c.vstep(dve, ins)
                    for t, (_, n) in enumerate(TILES):
                        dve.max_index(I(t, 0), T(t, 0), S[0:n, t])
                        ins = dve.match_replace(sc2[0:n, t], T(t, 0), S[0:n, t], NEG)
                    c.vstep(dve, ins)
                    for t, (_, n) in enumerate(TILES):
                        ins = dve.max(T(t, 8), sc2[0:n, t])
                    c.vstep(dve, ins)
                    for t, (_, n) in enumerate(TILES):
                        ins = dve.max_index(I(t, 8), T(t, 8), sc2[0:n, t])
                    c.vstep(dve, ins)
                    dve.engine_nop().then_inc(s["top"], 1)
                ah.low(dve, 0, 0)
                for t, (t0, n) in enumerate(TILES):
                    C, R = cand, res[t % 2]
                    lows = list(ahead_tiles(t))
                    ah.low(dve, 0, lows[0] + 1)
                    four = [n, PH, TOPK, TOPK]
                    c.vstep(dve, dve.tensor_tensor(C[0:n].rearrange("p h (a b) -> p h a b", b=TOPK),
                                                   top[0:n, t, :, 0].unsqueeze(3).to_broadcast(four),
                                                   top[0:n, t, :, 1].unsqueeze(2).to_broadcast(four), ALU.add))
                    if t:
                        dve.wait_ge(s["exp"], t)
                    for h in range(PH):
                        ins = dve.max(best[0:n, h, 0:8], C[0:n, h])
                    c.vstep(dve, ins)
                    for h in range(PH):
                        dve.max_index(besti[0:n, h, 0:8], best[0:n, h, 0:8], C[0:n, h])
                        ins = dve.match_replace(rest[0:n, h], best[0:n, h, 0:8], C[0:n, h], NEG)
                    c.vstep(dve, ins)
                    for h in range(PH):
                        ins = dve.max(best[0:n, h, 8:16], rest[0:n, h])
                    c.vstep(dve, ins)
                    for h in range(PH):
                        ins = dve.max_index(besti[0:n, h, 8:16], best[0:n, h, 8:16], rest[0:n, h])
                    c.vstep(dve, dve.tensor_copy(st[0:n, 0], best[0:n, :, 0]))
                    dve.tensor_tensor(best[0:n], best[0:n], st[0:n, 0].unsqueeze(2).to_broadcast([n, PH, TOPK]),
                                      ALU.subtract).then_inc(s["diff"], 1)
                    ah.low(dve, 0, lows[1] + 1)
                    dve.tensor_scalar(part[0:n, 0], besti[0:n], 4, None, ALU.logical_shift_right)
                    dve.tensor_scalar(part[0:n, 1], besti[0:n], 15, None, ALU.bitwise_and)
                    c.vstep(dve, dve.tensor_copy(topf[0:n], topi[0:n, t]))
                    c.vstep(dve, dve.tensor_copy(partf[0:n], part[0:n]))
                    if t >= 2:
                        dve.wait_ge(s["turn"], t - 1)
                    for j in range(2):
                        c.vstep(dve, dve.tensor_tensor(
                            eq[j][0:n], partf[0:n, j].unsqueeze(3).to_broadcast(four),
                            c.iota[0:n, 0:TOPK].unsqueeze(1).unsqueeze(1).to_broadcast(four), ALU.is_equal))
                        c.vstep(dve, dve.tensor_tensor(
                            eq[j][0:n], eq[j][0:n], topf[0:n, :, j].unsqueeze(2).to_broadcast(four), ALU.mult))
                        dve.tensor_reduce(R[0:n, j].rearrange("p (h k) -> p h k", k=TOPK), eq[j][0:n], AX.X, ALU.add)
                    ah.low(dve, 0, lows[2] + 1)
                    dve.wait_ge(s["exp"], t + 1)
                    c.vstep(dve, dve.tensor_reduce(st[0:n, 0], best[0:n], AX.X, ALU.add))
                    c.vstep(dve, dve.reciprocal(st[0:n, 1], st[0:n, 0]))
                    dve.tensor_tensor(R[0:n, 2].rearrange("p (h k) -> p h k", k=TOPK), best[0:n],
                                      st[0:n, 1].unsqueeze(2).to_broadcast([n, PH, TOPK]), ALU.mult)\
                       .then_inc(s["res"], 1)
                    for x in lows[3:]:
                        ah.low(dve, 0, x + 1)


def stage_gates(c):
    nc = c.nc
    ah = c.ahead
    RQ, QB = 4, 4
    BLK = GBLK
    TQ = P // 4
    BQ = BLK // 4
    TURNS = NPR // P
    A0 = Ahead.ROUTE // 4
    with ExitStack() as ctx:
        sb = lambda t, shape: ctx.enter_context(nc.sbuf_tensor("gt_" + t, shape, F32))
        first = [sb(f"first{i}", [P, 4, NK]) for i in range(RQ)]
        second = [sb(f"second{i}", [P, 4, NK]) for i in range(RQ)]
        stage = [sb(f"stage{i}", [P, NK, BLK]) for i in range(2)]
        s = {n: c.sem("gt_" + n) for n in "hot mm copy".split()}
        out = [c.sem(f"gt_out{i}") for i in range(2)]
        gates = c.dram["gates_dram"]
        NQ = TOK // 4
        TAIL = range(NPR // 4, NQ)

        def hots(dve, r, token):
            for i in range(4):
                pick = [c.pick[:, j, bass.ds(token + i, 1)] for j in range(3)]
                dve.tensor_scalar(first[r][:, i], c.iota[:], pick[0], pick[2], ALU.is_equal, ALU.mult)
                ins = dve.tensor_scalar(second[r][:, i], c.iota[:], pick[1], None, ALU.is_equal)
            ins.then_inc(s["hot"], 1)

        def products(pe, r, bank):
            for i in range(4):
                ins = pe.matmul(bank[:, i * NK:(i + 1) * NK], second[r][:, i], first[r][:, i], start=True, stop=True)
            ins.then_inc(s["mm"], 1)

        def to_stage(act, bank, buf, at):
            act.activation(buf[:, :, at:at + 4].rearrange("p a n -> p n a"),
                           bank[:].rearrange("p (n a) -> p n a", a=NK), ACT.Copy).then_inc(s["copy"], 1)

        def chunk(q):
            return (q // 8, (q % 8 - 1) // 2) if q % 2 and q % 8 < 6 else None

        HELD = (2, 3)

        def held(i, k):
            return isinstance(i, int) and i == TURNS - 1 and k in HELD

        last = lambda i, k, ahead: isinstance(i, int) and 4 * (i + A0) + k + ahead >= Ahead.TILES

        with nc.Block() as block:
            @block.vector
            def _(dve):
                def turn(i):
                    for q in range(TQ):
                        if not (isinstance(i, int) and i == 0 and q < RQ):
                            dve.wait_ge(s["mm"], i * TQ + (q - RQ + 1))
                        hots(dve, q % RQ, i * P + 4 * q)
                        if q % 8 == 4 and not last(i, q // 8, 1):
                            ah.low(dve, i + A0, q // 8 + 1)

                turn(0)
                with dve.Fori(1, TURNS - 1) as i:
                    turn(i)
                turn(TURNS - 1)
                for q in TAIL:
                    dve.wait_ge(s["mm"], q - RQ + 1)
                    hots(dve, q % RQ, 4 * q)

            @block.tensor
            def _(pe):
                def turn(i):
                    for q in range(TQ):
                        pe.wait_ge(s["hot"], i * TQ + q + 1)
                        if not (isinstance(i, int) and i == 0 and q < QB):
                            pe.wait_ge(s["copy"], i * TQ + (q - QB + 1))
                        products(pe, q % RQ, c.ps[4 + q % QB])
                        if chunk(q) and not held(i, q // 8):
                            ah.scores(pe, i + A0, *chunk(q))

                turn(0)
                with pe.Fori(1, TURNS - 1) as i:
                    turn(i)
                turn(TURNS - 1)
                for q in TAIL:
                    pe.wait_ge(s["hot"], q + 1)
                    pe.wait_ge(s["copy"], q - QB + 1)
                    products(pe, q % RQ, c.ps[4 + q % QB])
                for k in HELD:
                    for ch in range(NCH):
                        ah.scores(pe, TURNS - 1 + A0, k, ch)

            @block.scalar
            def _(act):
                def turn(i):
                    for q in range(TQ):
                        b = q // BQ
                        if q % BQ == 0 and not (isinstance(i, int) and i == 0):
                            act.wait_ge(out[b], i * 16)
                        act.wait_ge(s["mm"], i * TQ + q + 1)
                        to_stage(act, c.ps[4 + q % QB], stage[b], 4 * (q % BQ))
                        k = q // 8
                        if q % 8 == 0 and not last(i, k, 1):
                            ah.high(act, i + A0, k + 1)
                        if q % 8 == 4 and not last(i, k, 3):
                            ah.load(act, i + A0, k + 3)
                        if q % 8 in (3, 5, 7) and not held(i, k):
                            ah.gelus(act, i + A0, k, (q % 8 - 3) // 2)
                        if q % 8 == 7 and not held(i, k):
                            ah.store(act, i + A0, k)

                turn(0)
                with act.Fori(1, TURNS - 1) as i:
                    turn(i)
                turn(TURNS - 1)
                act.wait_ge(out[0], 16 * TURNS)
                for q in TAIL:
                    act.wait_ge(s["mm"], q + 1)
                    to_stage(act, c.ps[4 + q % QB], stage[0], 4 * (q - TAIL[0]))
                for k in HELD:
                    for ch in range(NCH):
                        ah.gelus(act, TURNS - 1 + A0, k, ch)
                    ah.store(act, TURNS - 1 + A0, k)
                for n in range(2):
                    act.wait_ge(ah.out[n], 16 * (Ahead.TILES // 2))

            @block.sync
            def _(sp):
                with sp.Fori(0, TURNS) as i:
                    for b in range(2):
                        sp.wait_ge(s["copy"], i * TQ + (b + 1) * BQ)
                        sp.dma_start(gates[bass.ds(i * 2 + b, 1)].rearrange("o p a n -> (o p) (a n)"),
                                     stage[b][:].rearrange("p a n -> p (a n)")).then_inc(out[b], 16)
                sp.wait_ge(s["copy"], NQ)
                sp.dma_start(c.dram["gates_tail_dram"], stage[0][:, :, 0:NSA]).then_inc(out[0], 16)
                sp.wait_ge(out[0], 16 * (TURNS + 1))
                sp.wait_ge(out[1], 16 * TURNS)


def stage_experts(c):
    nc, IN = c.nc, c.IN
    GR = 2
    SL = 2 * GR
    UG = GR * NCH
    YG = KD * NCH
    NB = 4
    NGE = 3
    SPLIT_AT = (2, 7, 12, 18)
    turns = NK // SL
    T0 = Ahead.TILES // SL
    A_AT, V_AT = (1, 4, 7, 10, 13, 16), (19, 21)
    with ExitStack() as ctx:
        sb = lambda t, shape, dt=F32: ctx.enter_context(nc.sbuf_tensor("ex_" + t, shape, dt))
        ug = [sb(f"u{i}", [P, TOK]) for i in range(GR)]
        u = [x[:, 0:D].rearrange("p (k e) -> p k e", e=P) for x in ug]
        v = [sb(f"v{i}", [P, D]) for i in range(GR)]
        g = [sb(f"g{i}", [P, TOK]) for i in range(GR)]
        up = [[sb(f"u_{t}{i}", [P, KD, P], F32R) for t in ("high", "low")] for i in range(GR)]
        vp = [[sb(f"v_{t}{i}", [P, D], F32R) for t in ("high", "low")] for i in range(SL)]
        ap = [[sb(f"a_{t}{i}", [P, TOK], F32R) for t in ("high", "low")] for i in range(SL)]
        ge = [sb(f"gelu{i}", [P, CH]) for i in range(NGE)]
        u_in, v_in, g_in = ([c.sem(f"ex_{t}_in{i}") for i in range(GR)] for t in "uvg")
        s = {n: c.sem("ex_" + n) for n in "s_mm gelu prod a_hi a_lo u_hi u_lo v_hi v_lo y_mm y".split()}
        SB, YB = c.ps[0:NB], c.ps[NB:2 * NB]

        def scores(pe, i, grp):
            for j in range(GR):
                pe.wait_ge(s["u_lo"], (i - T0) * SL + grp * GR + j + 1)
                for ch in range(NCH):
                    unit = grp * UG + j * NCH + ch
                    if not (isinstance(i, int) and i == T0 and unit < NB):
                        pe.wait_ge(s["gelu"], (i - T0) * (2 * UG) + unit - NB + 1)
                    for k in range(KD):
                        ins = product3(pe, SB[unit % NB][:, 0:CH], [x[:, k, :] for x in up[j]],
                                       [x[:, k, ch * CH:(ch + 1) * CH] for x in c.hT2], k == 0, k == KD - 1)
                    ins.then_inc(s["s_mm"], 1)

        def sums(pe, i, grp):
            pe.wait_ge(s["v_lo"], i * SL + (grp + 1) * GR)
            pe.wait_ge(s["a_lo"], i * (2 * UG) + (grp + 1) * UG)
            for n in range(YG):
                m, ch = divmod(n, NCH)
                unit = grp * YG + n
                if not (isinstance(i, int) and i == 0 and unit < NB):
                    pe.wait_ge(s["y"], i * (2 * YG) + unit - NB + 1)
                for j in range(GR):
                    sl = grp * GR + j
                    ins = product3(pe, YB[n % NB][:, 0:CH], [x[:, m * P:(m + 1) * P] for x in vp[sl]],
                                   [x[:, ch * CH:(ch + 1) * CH] for x in ap[sl]], j == 0, j == GR - 1)
                ins.then_inc(s["y_mm"], 1)

        def u_high(act, i, grp):
            for j in range(GR):
                act.wait_ge(u_in[j], i * 32 + grp * 16 + 16)
                if not (isinstance(i, int) and i == T0 and grp == 0):
                    act.wait_ge(s["s_mm"], (i - T0) * (2 * UG) + (grp - 1) * UG + (j + 1) * NCH)
                act.activation(up[j][0][:], u[j], ACT.Copy).then_inc(s["u_hi"], 1)

        def v_high(act, i, grp):
            for j in range(GR):
                act.wait_ge(v_in[j], i * 32 + grp * 16 + 16)
                act.activation(vp[grp * GR + j][0][:], v[j][:], ACT.Copy).then_inc(s["v_hi"], 1)

        def gelus(act, i, grp):
            for r in range(UG + 1):
                unit = grp * UG + r
                if r < UG:
                    act.wait_ge(s["s_mm"], (i - T0) * (2 * UG) + unit + 1)
                    act.wait_ge(s["a_lo"], i * (2 * UG) + unit - NGE + 1)
                    act.activation(ge[r % NGE][:], SB[unit % NB][:, 0:CH], ACT.Gelu).then_inc(s["gelu"], 1)
                if r:
                    j, ch = divmod(r - 1, NCH)
                    act.wait_ge(s["prod"], i * (2 * UG) + unit)
                    if r == 1 and not (isinstance(i, int) and i == 0):
                        act.wait_ge(s["y_mm"], i * (2 * YG) + (grp - 1) * YG)
                    act.activation(ap[grp * GR + j][0][:, ch * CH:(ch + 1) * CH], ge[(r - 1) % NGE][:], ACT.Copy)\
                       .then_inc(s["a_hi"], 1)

        def gating(dve, i, grp):
            for r in range(UG + 1):
                unit = grp * UG + r
                if r < UG:
                    j, ch = divmod(r, NCH)
                    if ch == 0:
                        dve.wait_ge(g_in[j], i * 64 + grp * 32 + 32)
                    dve.wait_ge(s["gelu"], (i - T0) * (2 * UG) + unit + 1)
                    x = ge[r % NGE][:]
                    dve.tensor_tensor(x, x, g[j][:, ch * CH:(ch + 1) * CH], ALU.mult).then_inc(s["prod"], 1)
                if r:
                    j, ch = divmod(r - 1, NCH)
                    cols = slice(ch * CH, (ch + 1) * CH)
                    dve.wait_ge(s["a_hi"], i * (2 * UG) + unit)
                    low_part(dve, ap[grp * GR + j][1][:, cols], ge[(r - 1) % NGE][:],
                             ap[grp * GR + j][0][:, cols]).then_inc(s["a_lo"], 1)

        def low_of(dve, i, grp, n):
            j = n % GR
            if n < GR:
                dve.wait_ge(s["u_hi"], (i - T0) * SL + (grp + 1) * GR + j + 1)
                low_part(dve, up[j][1][:], u[j], up[j][0][:]).then_inc(s["u_lo"], 1)
            else:
                sl = grp * GR + j
                dve.wait_ge(s["v_hi"], i * SL + sl + 1)
                low_part(dve, vp[sl][1][:], v[j][:], vp[sl][0][:]).then_inc(s["v_lo"], 1)

        def a_high(act, i, grp):
            for r in range(UG):
                j, ch = divmod(r, NCH)
                act.wait_ge(s["prod"], i * (2 * UG) + grp * UG + r + 1)
                if r == 0 and not (isinstance(i, int) and i == 0):
                    act.wait_ge(s["y_mm"], i * (2 * YG) + (grp - 1) * YG)
                cols = slice(ch * CH, (ch + 1) * CH)
                act.activation(ap[grp * GR + j][0][:, cols], ug[j][:, cols], ACT.Copy).then_inc(s["a_hi"], 1)

        def a_low(dve, i, grp, r):
            j, ch = divmod(r, NCH)
            cols = slice(ch * CH, (ch + 1) * CH)
            dve.wait_ge(s["a_hi"], i * (2 * UG) + grp * UG + r + 1)
            low_part(dve, ap[grp * GR + j][1][:, cols], ug[j][:, cols], ap[grp * GR + j][0][:, cols])\
                .then_inc(s["a_lo"], 1)

        def adding(dve, i, grp, lows):
            for n in range(YG):
                m, ch = divmod(n, NCH)
                dve.wait_ge(s["y_mm"], i * (2 * YG) + grp * YG + n + 1)
                if n == 0:
                    dve.wait_ge(s["y"], i * (2 * YG) + grp * YG)
                at = c.acc[:, m, ch * CH:(ch + 1) * CH]
                dve.tensor_tensor(at, at, YB[n % NB][:, 0:CH], ALU.add).then_inc(s["y"], 1)
                if n in lows:
                    lows[n]()

        with nc.Block() as block:
            @block.sync
            def _(sp):
                def load(i, grp, scored):
                    later = not (isinstance(i, int) and i == 0 and grp == 0)
                    for j in range(GR):
                        tile = bass.ds(i * SL + grp * GR + j, 1)
                        one = lambda ap: ap[tile].rearrange("o p n -> (o p) n")
                        if scored and not (isinstance(i, int) and i == T0 and grp == 0):
                            sp.wait_ge(s["u_lo"], ((i - T0) * SL + grp * GR + j) - GR + 1)
                        elif later:
                            sp.wait_ge(s["a_lo"], (i * (2 * UG) + grp * UG) + (j + 1) * NCH - UG)
                        if scored:
                            sp.dma_start(ug[j][:, 0:D], one(IN["uT"].rearrange("t p k e -> t p (k e)")))\
                              .then_inc(u_in[j], 16)
                        else:
                            sp.dma_start(ug[j][:], one(c.dram["gelu_dram"])).then_inc(u_in[j], 16)
                        if later:
                            sp.wait_ge(s["prod"], (i * (2 * UG) + grp * UG) + (j + 1) * NCH - UG)
                        sp.dma_start(g[j][:, 0:NPR].rearrange("p (b n) -> p b n", n=GBLK),
                                     c.dram["gates_dram"].rearrange("b p a n -> p b a n")[:, :, tile]
                                     .rearrange("p b o n -> p b (o n)")).then_inc(g_in[j], 16)
                        sp.dma_start(g[j][:, NPR:TOK], c.dram["gates_tail_dram"][:, tile]
                                     .rearrange("p o n -> p (o n)")).then_inc(g_in[j], 16)
                    for j in range(GR):
                        tile = bass.ds(i * SL + grp * GR + j, 1)
                        if later:
                            sp.wait_ge(s["v_lo"], (i * SL + grp * GR + j) - GR + 1)
                        sp.dma_start(v[j][:], IN["v"][tile].rearrange("o p n -> (o p) n")).then_inc(v_in[j], 16)

                load(0, 0, False)
                load(0, 1, False)
                with sp.Fori(1, T0) as i:
                    load(i, 0, False)
                    load(i, 1, False)
                load(T0, 0, True)
                load(T0, 1, True)
                with sp.Fori(T0 + 1, turns) as i:
                    load(i, 0, True)
                    load(i, 1, True)

            @block.gpsimd
            def _(pool):
                def gate(i, grp):
                    for r in range(UG):
                        j, ch = divmod(r, NCH)
                        if ch == 0:
                            pool.wait_ge(u_in[j], i * 32 + grp * 16 + 16)
                            pool.wait_ge(g_in[j], i * 64 + grp * 32 + 32)
                        x = ug[j][:, ch * CH:(ch + 1) * CH]
                        pool.tensor_tensor(x, x, g[j][:, ch * CH:(ch + 1) * CH], ALU.mult).then_inc(s["prod"], 1)

                with pool.Fori(0, T0) as i:
                    gate(i, 0)
                    gate(i, 1)

            @block.tensor
            def _(pe):
                sums(pe, 0, 0)
                sums(pe, 0, 1)
                with pe.Fori(1, T0 - 1) as i:
                    sums(pe, i, 0)
                    sums(pe, i, 1)
                sums(pe, T0 - 1, 0)
                scores(pe, T0, 0)
                sums(pe, T0 - 1, 1)
                scores(pe, T0, 1)
                sums(pe, T0, 0)
                with pe.Fori(T0 + 1, turns) as i:
                    scores(pe, i, 0)
                    sums(pe, i - 1, 1)
                    scores(pe, i, 1)
                    sums(pe, i, 0)
                sums(pe, turns - 1, 1)

            @block.scalar
            def _(act):
                def step(i, grp, more=True):
                    gelus(act, i, grp)
                    if more and grp == 0:
                        u_high(act, i, 1)
                    elif more:
                        u_high(act, i + 1, 0)
                    v_high(act, i, grp)

                for grp in range(2):
                    a_high(act, 0, grp)
                    v_high(act, 0, grp)
                with act.Fori(1, T0) as i:
                    for grp in range(2):
                        a_high(act, i, grp)
                        v_high(act, i, grp)
                u_high(act, T0, 0)
                step(T0, 0)
                step(T0, 1)
                with act.Fori(T0 + 1, turns - 1) as i:
                    step(i, 0)
                    step(i, 1)
                step(turns - 1, 0)
                step(turns - 1, 1, more=False)

            @block.vector
            def _(dve):
                def first_step(i, grp, before=True):
                    lows = {at: (lambda r=r: a_low(dve, i, grp, r)) for r, at in enumerate(A_AT)}
                    lows |= {at: (lambda n=n: low_of(dve, i, grp, GR + n)) for n, at in enumerate(V_AT)}
                    if not before:
                        for n in sorted(lows):
                            lows[n]()
                    else:
                        adding(dve, i if grp else i - 1, 1 - grp, lows)

                def step(i, grp, more=True):
                    gating(dve, i, grp)
                    todo = [n for n in range(2 * GR) if more or n >= GR]
                    adding(dve, i if grp else i - 1, 1 - grp,
                           {SPLIT_AT[n]: (lambda n=n: low_of(dve, i, grp, n)) for n in todo})

                c.vstep(dve, dve.memset(c.acc[:], 0.0))
                first_step(0, 0, before=False)
                first_step(0, 1)
                with dve.Fori(1, T0) as i:
                    first_step(i, 0)
                    first_step(i, 1)
                for j in range(GR):
                    dve.wait_ge(s["u_hi"], j + 1)
                    low_part(dve, up[j][1][:], u[j], up[j][0][:]).then_inc(s["u_lo"], 1)
                step(T0, 0)
                step(T0, 1)
                with dve.Fori(T0 + 1, turns - 1) as i:
                    step(i, 0)
                    step(i, 1)
                step(turns - 1, 0)
                step(turns - 1, 1, more=False)
                adding(dve, turns - 1, 1, {})


def stage_output(c):
    nc, OUT = c.nc, c.OUT
    with ExitStack() as ctx:
        x1 = ctx.enter_context(nc.sbuf_tensor("out_x1", [P, KD, TOK], F32))
        s = {n: c.sem("out_" + n) for n in "x_in y stored".split()}
        gate2, acc = c.mod[:, 5], c.acc
        with nc.Block() as block:
            @block.sync
            def _(sp):
                sp.dma_start(x1[:], c.dram["x1_dram"]).then_inc(s["x_in"], 16)
                for m in range(KD):
                    sp.wait_ge(s["y"], m + 1)
                    sp.dma_start(OUT["yT"][:, m], x1[:, m]).then_inc(s["stored"], 16)
                sp.wait_ge(s["stored"], 16 * KD)

            @block.vector
            def _(dve):
                dve.wait_ge(s["x_in"], 16)
                c.vstep(dve, dve.tensor_tensor(acc[:, :, NPR:TOK], acc[:, :, NPR:TOK], gate2[:, :, 1:], ALU.mult))
                c.vstep(dve, dve.tensor_tensor(x1[:, :, NPR:TOK], x1[:, :, NPR:TOK], acc[:, :, NPR:TOK], ALU.add))
                for m in range(KD):
                    dve.scalar_tensor_tensor(out=x1[:, m, 0:NPR], in0=acc[:, m, 0:NPR], scalar=gate2[:, m, 0:1],
                                             in1=x1[:, m, 0:NPR], op0=ALU.mult, op1=ALU.add).then_inc(s["y"], 1)


def build_program(nc, IN, OUT, upto=99, dbg=None):
    with ExitStack() as ctx:
        c = Core()
        setup(nc, c, ctx, IN, OUT)
        late = ctx.enter_context(ExitStack())
        c.ident, c.ones, c.iota = right_side(c, late, dict(ident=[P, P], ones=[P, P], iota=[P, NK]))
        with ExitStack() as outs, ExitStack() as early:
            c.silu_c, c.b_adaT, c.rows, c.rot, c.masks, c.QTs, c.KTs, c.lat_s = right_side(c, early, dict(
                silu_c=[P, KD, 1 + NSA], b_adaT=[P, ADA * KD], rows=[P, ROWG], rot=[P, NG + 1, len(TILES), 2 * RH], masks=[P, 3, P],
                QTs=[QK, MH, NSA], KTs=[QK, MH, NSA], lat_s=[NSA, LAT]))
            c.hT_life = early.enter_context(ExitStack())
            c.hT, = right_side(c, c.hT_life, dict(hT=[P, KD, TOK]))
            c.o_mlaT = outs.enter_context(nc.sbuf_tensor("o_mlaT", [P, MH * VH // P, TOK], F32))
            stage_ada(c)
            stage_norm(c, "norm1", IN["xT"], 0)
            with ExitStack() as mla:
                c.QT = mla.enter_context(nc.sbuf_tensor("QT", [QK, MH, NPR], F32))
                c.KT = mla.enter_context(nc.sbuf_tensor("KT", [QK, MH, NPR], F32))
                c.Vm = mla.enter_context(nc.sbuf_tensor("Vm", [P, NPR // P, MH * VH], F32))
                stage_mla_project(c)
                c.end_stage()
                stage_attention(c, "ma", MH, VH, c.QT, c.KT, c.Vm, lambda b: (0, b + 1, b, c.masks[:, 1, :]),
                                TurnOutput(c, c.o_mlaT), True)
                c.end_stage()
            stage_mla_sample(c)
            c.end_stage()
            c.hh, c.x_mix = same_place(c, outs, [P, KD, TOK], [("h1_high", F32R), ("mx_x", F32)])
            c.hT_life.close()
            c.hl, c.y_high = same_place(c, c.hT_life, [P, KD, TOK], [("h1_low", F32R), ("mx_y_high", F32R)], side="right")
            dsb = lambda t, shape: outs.enter_context(nc.sbuf_tensor("d_" + t, shape, F32))
            c.dqs, c.dks = (dsb(t, [P, NG, DH, NSA]) for t in ("qs", "ks"))
            c.dvs = dsb("vs", [NSA, NG, GW])
            with ExitStack() as work:
                wsb = lambda t, shape, dt=F32: work.enter_context(nc.sbuf_tensor("d_" + t, shape, dt))
                c.dQ, c.dK = (wsb(t, [P, DH, NPR]) for t in ("Q", "K"))
                c.dV = wsb("V", [P, NPR // P, GW])
                w, wl = zip(*(same_place(c, work, [P, KD, GW], [(f"d_w{i}", F32), (f"d_w_low{i}", F32R)])
                              for i in range(2)))
                wh = wsb("w_high", [P, KD, GW], F32R)
                for g in range(NG):
                    with ExitStack() as one:
                        stage_dilated_project(c, g, w, wh, wl, lambda t, shape: one.enter_context(
                            nc.sbuf_tensor(f"d{g}_{t}", shape, F32)))
                    stage_attention(c, f"da{g}", DH, DE, c.dQ, c.dK, c.dV, lambda b: dilated_span(c, g, b),
                                    StoreOutput(c, g, w), False)
                    c.end_stage()
            c.o_dilT = outs.enter_context(nc.sbuf_tensor("o_dilT", [P, GW // P, TOK], F32))
            stage_dilated_combine(c)
            stage_dilated_sample(c)
            c.end_stage()
            if upto == 5:
                dump(nc, c, dbg)
                return
            stage_mix(c)
        c.hT2 = [ctx.enter_context(nc.sbuf_tensor(f"h_{t}", [P, KD, TOK], F32R)) for t in ("high", "low")]
        stage_norm(c, "norm2", c.dram["x1_dram"], 1, c.hT2)
        c.end_stage()
        if upto == 6:
            dump(nc, c, dbg)
            return
        with ExitStack() as route:
            c.pick = route.enter_context(nc.sbuf_tensor("pick", [P, 3, TOK], F32))
            c.ahead = Ahead(c, route)
            stage_route(c)
            if upto == 7:
                dump(nc, c, dbg)
                return
            stage_gates(c)
            c.end_stage()
        late.close()
        c.acc = ctx.enter_context(nc.sbuf_tensor("experts_out", [P, KD, TOK], F32))
        with ExitStack() as experts:
            stage_experts(c)
        stage_output(c)


def dump(nc, c, dbg):
    s = c.sem("dbg")
    with nc.Block() as block:
        @block.sync
        def _(sp):
            for i, (dst, src) in enumerate(dbg(c)):
                sp.dma_start(dst, src).then_inc(s, 16)
                sp.wait_ge(s, 16 * i + 16)


def feature_tiles(a, inner):
    r, n = a.shape
    return np.ascontiguousarray(a.reshape(r // P, P, n // inner, inner).transpose(2, 1, 0, 3))


def angles(pos, half):
    inv = (np.float32(THETA) ** (-np.arange(half, dtype=np.float32) / np.float32(half))).astype(np.float32)
    ang = pos.astype(np.float32)[:, None] * inv[None]
    return np.cos(ang), np.sin(ang)


OUTS = dict(yT=(P, KD, TOK), latent_prompt=(NPR, LAT), latent_sample=(NSA, LAT))
for _g, (_w, _) in enumerate(GROUPS):
    OUTS[f"dil{_g}_prompt"] = (min(_w, NPR), 2, GW)
    OUTS[f"dil{_g}_sample"] = (NSA, 2, GW)


def lay_out(x):
    a = {k: np.asarray(v) for k, v in x.items()}
    w = {k: a[k][0] for k in a if a[k].shape[:1] == (1,) and k not in ("x_prompt", "c_prompt")}
    col = lambda v: v.reshape(-1, P).T
    fm = lambda t: np.ascontiguousarray(t.T.reshape(KD, P, -1).transpose(1, 0, 2))
    out = {}
    out["xT"] = fm(np.concatenate([a["x_prompt"][0], a["x_sample"][:, 0]]))
    out["cT"] = fm(np.concatenate([a["c_prompt"], a["c_sample"]]))
    out["w_ada"] = feature_tiles(w["w_ada"], P)
    out["b_adaT"] = np.ascontiguousarray(col(w["b_ada"]))
    kn = np.zeros((P, 1), np.float32)
    kn[0:NOPE, 0] = w["g_mla_kn"][0:NOPE]
    out["gainsT"] = np.concatenate([col(w["norm_mix_g"]), col(w["norm_ffn_g"]), col(w["g_q_lora"]), kn], 1)
    rg = np.concatenate([w["g_kv_lora"], w["g_mla_qn"], w["g_mla_kn"], w["g_dil_qn"], w["g_dil_kn"]])
    out["row_gains"] = np.ascontiguousarray(np.broadcast_to(rg, (P, ROWG)))
    out["ident"] = np.eye(P, dtype=np.float32)
    w_in = w["w_in"]
    out["w_q"] = feature_tiles(w_in[:, 0:QL], P)
    out["w_kv"] = feature_tiles(w_in[:, QL:O_DIL], LAT)[0]
    out["w_dil"] = feature_tiles(w_in[:, O_DIL:O_GATE], GW)
    out["w_gate"] = feature_tiles(w_in[:, O_GATE:], P)
    out["w_uq"] = feature_tiles(w["w_uq"].reshape(QL, MH * QK), MH * QK)[0]
    out["w_uk"] = np.ascontiguousarray(w["w_uk"].reshape(KVL, MH * NOPE))
    out["w_uv"] = np.ascontiguousarray(w["w_uv"].reshape(KVL, MH * VH))
    out["w_ukT"] = np.ascontiguousarray(w["w_uk"].transpose(2, 1, 0))
    out["w_mla"] = feature_tiles(w["w_branch_mla"], P)
    out["w_dilb"] = feature_tiles(w["w_branch_dil"], P)
    out["w_out"] = feature_tiles(w["w_out"], P)
    out["w_pq"] = feature_tiles(w["w_pq"], P)
    out["keysT"] = np.ascontiguousarray(w["sub_keys"].transpose(3, 0, 1, 2).reshape(P, 2 * PH, NK))
    u = w["expert_u"].reshape(NK, NK, KD, P)
    out["uT"] = np.ascontiguousarray(u.transpose(0, 3, 2, 1))
    out["v"] = w["expert_v"].reshape(NK, NK, D)
    out["cache"] = w["cache_latent"]
    out["page_table"] = a["page_table"].reshape(1, -1)
    for g in range(NG):
        out[f"state{g}"] = w[f"state_dil{g}"].reshape(NSA, -1, 2 * GW)
    pos = np.arange(NPR)
    orders = [pos] + [np.concatenate([pos[sub_slice(g, b)] for b in range(NPR // P)]) for g in range(NG)]
    rot = np.zeros((P, 4, len(TILES), 2 * RH), np.float32)
    for n, o in enumerate(orders):
        cs = np.concatenate(angles(o, RH), 1).reshape(-1, P, 2 * RH)
        rot[:, n, 0:8] = cs.transpose(1, 0, 2)
        rot[:, n, 8] = np.concatenate(angles(np.array([PAST]), RH), 1)
    out["rot"] = rot
    q, k = np.arange(P)[:, None], np.arange(P)[None]
    causal = np.where(k <= q, 0, NEG)
    prev = np.where(k >= q, 0, NEG)
    pair = np.where((k <= q) & (k % 2 == q % 2), 0, NEG)
    out["iota"] = np.broadcast_to(np.arange(NK, dtype=np.float32), (P, NK))
    hb = np.arange(MH * NSA)[:, None]
    out["diag"] = np.where(hb % NSA == np.arange(NSA)[None], 0, NEG).astype(np.float32)
    out["masks"] = np.stack([prev, causal, pair], 1).astype(np.float32)
    return {k: np.ascontiguousarray(v) for k, v in out.items()}


def kernel(**inputs):
    from concourse import bacc
    from concourse.bass_utils import run_bass_kernel_spmd

    nc = bacc.Bacc("TRN2", target_bir_lowering=False, num_devices=1)
    arrays = lay_out(inputs)
    IN = {k: nc.dram_tensor("in_" + k, v.shape, mybir.dt.from_np(v.dtype), kind="ExternalInput").ap()
          for k, v in arrays.items()}
    OUT = {k: nc.dram_tensor("out_" + k, shape, F32, kind="ExternalOutput").ap() for k, shape in OUTS.items()}
    build_program(nc, IN, OUT)
    res = run_bass_kernel_spmd(nc, [{"in_" + k: v for k, v in arrays.items()}], core_ids=[0]).results[0]
    r = {k: res["out_" + k] for k in OUTS}
    y = r["yT"].transpose(2, 1, 0).reshape(TOK, D)
    dil = [r[f"dil{g}_prompt"].reshape(1, 1, -1, 2, DH, DE) for g in range(NG)]
    dil += [r[f"dil{g}_sample"].reshape(1, NSA, 1, 2, DH, DE) for g in range(NG)]
    return (y[0:NPR].reshape(1, NPR, D), y[NPR:].reshape(NSA, 1, D), r["latent_prompt"].reshape(1, 1, NPR, LAT),
            r["latent_sample"].reshape(1, NSA, 1, LAT), *dil)
```
